# Optimizing a Trainium2 kernel written in Bass

```python
import math
import jax, jax.numpy as jnp
from jax import lax
import numpy as np

D_MODEL = 1024
BATCH = 1
SEQ = 512
DEPTH = 2

CHUNK = 64
Q_BLOCK = 128
ROPE_THETA = 10000.0
LN_EPS = 1e-5
RMS_EPS = 1e-6
NEG_INF = -1e30
DEEPNORM_ALPHA = (2.0 * DEPTH) ** 0.25
DEEPNORM_BETA = (8.0 * DEPTH) ** -0.25

MLA_HEADS = 8
MLA_Q_RANK = 384
MLA_KV_RANK = 256
MLA_NOPE = 64
MLA_ROPE = 32
MLA_V = 64

REL_HEADS = 4
REL_DIM = 64
REL_BACK_CHUNKS = 8
MAX_REL_DIST = 256
REL_TABLE = (CHUNK - 1) + MAX_REL_DIST + 1

SWA_Q_HEADS = 4
SWA_KV_HEADS = 2
SWA_GROUP = SWA_Q_HEADS // SWA_KV_HEADS
SWA_DIM = 64
SWA_WINDOW = 128
SWA_BACK_CHUNKS = SWA_WINDOW // CHUNK

MIX_WIDTH = MLA_HEADS * MLA_V + REL_HEADS * REL_DIM + SWA_Q_HEADS * SWA_DIM

IN_SPLITS = [
    MLA_Q_RANK, MLA_KV_RANK, MLA_ROPE,
    REL_HEADS * REL_DIM, REL_HEADS * REL_DIM, REL_HEADS * REL_DIM,
    SWA_Q_HEADS * SWA_DIM, SWA_KV_HEADS * SWA_DIM, SWA_KV_HEADS * SWA_DIM,
]
IN_COLS = int(sum(IN_SPLITS))
IN_SPLIT_POINTS = [int(c) for c in np.cumsum(IN_SPLITS)[:-1]]

PEER_HEADS = 8
N_KEYS = 128
N_EXPERTS = N_KEYS * N_KEYS
PEER_KEY_DIM = 128
PEER_TOPK = 16
PEER_TOKEN_BLOCK = 128

kernel_name = 'hymba_mla_chunkrel_swasink_peer_deepnorm'

def layer_norm(x, g, b):
    xf = x.astype(jnp.float32)
    mu = jnp.mean(xf, axis=-1, keepdims=True)
    var = jnp.mean(jnp.square(xf - mu), axis=-1, keepdims=True)
    y = (xf - mu) * lax.rsqrt(var + LN_EPS) * g.astype(jnp.float32) + b.astype(jnp.float32)
    return y.astype(x.dtype)

def rms_norm(x, g):
    xf = x.astype(jnp.float32)
    y = xf * lax.rsqrt(jnp.mean(jnp.square(xf), axis=-1, keepdims=True) + RMS_EPS) * g.astype(jnp.float32)
    return y.astype(x.dtype)

def rope_tables(seq, dim):
    inv = ROPE_THETA ** (-jnp.arange(0, dim, 2, dtype=jnp.float32) / dim)
    ang = jnp.arange(seq, dtype=jnp.float32)[:, None] * inv[None, :]
    return jnp.cos(ang), jnp.sin(ang)

def apply_rope(x, cos, sin):
    xf = x.astype(jnp.float32)
    half = xf.shape[-1] // 2
    x1, x2 = xf[..., :half], xf[..., half:]
    c, s = cos[:, None, :], sin[:, None, :]
    return jnp.concatenate([x1 * c - x2 * s, x1 * s + x2 * c], axis=-1).astype(x.dtype)

def chunk_band(x, n_back):
    b, s, h, d = x.shape
    nc = s // CHUNK
    nb = n_back + 1
    xc = jnp.pad(x.reshape(b, nc, CHUNK, h, d), ((0, 0), (n_back, 0), (0, 0), (0, 0), (0, 0)))
    idx = jnp.arange(nc)[:, None] + jnp.arange(nb)[None, :]
    band = xc[:, idx].reshape(b, nc, nb * CHUNK, h, d)
    valid = (jnp.arange(nc)[:, None] - n_back + jnp.arange(nb)[None, :]) >= 0
    return band, jnp.repeat(valid, CHUNK, axis=1)

def mla_attention(c_q, c_kv, k_rope, q_norm, w_uq, kv_norm, w_ukv):
    b, s, _ = c_q.shape
    dk = MLA_NOPE + MLA_ROPE
    q = (rms_norm(c_q, q_norm) @ w_uq).reshape(b, s, MLA_HEADS, dk)
    kv = (rms_norm(c_kv, kv_norm) @ w_ukv).reshape(b, s, MLA_HEADS, MLA_NOPE + MLA_V)
    k_nope, v = kv[..., :MLA_NOPE], kv[..., MLA_NOPE:]
    cos, sin = rope_tables(s, MLA_ROPE)
    q = jnp.concatenate([q[..., :MLA_NOPE], apply_rope(q[..., MLA_NOPE:], cos, sin)], axis=-1)
    k_pe = apply_rope(k_rope[:, :, None, :], cos, sin)
    k = jnp.concatenate([k_nope, jnp.broadcast_to(k_pe, (b, s, MLA_HEADS, MLA_ROPE))], axis=-1)
    scale = dk ** -0.5
    nqb = s // Q_BLOCK
    qb = q.reshape(b, nqb, Q_BLOCK, MLA_HEADS, dk).transpose(1, 0, 2, 3, 4)
    k_chunk = jnp.arange(s) // CHUNK

    def block(args):
        i, qi = args
        sc = jnp.einsum('bqhd,bkhd->bhqk', qi, k).astype(jnp.float32) * scale
        q_chunk = (i * Q_BLOCK + jnp.arange(Q_BLOCK)) // CHUNK
        mask = k_chunk[None, :] <= q_chunk[:, None]
        p = jax.nn.softmax(jnp.where(mask, sc, NEG_INF), axis=-1).astype(v.dtype)
        return jnp.einsum('bhqk,bkhd->bqhd', p, v)

    o = lax.map(block, (jnp.arange(nqb), qb))
    return o.transpose(1, 0, 2, 3, 4).reshape(b, s, MLA_HEADS * MLA_V)

def chunk_relpos_attention(q, k, v, rel_bias):
    b, s, _ = q.shape
    nc = s // CHUNK
    band_len = (REL_BACK_CHUNKS + 1) * CHUNK
    qc = q.reshape(b, nc, CHUNK, REL_HEADS, REL_DIM)
    kb, valid = chunk_band(k.reshape(b, s, REL_HEADS, REL_DIM), REL_BACK_CHUNKS)
    vb, _ = chunk_band(v.reshape(b, s, REL_HEADS, REL_DIM), REL_BACK_CHUNKS)
    sc = jnp.einsum('bcqhd,bcjhd->bhcqj', qc, kb).astype(jnp.float32) * (REL_DIM ** -0.5)
    rel = (REL_BACK_CHUNKS * CHUNK + jnp.arange(CHUNK))[:, None] - jnp.arange(band_len)[None, :]
    rel_idx = jnp.clip(rel, -(CHUNK - 1), MAX_REL_DIST) + (CHUNK - 1)
    bias = rel_bias[:, rel_idx].astype(jnp.float32)
    sc = jnp.where(valid[None, None, :, None, :], sc + bias[None, :, None], NEG_INF)
    p = jax.nn.softmax(sc, axis=-1).astype(v.dtype)
    return jnp.einsum('bhcqj,bcjhd->bcqhd', p, vb).reshape(b, s, REL_HEADS * REL_DIM)

def sliding_sink_attention(q, k, v, sinks):
    b, s, _ = q.shape
    nc = s // CHUNK
    cos, sin = rope_tables(s, SWA_DIM)
    q = apply_rope(q.reshape(b, s, SWA_Q_HEADS, SWA_DIM), cos, sin)
    k = apply_rope(k.reshape(b, s, SWA_KV_HEADS, SWA_DIM), cos, sin)
    qc = q.reshape(b, nc, CHUNK, SWA_KV_HEADS, SWA_GROUP, SWA_DIM)
    kb, valid = chunk_band(k, SWA_BACK_CHUNKS)
    vb, _ = chunk_band(v.reshape(b, s, SWA_KV_HEADS, SWA_DIM), SWA_BACK_CHUNKS)
    sc = jnp.einsum('bcqkgd,bcjkd->bkgcqj', qc, kb).astype(jnp.float32) * (SWA_DIM ** -0.5)
    sc = jnp.where(valid[None, None, None, :, None, :], sc, NEG_INF)
    sink = jnp.broadcast_to(sinks.reshape(SWA_KV_HEADS, SWA_GROUP).astype(jnp.float32)[None, :, :, None, None, None],
                            sc.shape[:-1] + (1,))
    p = jax.nn.softmax(jnp.concatenate([sc, sink], axis=-1), axis=-1)[..., :-1].astype(v.dtype)
    return jnp.einsum('bkgcqj,bcjkd->bcqkgd', p, vb).reshape(b, s, SWA_Q_HEADS * SWA_DIM)

def hybrid_mixer(x, w_in, mla_q_norm, mla_w_uq, mla_kv_norm, mla_w_ukv, rel_bias, swa_sinks, w_out):
    h = x @ w_in
    a_q, a_kv, a_kr, b_q, b_k, b_v, c_q, c_k, c_v = jnp.split(h, IN_SPLIT_POINTS, axis=-1)
    y_a = mla_attention(a_q, a_kv, a_kr, mla_q_norm, mla_w_uq, mla_kv_norm, mla_w_ukv)
    y_b = chunk_relpos_attention(b_q, b_k, b_v, rel_bias)
    y_c = sliding_sink_attention(c_q, c_k, c_v, swa_sinks)
    return jnp.concatenate([y_a, y_b, y_c], axis=-1) @ w_out

def peer_ffn(x, wq, keys, u, v):
    b, s, d = x.shape
    t = b * s
    xf = x.reshape(t, d)
    q = (xf @ wq).reshape(t, PEER_HEADS, 2, PEER_KEY_DIM // 2)
    sc = jnp.einsum('thpd,hpnd->thpn', q, keys).astype(jnp.float32)
    s_top, i_top = lax.top_k(sc, PEER_TOPK)
    cand = (s_top[:, :, 0, :, None] + s_top[:, :, 1, None, :]).reshape(t, PEER_HEADS, PEER_TOPK * PEER_TOPK)
    cand_idx = (i_top[:, :, 0, :, None] * N_KEYS + i_top[:, :, 1, None, :]).reshape(t, PEER_HEADS, PEER_TOPK * PEER_TOPK)
    g_s, pos = lax.top_k(cand, PEER_TOPK)
    experts = jnp.take_along_axis(cand_idx, pos, axis=-1)
    gates = jax.nn.softmax(g_s, axis=-1)
    nb = t // PEER_TOKEN_BLOCK

    def block(args):
        xb, eb, gb = args
        hid = jnp.einsum('td,thkd->thk', xb, u[eb]).astype(jnp.float32)
        act = (jax.nn.gelu(hid, approximate=False) * gb).astype(x.dtype)
        return jnp.einsum('thk,thkd->td', act, v[eb])

    out = lax.map(block, (xf.reshape(nb, PEER_TOKEN_BLOCK, d),
                          experts.reshape(nb, PEER_TOKEN_BLOCK, PEER_HEADS, PEER_TOPK),
                          gates.reshape(nb, PEER_TOKEN_BLOCK, PEER_HEADS, PEER_TOPK)))
    return out.reshape(b, s, d)

def setup_inputs(seed: int = 0) -> dict:
    key = jax.random.key(seed)
    ks = jax.random.split(key, 17)
    n = lambda k, shape: jax.random.normal(k, shape, dtype=jnp.float32)
    dk = MLA_NOPE + MLA_ROPE
    return {
        'x': n(ks[0], (BATCH, SEQ, D_MODEL)),
        'w_in': n(ks[1], (DEPTH, D_MODEL, IN_COLS)) * D_MODEL ** -0.5,
        'mla_q_norm': 1.0 + 0.01 * n(ks[2], (DEPTH, MLA_Q_RANK)),
        'mla_w_uq': n(ks[3], (DEPTH, MLA_Q_RANK, MLA_HEADS * dk)) * MLA_Q_RANK ** -0.5,
        'mla_kv_norm': 1.0 + 0.01 * n(ks[4], (DEPTH, MLA_KV_RANK)),
        'mla_w_ukv': n(ks[5], (DEPTH, MLA_KV_RANK, MLA_HEADS * (MLA_NOPE + MLA_V))) * MLA_KV_RANK ** -0.5,
        'rel_bias': 0.2 * n(ks[6], (DEPTH, REL_HEADS, REL_TABLE)),
        'swa_sinks': 0.5 * n(ks[7], (DEPTH, SWA_Q_HEADS)),
        'w_out': n(ks[8], (DEPTH, MIX_WIDTH, D_MODEL)) * (MIX_WIDTH ** -0.5 * DEEPNORM_BETA),
        'ln1_g': 1.0 + 0.01 * n(ks[9], (DEPTH, D_MODEL)),
        'ln1_b': 0.01 * n(ks[10], (DEPTH, D_MODEL)),
        'peer_wq': n(ks[11], (DEPTH, D_MODEL, PEER_HEADS * PEER_KEY_DIM)) * D_MODEL ** -0.5,
        'peer_keys': n(ks[12], (DEPTH, PEER_HEADS, 2, N_KEYS, PEER_KEY_DIM // 2)) * (PEER_KEY_DIM // 2) ** -0.5,
        'peer_u': n(ks[13], (DEPTH, N_EXPERTS, D_MODEL)) * D_MODEL ** -0.5,
        'peer_v': n(ks[14], (DEPTH, N_EXPERTS, D_MODEL)) * DEEPNORM_BETA,
        'ln2_g': 1.0 + 0.01 * n(ks[15], (DEPTH, D_MODEL)),
        'ln2_b': 0.01 * n(ks[16], (DEPTH, D_MODEL)),
    }

def reference(x, w_in, mla_q_norm, mla_w_uq, mla_kv_norm, mla_w_ukv, rel_bias, swa_sinks, w_out,
              ln1_g, ln1_b, peer_wq, peer_keys, peer_u, peer_v, ln2_g, ln2_b):
    for l in range(DEPTH):
        mix = hybrid_mixer(x, w_in[l], mla_q_norm[l], mla_w_uq[l], mla_kv_norm[l], mla_w_ukv[l],
                           rel_bias[l], swa_sinks[l], w_out[l])
        x = layer_norm(DEEPNORM_ALPHA * x + mix, ln1_g[l], ln1_b[l])
        ffn = peer_ffn(x, peer_wq[l], peer_keys[l], peer_u[l], peer_v[l])
        x = layer_norm(DEEPNORM_ALPHA * x + ffn, ln2_g[l], ln2_b[l])
    return x


_drawn_inputs = setup_inputs


def setup_inputs(seed=0):
    import zlib

    import numpy as np

    out = dict(_drawn_inputs(seed))
    spreads = {}
    factors = {'mla_q_norm': 7.369, 'mla_kv_norm': 6.796, 'swa_sinks': 44.267}
    for name, (base, spread) in spreads.items():
        noise = np.random.default_rng([zlib.crc32(name.encode()), seed]).standard_normal(out[name].shape)
        drawn = base * np.exp(spread * noise) if base else spread * noise
        out[name] = __import__('jax').numpy.asarray(drawn.astype(out[name].dtype))
    for name, factor in factors.items():
        out[name] = (out[name] * factor).astype(out[name].dtype)
    return out
```

```python
import math
from contextlib import ExitStack

import numpy as np
import concourse.bass as bass
from concourse import mybir

F32 = mybir.dt.float32
F32R = mybir.dt.float32r
U32 = mybir.dt.uint32
ALU = mybir.AluOpType
ACT = mybir.ActivationFunctionType
AX = mybir.AxisListType

P = 128
D = 1024
T = 512
DEPTH = 2
KD = D // P
NT = T // P
ALPHA = (2.0 * DEPTH) ** 0.25
LN_EPS = 1e-5
RMS_EPS = 1e-6
MASKED = -1e30
HUGE = 3e38
CHUNK = 64

Q_RANK, KV_RANK, ROPE, NOPE, V_DIM, A_HEADS = 384, 256, 32, 64, 64, 8
QK = NOPE + ROPE
KQ, KKV = Q_RANK // P, KV_RANK // P
B_HEADS, C_HEADS, HD = 4, 4, 64
MAX_REL = 256
REL_TABLE = (CHUNK - 1) + MAX_REL + 1
REL_ROW = 640
V_COLS = 384

W_TILES = 16
(T_AQ, T_AKV, T_KR, T_BQ, T_BK, T_CQ, T_CQR, T_CK, T_CKR) = (0, 3, 5, 6, 8, 10, 12, 14, 15)

PH, NK, TOPK, KEY_HALF = 8, 128, 16, 64
NEXP = NK * NK
SEG = 2 * PH
JG = 4
GROUPS = NK // JG


def layer_norm(nc, layer, which, x, bank, ln_gb, s):
    with ExitStack() as ctx:
        gb = ctx.enter_context(nc.sbuf_tensor(f"ln_gb{which}", [P, 2, D], F32))
        neg_mean = ctx.enter_context(nc.sbuf_tensor(f"ln_neg_mean{which}", [P, NT], F32))
        var = ctx.enter_context(nc.sbuf_tensor(f"ln_var_t{which}", [P, NT], F32))
        with nc.Block() as block:
            @block.sync
            def _(sp):
                sp.dma_start(gb[:], ln_gb[layer, which].partition_broadcast(P)).then_inc(s["land"], 16)

            @block.scalar
            def _(act):
                for t in range(NT):
                    act.wait_ge(s["mean"], NT + 1)
                    squares_out = bank[:, 2 * t:2 * t + 2, :].rearrange("p b n -> p (b n)")
                    nc.scalar.activation(squares_out, x[:, t, :], ACT.Square, bias=neg_mean[:, t:t + 1],
                                         accum_out=var[:, t:t + 1]).then_inc(s["squares"], 1)
                act.wait_ge(s["var"], 1)
                nc.scalar.activation(var[:], var[:], ACT.Sqrt).then_inc(s["root"], 1)

            @block.vector
            def _(dve):
                for t in range(NT):
                    nc.vector.reduce_sum(neg_mean[:, t:t + 1], x[:, t, :], AX.X).then_inc(s["mean"], 1)
                dve.wait_ge(s["mean"], NT)
                nc.vector.tensor_scalar(neg_mean[:], neg_mean[:], -1.0 / D, None,
                                        ALU.mult).then_inc(s["mean"], 1)
                dve.wait_ge(s["squares"], NT)
                nc.vector.tensor_scalar(var[:], var[:], 1.0 / D, LN_EPS, ALU.mult,
                                        ALU.add).then_inc(s["var"], 1)
                dve.wait_ge(s["root"], 1)
                nc.vector.reciprocal(var[:], var[:]).then_inc(s["chain"], 1)
                dve.wait_ge(s["chain"], 1)
                dve.wait_ge(s["land"], 16)
                for t in range(NT):
                    nc.vector.tensor_scalar(x[:, t, :], x[:, t, :], neg_mean[:, t:t + 1], var[:, t:t + 1],
                                            ALU.add, ALU.mult).then_inc(s["chain"], 1)
                for j, op in enumerate((ALU.mult, ALU.add)):
                    for t in range(NT):
                        dve.wait_ge(s["chain"], 2 + j * NT + t)
                        nc.vector.tensor_tensor(x[:, t, :], x[:, t, :], gb[:, j, :], op).then_inc(s["chain"], 1)


def program(nc, x_in, rope_tab, w_in, w_v, norms, w_uq, w_uk, w_uv, rel_bias, sinks, w_out,
            ln_gb, peer_wq, peer_keys, peer_u, peer_v, out):
    top = ExitStack()

    def sb(ctx, name, shape, dt=F32):
        return ctx.enter_context(nc.sbuf_tensor(name, shape, dt))

    def sem(name):
        s = top.enter_context(nc.semaphore(name))
        layer_sems.append(s)
        return s

    layer_sems = []
    with top:
        bank = top.enter_context(nc.psum_tensor("bank", [P, 8, 512], F32))
        gate_dram = nc.dram_tensor("gate_dram", [GROUPS, P, JG, T], F32, kind="Internal")
        rel_dram = nc.dram_tensor("rel_dram", [DEPTH * B_HEADS, REL_ROW], F32, kind="Internal")
        rel_copies = nc.dram_tensor("rel_copies", [B_HEADS, P, REL_ROW], F32, kind="Internal")

        x = sb(top, "x", [P, NT, D])
        ident = sb(top, "ident", [P, P])
        ones = sb(top, "ones", [P, P])
        iota = sb(top, "iota", [P, P])
        rope_c = sb(top, "rope_c", [P, 2, T])
        rope_a = sb(top, "rope_a", [P, 2, T])
        mask_causal = sb(top, "mask_causal", [P, T])
        mask_window = sb(top, "mask_window", [P, 2 * P])

        setup_dma = top.enter_context(nc.semaphore("setup_dma"))
        setup_row = top.enter_context(nc.semaphore("setup_row"))
        setup_pool = top.enter_context(nc.semaphore("setup_pool"))
        setup_store = top.enter_context(nc.semaphore("setup_store"))
        with ExitStack() as ctx:
            rel_rows = sb(ctx, "rel_rows", [DEPTH * B_HEADS, REL_ROW])
            with nc.Block() as block:
                @block.sync
                def _(sp):
                    sp.dma_start(rel_rows[:, MAX_REL - 1:MAX_REL - 1 + REL_TABLE],
                                 rel_bias).then_inc(setup_row, 16)
                    for t in range(NT):
                        sp.dma_start(x[:, t, :], x_in[t * P:(t + 1) * P, :]).then_inc(setup_dma, 16)
                    sp.dma_start(rope_c[:], rope_tab[0]).then_inc(setup_dma, 16)
                    sp.dma_start(rope_a[:], rope_tab[1]).then_inc(setup_dma, 16)
                    sp.wait_ge(setup_pool, 7)
                    sp.dma_start(rel_dram[:, :], rel_rows[:]).then_inc(setup_store, 16)
                    sp.wait_ge(setup_store, 16)
                    sp.wait_ge(setup_dma, 16 * (NT + 2))

                @block.gpsimd
                def _(pool):
                    nc.gpsimd.memset(ident[:], 0.0).then_inc(setup_pool, 1)
                    nc.gpsimd.memset(ones[:], 1.0).then_inc(setup_pool, 1)
                    nc.gpsimd.memset(mask_causal[:], 0.0).then_inc(setup_pool, 1)
                    nc.gpsimd.memset(mask_window[:], 0.0).then_inc(setup_pool, 1)
                    nc.gpsimd.memset(rel_rows[:, MAX_REL - 1 + REL_TABLE:REL_ROW], 0.0).then_inc(setup_pool, 1)
                    pool.wait_ge(setup_pool, 5)
                    nc.gpsimd.affine_select(out=ident[:], in_=ident[:], compare_op=ALU.not_equal, fill=1.0,
                                            base=0, pattern=[[-1, P]], channel_multiplier=1).then_inc(setup_pool, 1)
                    pool.wait_ge(setup_row, 16)
                    nc.gpsimd.tensor_copy(rel_rows[:, 0:MAX_REL - 1],
                                          rel_rows[:, MAX_REL - 1:MAX_REL].broadcast_to(
                                              [DEPTH * B_HEADS, MAX_REL - 1])).then_inc(setup_pool, 1)
                    nc.gpsimd.iota(iota[:], pattern=[[1, P]], base=0, channel_multiplier=0,
                                   allow_small_or_imprecise_dtypes=True).then_inc(setup_pool, 1)

                @block.vector
                def _(dve):
                    dve.wait_ge(setup_pool, 5)
                    nc.vector.memset(mask_causal[0:CHUNK, T - CHUNK:T], MASKED)
                    nc.vector.memset(mask_window[0:CHUNK, 2 * P - CHUNK:2 * P], MASKED)
                    nc.vector.memset(mask_window[CHUNK:P, 0:CHUNK], MASKED)

        w_land = [sem(f"w_land{i}") for i in range(4)]
        xt_psum = sem("xt_psum")
        xt_copied = sem("xt_copied")
        vw_land = sem("vw_land")
        up_land = sem("up_land")
        norms_land = sem("norms_land")
        job_done = sem("job_done")
        job_free = [sem(f"job_free{i}") for i in range(6)]
        dve_step = sem("dve_step")
        up_job_done = sem("up_job_done")
        up_free = [sem(f"up_free{i}") for i in range(6)]
        squares_summed = sem("squares_summed")
        mean_square = sem("mean_square")
        root = sem("root")
        latent_ready = sem("latent_ready")
        rel_land = sem("rel_land")
        sink_land = sem("sink_land")
        rel_masked = sem("rel_masked")
        scores_done = sem("scores_done")
        shifted = sem("shifted")
        exp_done = sem("exp_done")
        sink_exp = sem("sink_exp")
        inverse = sem("inverse")
        probs_ready = sem("probs_ready")
        probs_turned = sem("probs_turned")
        turned_copied = sem("turned_copied")
        pv_done = sem("pv_done")
        mixed_copied = sem("mixed_copied")
        wo_land = sem("wo_land")
        mix_out = sem("mix_out")
        mix_added = sem("mix_added")
        ln_land = [sem(f"ln_land{i}") for i in range(2)]
        ln_mean = [sem(f"ln_mean{i}") for i in range(2)]
        ln_squares = [sem(f"ln_squares{i}") for i in range(2)]
        ln_var = [sem(f"ln_var{i}") for i in range(2)]
        ln_root = [sem(f"ln_root{i}") for i in range(2)]
        ln_chain = [sem(f"ln_chain{i}") for i in range(2)]
        rq_land = [sem(f"rq_land{i}") for i in range(4)]
        rq_used = sem("rq_used")
        keys_land = sem("keys_land")
        r_xt_psum = sem("r_xt_psum")
        r_xt_copied = sem("r_xt_copied")
        x_high = sem("x_high")
        query_done = sem("query_done")
        query_copied = sem("query_copied")
        keysc_done = sem("keysc_done")
        keysc_copied = sem("keysc_copied")
        route = sem("route")
        gate_shift = sem("gate_shift")
        gate_exp = sem("gate_exp")
        routed = sem("routed")
        route_turned = sem("route_turned")
        route_copied = sem("route_copied")
        rows_ready = sem("rows_ready")
        cols_ready = sem("cols_ready")
        cols_taken = sem("cols_taken")
        slots_free = sem("slots_free")
        gate_mm = sem("gate_mm")
        gate_copied = sem("gate_copied")
        gate_store = [sem(f"gate_store{i}") for i in range(2)]
        u_land = [sem(f"u_land{i}") for i in range(2)]
        v_land = [sem(f"v_land{i}") for i in range(2)]
        g_land = [sem(f"g_land{i}") for i in range(2)]
        u_raw_free = sem("u_raw_free")
        v_raw_free = sem("v_raw_free")
        g_free = sem("g_free")
        u_high = sem("u_high")
        u_low = sem("u_low")
        v_high = sem("v_high")
        v_low = sem("v_low")
        u_free = sem("u_free")
        hid_done = sem("hid_done")
        gelu_done = sem("gelu_done")
        weighted = sem("weighted")
        act_high = sem("act_high")
        act_low = sem("act_low")
        down_free = sem("down_free")
        down_done = sem("down_done")
        down_added = sem("down_added")
        x_scaled = sem("x_scaled")
        ln_sems = [{"land": ln_land[i], "mean": ln_mean[i], "squares": ln_squares[i], "var": ln_var[i],
                    "root": ln_root[i], "chain": ln_chain[i]} for i in range(2)]

        with nc.Fori(0, DEPTH) as layer:
            with nc.Block() as block:
                @block.gpsimd
                def _(pool):
                    for s in layer_sems:
                        pool.sem_clear(s)

            with ExitStack() as mixer:
                q_a = sb(mixer, "q_a", [QK, A_HEADS, T])
                k_a = sb(mixer, "k_a", [QK, A_HEADS, T])
                v_a = sb(mixer, "v_a", [P, NT, A_HEADS * V_DIM])
                v_bc = sb(mixer, "v_bc", [P, NT, V_COLS])
                q_b = sb(mixer, "q_b", [P, 2, T])
                k_b = sb(mixer, "k_b", [P, 2, T])
                q_c = sb(mixer, "q_c", [P, 2, T])
                k_c = sb(mixer, "k_c", [P, T])

                with ExitStack() as ctx:
                    xt = sb(ctx, "xt", [P, KD, T])
                    wt = sb(ctx, "wt", [P, 4, KD, P])
                    wv = sb(ctx, "wv", [P, KD, V_COLS])
                    latent = sb(ctx, "latent", [P, KQ + KKV, T])
                    squares = sb(ctx, "squares", [P, KQ + KKV, T])
                    gains = sb(ctx, "gains", [P, KQ + KKV])
                    wuq = sb(ctx, "wuq", [P, KQ, A_HEADS, P])
                    wuk = sb(ctx, "wuk", [P, KKV, A_HEADS * NOPE])
                    wuv = sb(ctx, "wuv", [P, KKV, A_HEADS * V_DIM])
                    k_rope = sb(ctx, "k_rope", [QK, T])
                    turn = sb(ctx, "turn", [P, 2, T])
                    scale_row = sb(ctx, "scale_row", [P, 2, T])

                    jobs = [(T_AQ + m, 0, P, "latent", m) for m in range(KQ + KKV)]
                    jobs += [(T_KR, 0, ROPE, "rope_cos", None), (T_KR, ROPE, ROPE, "rope_sin", "k_rope")]
                    jobs += [(T_BQ + m, 0, P, "copy_q", m) for m in range(2)]
                    jobs += [(T_BK + m, 0, P, "copy_k", m) for m in range(2)]
                    for m in range(2):
                        jobs += [(T_CQ + m, 0, P, "rope_cos", None), (T_CQR + m, 0, P, "rope_sin", ("q_c", m))]
                    jobs += [(T_CK, 0, P, "rope_cos", None), (T_CKR, 0, P, "rope_sin", "k_c")]
                    order = [j[0] for j in jobs]
                    tiles = sorted(set(order), key=order.index)
                    jobs += [(None, t, V_COLS, "values", t) for t in range(NT)]

                    def job_bank(n):
                        return bank[:, 2 + n % 6, :]

                    def rope_rows(n):
                        return slice(NOPE, QK) if jobs[n][0] == T_KR else slice(0, P)

                    with nc.Block() as block:
                        @block.sync
                        def _(sp):
                            sp.dma_start(gains[:], norms[layer]).then_inc(norms_land, 16)
                            for n, tile in enumerate(tiles):
                                if n >= 4:
                                    sp.wait_ge(job_done, len(order) - order[::-1].index(tiles[n - 4]))
                                sp.dma_start(wt[:, n % 4], w_in[layer, tile]).then_inc(w_land[n % 4], 16)
                                if n == 3:
                                    sp.dma_start(wv[:], w_v[layer]).then_inc(vw_land, 16)
                            sp.dma_start(wuq[:], w_uq[layer]).then_inc(up_land, 16)
                            sp.dma_start(wuk[:], w_uk[layer]).then_inc(up_land, 16)
                            sp.dma_start(wuv[:], w_uv[layer]).then_inc(up_land, 16)

                        @block.tensor
                        def _(pe):
                            for k in range(KD):
                                if k >= 2:
                                    pe.wait_ge(xt_copied, k - 1)
                                for t in range(NT):
                                    mm = nc.tensor.transpose(bank[:, k % 2, t * P:(t + 1) * P],
                                                             x[:, t, k * P:(k + 1) * P], ident[:])
                                mm.then_inc(xt_psum, 1)
                            for n, (tile, c0, width, kind, _) in enumerate(jobs):
                                if n >= 6:
                                    pe.wait_ge(job_free[n % 6], n // 6)
                                if kind == "values":
                                    if c0 == 0:
                                        pe.wait_ge(vw_land, 16)
                                    for k in range(KD):
                                        mm = nc.tensor.matmul(job_bank(n)[:, 0:width],
                                                              xt[:, k, c0 * P:(c0 + 1) * P],
                                                              wv[:, k, :], start=(k == 0), stop=(k == KD - 1))
                                    mm.then_inc(job_done, 1)
                                    continue
                                at = tiles.index(tile)
                                if c0 == 0:
                                    pe.wait_ge(w_land[at % 4], 16 * (at // 4 + 1))
                                rows_out = rope_rows(n) if tile == T_KR else slice(0, P)
                                for k in range(KD):
                                    if n == 0:
                                        pe.wait_ge(xt_copied, k + 1)
                                    mm = nc.tensor.matmul(job_bank(n)[rows_out, :],
                                                          wt[:, at % 4, k, c0:c0 + width], xt[:, k, :],
                                                          start=(k == 0), stop=(k == KD - 1))
                                mm.then_inc(job_done, 1)

                        @block.scalar
                        def _(act):
                            for n, (_, _, width, kind, m) in enumerate(jobs):
                                if kind.startswith("rope"):
                                    continue
                                act.wait_ge(job_done, n + 1)
                                if kind == "latent":
                                    nc.scalar.copy(latent[:, m, :], job_bank(n))
                                    nc.scalar.activation(squares[:, m, :], job_bank(n),
                                                         ACT.Square).then_inc(job_free[n % 6], 1)
                                elif kind == "copy_q":
                                    nc.scalar.mul(q_b[:, m, :], job_bank(n), HD ** -0.5).then_inc(job_free[n % 6], 1)
                                elif kind == "copy_k":
                                    nc.scalar.copy(k_b[:, m, :], job_bank(n)).then_inc(job_free[n % 6], 1)
                                else:
                                    nc.scalar.copy(v_bc[:, m, :], job_bank(n)[:, 0:width]).then_inc(job_free[n % 6], 1)

                        @block.vector
                        def _(dve):
                            for k in range(KD):
                                dve.wait_ge(xt_psum, k + 1)
                                nc.vector.tensor_copy(xt[:, k, :], bank[:, k % 2, :]).then_inc(xt_copied, 1)
                            steps = 0
                            for n, (tile, _, _, kind, what) in enumerate(jobs):
                                if not kind.startswith("rope"):
                                    continue
                                r = rope_rows(n)
                                table = rope_a if tile == T_KR else rope_c
                                dve.wait_ge(job_done, n + 1)
                                part = 0 if kind == "rope_cos" else 1
                                nc.vector.tensor_tensor(turn[r, part, :], job_bank(n)[r, :], table[r, part, :],
                                                        ALU.mult).then_inc(job_free[n % 6], 1)
                                if part == 1:
                                    if what == "k_rope":
                                        dst = k_rope[r, :]
                                    else:
                                        dst = k_c[:] if what == "k_c" else q_c[:, what[1], :]
                                    dve.wait_ge(job_free[n % 6], n // 6 + 1)
                                    nc.vector.tensor_tensor(dst, turn[r, 0, :], turn[r, 1, :],
                                                            ALU.add).then_inc(dve_step, 1)
                                    steps += 1
                                    dve.wait_ge(dve_step, steps)

                    up_jobs = [("q", h) for h in range(A_HEADS)]
                    up_jobs = [(kind, h) for _, h in up_jobs for kind in ("q", "q_turned")]
                    up_jobs += [("k", h) for h in range(A_HEADS)] + [("v", t) for t in range(NT)]
                    up_reads = [2 if kind == "q" else 1 for kind, _ in up_jobs]

                    with nc.Block() as block:
                        @block.tensor
                        def _(pe):
                            for part, (m0, m1) in enumerate(((0, KQ), (KQ, KQ + KKV))):
                                for m in range(m0, m1):
                                    mm = nc.tensor.matmul(bank[:, 6 + part, :], ones[:], squares[:, m, :],
                                                          start=(m == m0), stop=(m == m1 - 1))
                                mm.then_inc(squares_summed, 1)
                            pe.wait_ge(up_land, 48)
                            for n, (kind, h) in enumerate(up_jobs):
                                if n >= 6:
                                    pe.wait_ge(up_free[n % 6], sum(up_reads[n % 6:n:6]))
                                if n == 0:
                                    pe.wait_ge(latent_ready, KQ)
                                if (kind, h) == ("k", 0):
                                    pe.wait_ge(latent_ready, KQ + KKV)
                                b = bank[:, n % 6, :]
                                if kind == "q":
                                    for k in range(KQ):
                                        mm = nc.tensor.matmul(b[0:QK, :], wuq[:, k, h, 0:QK], latent[:, k, :],
                                                              start=(k == 0), stop=(k == KQ - 1))
                                elif kind == "q_turned":
                                    for k in range(KQ):
                                        mm = nc.tensor.matmul(b[NOPE:QK, :], wuq[:, k, h, QK:P], latent[:, k, :],
                                                              start=(k == 0), stop=(k == KQ - 1))
                                elif kind == "k":
                                    for k in range(KKV):
                                        mm = nc.tensor.matmul(b[0:NOPE, :], wuk[:, k, h * NOPE:(h + 1) * NOPE],
                                                              latent[:, KQ + k, :],
                                                              start=(k == 0), stop=(k == KKV - 1))
                                else:
                                    for k in range(KKV):
                                        mm = nc.tensor.matmul(b, latent[:, KQ + k, h * P:(h + 1) * P], wuv[:, k, :],
                                                              start=(k == 0), stop=(k == KKV - 1))
                                mm.then_inc(up_job_done, 1)

                        @block.scalar
                        def _(act):
                            for part in range(2):
                                act.wait_ge(mean_square, part + 1)
                                nc.scalar.activation(scale_row[:, part, :], scale_row[:, part, :],
                                                     ACT.Sqrt).then_inc(root, 1)
                            for n, (kind, h) in enumerate(up_jobs):
                                if kind == "q_turned":
                                    continue
                                act.wait_ge(up_job_done, n + 1)
                                b = bank[:, n % 6, :]
                                dst = {"q": lambda: q_a[0:NOPE, h, :], "k": lambda: k_a[0:NOPE, h, :],
                                       "v": lambda: v_a[:, h, :]}[kind]()
                                src = b if kind == "v" else b[0:NOPE, :]
                                nc.scalar.copy(dst, src).then_inc(up_free[n % 6], 1)

                        @block.vector
                        def _(dve):
                            for part, rank in enumerate((Q_RANK, KV_RANK)):
                                dve.wait_ge(squares_summed, part + 1)
                                nc.vector.tensor_scalar(scale_row[:, part, :], bank[:, 6 + part, :], 1.0 / rank,
                                                        RMS_EPS, ALU.mult, ALU.add).then_inc(mean_square, 1)
                            dve.wait_ge(norms_land, 16)
                            for part, (m0, m1) in enumerate(((0, KQ), (KQ, KQ + KKV))):
                                dve.wait_ge(root, part + 1)
                                nc.vector.reciprocal(scale_row[:, part, :],
                                                     scale_row[:, part, :]).then_inc(mean_square, 1)
                                dve.wait_ge(mean_square, 3 + part)
                                for m in range(m0, m1):
                                    nc.vector.scalar_tensor_tensor(
                                        out=latent[:, m, :], in0=latent[:, m, :], scalar=gains[:, m:m + 1],
                                        in1=scale_row[:, part, :], op0=ALU.mult,
                                        op1=ALU.mult).then_inc(latent_ready, 1)
                            r = slice(NOPE, QK)
                            for n, (kind, h) in enumerate(up_jobs):
                                if kind not in ("q", "q_turned"):
                                    continue
                                dve.wait_ge(up_job_done, n + 1)
                                part = 0 if kind == "q" else 1
                                nc.vector.tensor_tensor(turn[r, part, :], bank[r, n % 6, :], rope_a[r, part, :],
                                                        ALU.mult).then_inc(up_free[n % 6], 1)
                                if part == 1:
                                    dve.wait_ge(up_free[n % 6], sum(up_reads[n % 6:n + 1:6]))
                                    nc.vector.tensor_tensor(q_a[r, h, :], turn[r, 0, :], turn[r, 1, :],
                                                            ALU.add).then_inc(dve_step, 1)
                                    dve.wait_ge(dve_step, 4 + h + 1)

                        @block.gpsimd
                        def _(pool):
                            for h in range(A_HEADS):
                                nc.gpsimd.tensor_copy(k_a[NOPE:QK, h, :], k_rope[NOPE:QK, :])

                with ExitStack() as ctx:
                    mixed = sb(ctx, "mixed", [P, KD, T])
                    wo = sb(ctx, "wo", [P, KD, D])
                    with ExitStack() as inner:
                        rel = sb(inner, "rel", [P, B_HEADS, T])
                        sink = sb(inner, "sink", [P, C_HEADS])
                        neg_sink = sb(inner, "neg_sink", [P, C_HEADS])
                        shifted_s = sb(inner, "shifted_s", [P, 3, T])
                        probs = sb(inner, "probs", [P, 3, T])
                        probs_t = sb(inner, "probs_t", [P, 3, T])
                        neg_max = sb(inner, "neg_max", [P, 64])
                        row_sum = sb(inner, "row_sum", [P, 64])
                        sink_e = sb(inner, "sink_e", [P, 16])
                        row_inv = sb(inner, "row_inv", [P, 64])
                        units = [("a", h, i) for h in range(A_HEADS) for i in range(NT)]
                        units += [("b", h, i) for h in range(B_HEADS) for i in range(NT)]
                        units += [("c", h, i) for h in range(C_HEADS) for i in range(NT)]
                        U = len(units)

                        def key_tiles(u):
                            kind, _, i = units[u]
                            return list(range(i + 1)) if kind != "c" else list(range(max(0, i - 1), i + 1))

                        def n_keys(u):
                            return P * len(key_tiles(u))

                        with nc.Block() as block:
                            @block.sync
                            def _(sp):
                                sp.dma_start(rel_copies[:, :, :].rearrange("h p n -> p h n"),
                                             rel_dram[bass.ts(layer, B_HEADS), :].partition_broadcast(P)
                                             ).then_inc(rel_land, 16)
                                sp.dma_start(sink[:], sinks[layer].partition_broadcast(P)).then_inc(sink_land, 16)
                                sp.wait_ge(rel_land, 16)
                                sp.dma_start(rel[:], bass.AP(rel_copies, P - 1, [[REL_ROW - 1, P], [P * REL_ROW, B_HEADS], [1, T]])
                                             ).then_inc(rel_land, 16)
                                sp.dma_start(wo[:], w_out[layer]).then_inc(wo_land, 16)

                            @block.gpsimd
                            def _(pool):
                                pool.wait_ge(rel_land, 32)
                                for h in range(B_HEADS):
                                    mm = nc.gpsimd.memset(rel[0:CHUNK, h, T - CHUNK:T], MASKED)
                                mm.then_inc(rel_masked, 1)
                                for u in range(U):
                                    n = n_keys(u)
                                    pool.wait_ge(inverse, u + 1)
                                    nc.gpsimd.tensor_scalar(probs[:, u % 3, 0:n], probs[:, u % 3, 0:n],
                                                            row_inv[:, u:u + 1], None,
                                                            ALU.mult).then_inc(probs_ready, 1)

                            @block.tensor
                            def _(pe):
                                def scores(u):
                                    kind, h, i = units[u]
                                    if u >= 3:
                                        pe.wait_ge(shifted, u - 2)
                                    qc, kc = slice(i * P, (i + 1) * P), slice(key_tiles(u)[0] * P, (i + 1) * P)
                                    r = slice(CHUNK * (h % 2), CHUNK * (h % 2) + CHUNK)
                                    q, k = {"a": lambda: (q_a[:, h, qc], k_a[:, h, kc]),
                                            "b": lambda: (q_b[r, h // 2, qc], k_b[r, h // 2, kc]),
                                            "c": lambda: (q_c[r, h // 2, qc], k_c[r, kc])}[kind]()
                                    nc.tensor.matmul(bank[:, u % 3, 0:n_keys(u)], q, k, start=True,
                                                     stop=True).then_inc(scores_done, 1)

                                def turn_probs(u):
                                    pe.wait_ge(probs_ready, u + 1)
                                    if u >= 2:
                                        pe.wait_ge(turned_copied, u - 1)
                                    for j in range(len(key_tiles(u))):
                                        mm = nc.tensor.transpose(bank[:, 3 + u % 2, j * P:(j + 1) * P],
                                                                 probs[:, u % 3, j * P:(j + 1) * P], ident[:])
                                    mm.then_inc(probs_turned, 1)

                                def values(u):
                                    kind, h, i = units[u]
                                    pair = u // (2 * NT)
                                    pe.wait_ge(turned_copied, u + 1)
                                    if u % (2 * NT) == 0 and pair >= 2:
                                        pe.wait_ge(mixed_copied, pair - 1)
                                    r = slice(V_DIM * (h % 2), V_DIM * (h % 2) + V_DIM)
                                    tiles_of = key_tiles(u)
                                    for j, kt in enumerate(tiles_of):
                                        v = {"a": lambda: v_a[:, kt, h * V_DIM:(h + 1) * V_DIM],
                                             "b": lambda: v_bc[:, kt, h * HD:(h + 1) * HD],
                                             "c": lambda: v_bc[:, kt, B_HEADS * HD + (h % 2) * HD:
                                                               B_HEADS * HD + (h % 2 + 1) * HD]}[kind]()
                                        mm = nc.tensor.matmul(bank[r, 5 + pair % 2, i * P:(i + 1) * P], v,
                                                              probs_t[:, u % 3, j * P:(j + 1) * P],
                                                              start=(j == 0), stop=(j == len(tiles_of) - 1))
                                    mm.then_inc(pv_done, 1)

                                for u in range(U + 3):
                                    if u < U:
                                        scores(u)
                                    if 2 <= u < U + 2:
                                        turn_probs(u - 2)
                                    if u >= 3:
                                        values(u - 3)

                            @block.scalar
                            def _(act):
                                act.wait_ge(sink_land, 16)
                                nc.scalar.mul(neg_sink[:], sink[:], -1.0).then_inc(sink_exp, 1)

                                def exponent(u):
                                    kind, h, i = units[u]
                                    n = n_keys(u)
                                    act.wait_ge(shifted, u + 1)
                                    if u >= 3:
                                        act.wait_ge(probs_turned, u - 2)
                                    if kind == "c":
                                        c = u - (U - C_HEADS * NT)
                                        nc.scalar.activation(sink_e[:, c:c + 1], sink[:, h:h + 1], ACT.Exp,
                                                             bias=neg_max[:, u:u + 1])
                                    nc.scalar.activation(probs[:, u % 3, 0:n], shifted_s[:, u % 3, 0:n], ACT.Exp,
                                                         bias=neg_max[:, u:u + 1], scale=-1.0,
                                                         accum_out=row_sum[:, u:u + 1]).then_inc(exp_done, 1)

                                def copy_turned(u):
                                    n = n_keys(u)
                                    act.wait_ge(probs_turned, u + 1)
                                    if u >= 3:
                                        act.wait_ge(pv_done, u - 2)
                                    nc.scalar.copy(probs_t[:, u % 3, 0:n],
                                                   bank[:, 3 + u % 2, 0:n]).then_inc(turned_copied, 1)

                                for u in range(U + 2):
                                    if u < U:
                                        exponent(u)
                                    if u >= 2:
                                        copy_turned(u - 2)

                            @block.vector
                            def _(dve):
                                def shift(u):
                                    kind, h, i = units[u]
                                    n = n_keys(u)
                                    bias, scale, start = {
                                        "a": lambda: (mask_causal[:, T - n:T], -QK ** -0.5, HUGE),
                                        "b": lambda: (rel[:, h, T - n:T], -1.0, HUGE),
                                        "c": lambda: (mask_window[:, 2 * P - n:2 * P], -HD ** -0.5,
                                                      neg_sink[:, h:h + 1])}[kind]()
                                    dve.wait_ge(scores_done, u + 1)
                                    if u >= 3:
                                        dve.wait_ge(exp_done, u - 2)
                                    nc.vector.tensor_tensor_reduce(
                                        out=shifted_s[:, u % 3, 0:n], in0=bank[:, u % 3, 0:n], in1=bias,
                                        scale=scale, scalar=start, op0=ALU.add, op1=ALU.min,
                                        accum_out=neg_max[:, u:u + 1]).then_inc(shifted, 1)

                                def invert(u):
                                    dve.wait_ge(exp_done, u + 1)
                                    c = u - (U - C_HEADS * NT)
                                    if c >= 0:
                                        nc.vector.tensor_tensor(row_sum[:, u:u + 1], row_sum[:, u:u + 1],
                                                                sink_e[:, c:c + 1], ALU.add).then_inc(dve_step, 1)
                                        dve.wait_ge(dve_step, 4 + A_HEADS + c + 1)
                                    nc.vector.reciprocal(row_inv[:, u:u + 1],
                                                         row_sum[:, u:u + 1]).then_inc(inverse, 1)

                                dve.wait_ge(rel_masked, 1)
                                dve.wait_ge(sink_exp, 1)
                                for u in range(U + 5):
                                    if u < U:
                                        shift(u)
                                    if 1 <= u <= U:
                                        invert(u - 1)
                                    if u >= 4 + 2 * NT - 1 and (u - 4) % (2 * NT) == 2 * NT - 1:
                                        pair = (u - 4) // (2 * NT)
                                        dve.wait_ge(pv_done, (pair + 1) * 2 * NT)
                                        nc.vector.tensor_copy(mixed[:, pair, :],
                                                              bank[:, 5 + pair % 2, :]).then_inc(mixed_copied, 1)
                    with nc.Block() as block:
                        @block.tensor
                        def _(pe):
                            pe.wait_ge(wo_land, 16)
                            for t in range(NT):
                                if t >= 2:
                                    pe.wait_ge(mix_added, t - 1)
                                for half in range(2):
                                    for k in range(KD):
                                        mm = nc.tensor.matmul(bank[:, 2 * (t % 2) + half, :],
                                                              mixed[:, k, t * P:(t + 1) * P],
                                                              wo[:, k, half * 512:(half + 1) * 512],
                                                              start=(k == 0), stop=(k == KD - 1))
                                mm.then_inc(mix_out, 1)

                        @block.vector
                        def _(dve):
                            for t in range(NT):
                                dve.wait_ge(mix_out, t + 1)
                                b = 2 * (t % 2)
                                nc.vector.scalar_tensor_tensor(
                                    out=x[:, t, :], in0=x[:, t, :], scalar=ALPHA,
                                    in1=bank[:, b:b + 2, :].rearrange("p b n -> p (b n)"),
                                    op0=ALU.mult, op1=ALU.add).then_inc(mix_added, 1)
            layer_norm(nc, layer, 0, x, bank, ln_gb, ln_sems[0])

            with ExitStack() as peer:
                x_h = sb(peer, "x_h", [P, KD, T], F32R)
                x_l = sb(peer, "x_l", [P, KD, T], F32R)
                with ExitStack() as ctx:
                    row_t = sb(ctx, "row_t", [P, T])
                    col_t = sb(ctx, "col_t", [P, T])
                    gate_t = sb(ctx, "gate_t", [P, T])
                    with ExitStack() as inner:
                        xt1 = sb(inner, "xt1", [P, KD, T])
                        wqt = sb(inner, "wqt", [P, 4, KD, P])
                        keys = sb(inner, "keys", [P, PH, NK])
                        query = sb(inner, "query", [P, PH, T])
                        keysc = sb(inner, "keysc", [P, 2, SEG, NK])
                        rest = sb(inner, "rest", [P, SEG, NK])
                        best = sb(inner, "best", [P, SEG, TOPK])
                        best_i = sb(inner, "best_i", [P, SEG, TOPK], U32)
                        best_f = sb(inner, "best_f", [P, SEG, TOPK])
                        pair = sb(inner, "pair", [P, PH, TOPK * TOPK])
                        pair_rest = sb(inner, "pair_rest", [P, PH, TOPK * TOPK])
                        won = sb(inner, "won", [P, PH, TOPK])
                        won_i = sb(inner, "won_i", [P, PH * TOPK], U32)
                        half_i = sb(inner, "half_i", [P, 2, PH * TOPK], U32)
                        half_f = sb(inner, "half_f", [P, 2, PH * TOPK])
                        hit = sb(inner, "hit", [P, PH * TOPK, TOPK])
                        chosen = sb(inner, "chosen", [P, 2, 3, PH * TOPK])
                        gate_d = sb(inner, "gate_d", [P, PH, TOPK])
                        gate_e = sb(inner, "gate_e", [P, PH, TOPK])
                        gate_s = sb(inner, "gate_s", [P, PH])
                        gate_r = sb(inner, "gate_r", [P, PH])
                        with nc.Block() as block:
                            @block.sync
                            def _(sp):
                                for h in range(PH):
                                    if h >= 4:
                                        sp.wait_ge(query_done, h - 3)
                                    sp.dma_start(wqt[:, h % 4], peer_wq[layer, h]).then_inc(rq_land[h % 4], 16)
                                sp.dma_start(keys[:], peer_keys[layer]).then_inc(keys_land, 16)

                            @block.tensor
                            def _(pe):
                                for k in range(KD):
                                    if k >= 2:
                                        pe.wait_ge(r_xt_copied, k - 1)
                                    for t in range(NT):
                                        mm = nc.tensor.transpose(bank[:, k % 2, t * P:(t + 1) * P],
                                                                 x[:, t, k * P:(k + 1) * P], ident[:])
                                    mm.then_inc(r_xt_psum, 1)
                                for h in range(PH):
                                    if h >= 2:
                                        pe.wait_ge(query_copied, h - 1)
                                    pe.wait_ge(rq_land[h % 4], 16 * (h // 4 + 1))
                                    for k in range(KD):
                                        if h == 0:
                                            pe.wait_ge(r_xt_copied, k + 1)
                                        mm = nc.tensor.matmul(bank[:, 2 + h % 2, :], wqt[:, h % 4, k, :], xt1[:, k, :],
                                                              start=(k == 0), stop=(k == KD - 1))
                                    mm.then_inc(query_done, 1)
                                pe.wait_ge(keys_land, 16)
                                pe.wait_ge(query_copied, PH)

                                def key_scores(t):
                                    if t:
                                        pe.wait_ge(keysc_copied, 4 * t)
                                    for h in range(PH):
                                        for half in range(2):
                                            r = slice(KEY_HALF * half, KEY_HALF * half + KEY_HALF)
                                            mm = nc.tensor.matmul(
                                                bank[:, 4 + 2 * half + h // 4, (h % 4) * NK:(h % 4 + 1) * NK],
                                                query[r, h, t * P:(t + 1) * P], keys[r, h, :], start=True, stop=True)
                                    mm.then_inc(keysc_done, 1)

                                def turn_route(t):
                                    pe.wait_ge(routed, t + 1)
                                    if t >= 2:
                                        pe.wait_ge(route_copied, t - 1)
                                    for j in range(3):
                                        mm = nc.tensor.transpose(bank[:, t % 2, j * P:(j + 1) * P],
                                                                 chosen[:, t % 2, j, :], ident[:])
                                    mm.then_inc(route_turned, 1)

                                key_scores(0)
                                for t in range(NT):
                                    if t + 1 < NT:
                                        key_scores(t + 1)
                                    turn_route(t)

                            @block.scalar
                            def _(act):
                                for k in range(KD):
                                    act.wait_ge(r_xt_copied, k + 1)
                                    nc.scalar.copy(x_h[:, k, :], xt1[:, k, :]).then_inc(x_high, 1)
                                for h in range(PH):
                                    act.wait_ge(query_done, h + 1)
                                    nc.scalar.copy(query[:, h, :], bank[:, 2 + h % 2, :]).then_inc(query_copied, 1)

                                def copy_scores(t):
                                    act.wait_ge(keysc_done, t + 1)
                                    if t >= 2:
                                        act.wait_ge(routed, t - 1)
                                    for c in range(4):
                                        nc.scalar.copy(keysc[:, t % 2, 4 * c:4 * c + 4, :].rearrange("p s n -> p (s n)"),
                                                       bank[:, 4 + c, :]).then_inc(keysc_copied, 1)

                                copy_scores(0)
                                for t in range(NT):
                                    if t + 1 < NT:
                                        copy_scores(t + 1)
                                    act.wait_ge(gate_shift, t + 1)
                                    nc.scalar.activation(gate_e[:], gate_d[:], ACT.Exp).then_inc(gate_exp, 1)
                                    act.wait_ge(route_turned, t + 1)
                                    for j, dst in enumerate((row_t, col_t, gate_t)):
                                        last = nc.scalar.copy(dst[:, t * P:(t + 1) * P],
                                                              bank[:, t % 2, j * P:(j + 1) * P])
                                    last.then_inc(route_copied, 1)

                            @block.vector
                            def _(dve):
                                for k in range(KD):
                                    dve.wait_ge(r_xt_psum, k + 1)
                                    nc.vector.tensor_copy(xt1[:, k, :], bank[:, k % 2, :]).then_inc(r_xt_copied, 1)
                                for k in range(KD):
                                    dve.wait_ge(x_high, k + 1)
                                    nc.vector.tensor_tensor(x_l[:, k, :], xt1[:, k, :], x_h[:, k, :].bitcast(F32),
                                                            ALU.subtract)
                                step = [0]

                                def then_wait(ins):
                                    step[0] += 1
                                    ins.then_inc(route, 1)
                                    dve.wait_ge(route, step[0])

                                def top16(score, left, value, index, n):
                                    for s in range(n):
                                        ins = nc.vector.max(value[:, s, 0:8], score[:, s, :])
                                    then_wait(ins)
                                    for s in range(n):
                                        ins = nc.vector.match_replace(out=left[:, s, :], in_to_replace=value[:, s, 0:8],
                                                                      in_values=score[:, s, :], imm_value=-HUGE)
                                    then_wait(ins)
                                    for s in range(n):
                                        nc.vector.max(value[:, s, 8:16], left[:, s, :])
                                        ins = nc.vector.max_index(out=index[:, s, 0:8], in_max=value[:, s, 0:8],
                                                                  in_values=score[:, s, :])
                                    then_wait(ins)
                                    for s in range(n):
                                        ins = nc.vector.max_index(out=index[:, s, 8:16], in_max=value[:, s, 8:16],
                                                                  in_values=left[:, s, :])
                                    then_wait(ins)

                                first16 = iota[:, 0:TOPK].unsqueeze(1).broadcast_to([P, PH * TOPK, TOPK])
                                for t in range(NT):
                                    dve.wait_ge(keysc_copied, 4 * (t + 1))
                                    top16(keysc[:, t % 2], rest, best, best_i, SEG)
                                    nc.vector.tensor_copy(best_f[:], best_i[:])
                                    then_wait(nc.vector.tensor_tensor(
                                        pair[:].rearrange("p h (a b) -> p h a b", b=TOPK),
                                        best[:, 0:PH, :].unsqueeze(3).broadcast_to([P, PH, TOPK, TOPK]),
                                        best[:, PH:SEG, :].unsqueeze(2).broadcast_to([P, PH, TOPK, TOPK]), ALU.add))
                                    top16(pair, pair_rest, won, won_i[:].rearrange("p (h k) -> p h k", h=PH), PH)
                                    nc.vector.tensor_tensor(gate_d[:], won[:], won[:, :, 0:1].broadcast_to([P, PH, TOPK]),
                                                            ALU.subtract).then_inc(gate_shift, 1)
                                    nc.vector.tensor_scalar(half_i[:, 0, :], won_i[:], 4, None, ALU.logical_shift_right)
                                    then_wait(nc.vector.tensor_scalar(half_i[:, 1, :], won_i[:], TOPK - 1, None,
                                                                      ALU.bitwise_and))
                                    then_wait(nc.vector.tensor_copy(half_f[:], half_i[:]))
                                    if t >= 2:
                                        dve.wait_ge(route_turned, t - 1)
                                    for half in range(2):
                                        then_wait(nc.vector.tensor_tensor(
                                            hit[:], first16,
                                            half_f[:, half, :].unsqueeze(2).broadcast_to([P, PH * TOPK, TOPK]),
                                            ALU.is_equal))
                                        then_wait(nc.vector.tensor_tensor(
                                            hit[:].rearrange("p (h k) a -> p h k a", h=PH),
                                            hit[:].rearrange("p (h k) a -> p h k a", h=PH),
                                            best_f[:, half * PH:(half + 1) * PH, :].unsqueeze(2).broadcast_to(
                                                [P, PH, TOPK, TOPK]), ALU.mult))
                                        then_wait(nc.vector.reduce_sum(chosen[:, t % 2, half, :], hit[:], AX.X))
                                    dve.wait_ge(gate_exp, t + 1)
                                    then_wait(nc.vector.reduce_sum(gate_s[:], gate_e[:], AX.X))
                                    then_wait(nc.vector.reciprocal(gate_r[:], gate_s[:]))
                                    nc.vector.tensor_tensor(
                                        chosen[:, t % 2, 2, :].rearrange("p (h k) -> p h k", h=PH), gate_e[:],
                                        gate_r[:].unsqueeze(2).broadcast_to([P, PH, TOPK]),
                                        ALU.mult).then_inc(routed, 1)
                                    dve.wait_ge(routed, t + 1)
                    rows = sb(ctx, "rows", [P, 8, NK])
                    cols = sb(ctx, "cols", [P, 8, NK])
                    col_now = sb(ctx, "col_now", [P, 8])
                    stage = sb(ctx, "stage", [P, 2, NK, P])
                    with nc.Block() as block:
                        @block.sync
                        def _(sp):
                            for t in range(NT):
                                sp.wait_ge(gate_copied, 2 + (t + 1) * P // 4)
                                for j in range(JG):
                                    sp.dma_start(gate_dram[:, :, j, t * P:(t + 1) * P].rearrange("g i t -> i g t"),
                                                 stage[:, t % 2, j::JG, :]).then_inc(gate_store[t % 2], 16)
                            for i in range(2):
                                sp.wait_ge(gate_store[i], 16 * JG * NT // 2)

                        @block.vector
                        def _(dve):
                            for t in range(NT):
                                with dve.Fori(0, P // 8) as it:
                                    for four in range(2):
                                        dve.wait_ge(gate_mm, it * 2 + (t * P // 4 + four + 1))
                                        for s in range(4 * four, 4 * four + 4):
                                            at = it * 8 + (t * P + s)
                                            ins = nc.vector.tensor_scalar(rows[:, s, :], iota[:],
                                                                          row_t[:, bass.ds(at, 1)],
                                                                          gate_t[:, bass.ds(at, 1)],
                                                                          ALU.is_equal, ALU.mult)
                                        ins.then_inc(rows_ready, 1)

                        @block.gpsimd
                        def _(pool):
                            for t in range(NT):
                                with pool.Fori(0, P // 8) as it:
                                    for four in range(2):
                                        pool.wait_ge(gate_mm, it * 2 + (t * P // 4 + four + 1))
                                        nc.gpsimd.tensor_copy(
                                            col_now[:, 4 * four:4 * four + 4],
                                            col_t[:, bass.ds(it * 8 + (t * P + 4 * four), 4)]).then_inc(cols_taken, 1)
                                        pool.wait_ge(route_copied, NT)
                                        pool.wait_ge(cols_taken, it * 2 + (t * P // 4 + four + 1))
                                        for s in range(4 * four, 4 * four + 4):
                                            ins = nc.gpsimd.tensor_scalar(cols[:, s, :], iota[:], col_now[:, s:s + 1],
                                                                          None, ALU.is_equal)
                                        ins.then_inc(cols_ready, 1)

                        @block.tensor
                        def _(pe):
                            pe.sem_inc(gate_mm, 2)
                            for t in range(NT):
                                with pe.Fori(0, P // 8) as it:
                                    for four in range(2):
                                        n = it * 2 + (t * P // 4 + four)
                                        pe.wait_ge(rows_ready, n + 1)
                                        pe.wait_ge(cols_ready, n + 1)
                                        pe.wait_ge(gate_copied, n + 1)
                                        for s in range(4):
                                            mm = nc.tensor.matmul(bank[:, four, s * NK:(s + 1) * NK],
                                                                  rows[:, 4 * four + s, :], cols[:, 4 * four + s, :],
                                                                  start=True, stop=True)
                                        mm.then_inc(gate_mm, 1)

                        @block.scalar
                        def _(act):
                            act.sem_inc(gate_copied, 2)
                            for t in range(NT):
                                if t >= 2:
                                    act.wait_ge(gate_store[t % 2], 16 * JG * (t // 2))
                                with act.Fori(0, P // 8) as it:
                                    for four in range(2):
                                        act.wait_ge(gate_mm, it * 2 + (t * P // 4 + four + 3))
                                        nc.scalar.copy(
                                            stage[:, t % 2, :, bass.ds(it * 8 + 4 * four, 4)].rearrange("p j t -> p t j"),
                                            bank[:, four, :].rearrange("p (t j) -> p t j", t=4)).then_inc(gate_copied, 1)
                with ExitStack() as ctx:
                    u_raw = sb(ctx, "u_raw", [P, 2, KD, P])
                    u_h = sb(ctx, "u_h", [P, JG, KD, P], F32R)
                    u_l = sb(ctx, "u_l", [P, JG, KD, P], F32R)
                    v_raw = sb(ctx, "v_raw", [P, 2, D])
                    v_h = sb(ctx, "v_h", [P, JG, D], F32R)
                    v_l = sb(ctx, "v_l", [P, JG, D], F32R)
                    gates = sb(ctx, "gates", [P, JG, T])
                    gelu = sb(ctx, "gelu", [P, 2, T])
                    weight = sb(ctx, "weight", [P, 2, T])
                    a_h = sb(ctx, "a_h", [P, JG, T], F32R)
                    a_l = sb(ctx, "a_l", [P, JG, T], F32R)
                    with nc.Block() as block:
                        def passes(high, low, other_high, other_low):
                            return ((high, other_high), (high, other_low), (low, other_high))

                        @block.sync
                        def _(sp):
                            with sp.Fori(0, GROUPS) as g:
                                for j in range(JG):
                                    sp.wait_ge(u_low, g * JG + (j + 1))
                                    sp.dma_start(u_raw[:, j % 2], peer_u[layer, g * JG + j]).then_inc(u_land[j % 2], 16)
                                    if j == 1:
                                        sp.wait_ge(weighted, g * JG + 2)
                                        sp.dma_start(gates[:], gate_dram[g]).then_inc(g_land[0], 16)
                                for j in range(JG):
                                    sp.wait_ge(v_low, g * JG + (j + 1))
                                    sp.dma_start(v_raw[:, j % 2, :], peer_v[layer, :, g * JG + j, :]).then_inc(v_land[j % 2], 16)

                        @block.tensor
                        def _(pe):
                            pe.sem_inc(hid_done, JG)
                            with pe.Fori(0, GROUPS) as g:
                                for j in range(JG):
                                    n = g * JG + j
                                    pe.wait_ge(u_low, n + 3)
                                    pe.wait_ge(gelu_done, n + 1)
                                    for k in range(KD):
                                        for c, (w, m) in enumerate(passes(u_h[:, j, k, :], u_l[:, j, k, :],
                                                                          x_h[:, k, :], x_l[:, k, :])):
                                            mm = nc.tensor.matmul(bank[:, j % 2, :], w, m, start=(k == 0 and c == 0),
                                                                  stop=(k == KD - 1 and c == 2))
                                    mm.then_inc(hid_done, 1)
                                for t in range(NT):
                                    pe.wait_ge(down_added, g * NT + (t + 1))
                                    tok = slice(t * P, (t + 1) * P)
                                    for j in range(JG):
                                        if t == 0:
                                            pe.wait_ge(act_low, g * JG + (j + 1))
                                            pe.wait_ge(v_low, g * JG + (j + 3))
                                        for half in range(2):
                                            c0 = slice(half * 512, (half + 1) * 512)
                                            for c, (w, m) in enumerate(passes(a_h[:, j, tok], a_l[:, j, tok],
                                                                              v_h[:, j, c0], v_l[:, j, c0])):
                                                mm = nc.tensor.matmul(bank[:, 2 + 2 * (t % 2) + half, :], w, m,
                                                                      start=(j == 0 and c == 0),
                                                                      stop=(j == JG - 1 and c == 2))
                                    mm.then_inc(down_done, 1)

                        @block.scalar
                        def _(act):
                            def split_u(g, j):
                                act.wait_ge(u_land[j % 2], g * 32 + (16 * (j // 2) + 16))
                                act.wait_ge(hid_done, g * JG + (j + 1))
                                nc.scalar.copy(u_h[:, j], u_raw[:, j % 2]).then_inc(u_high, 1)

                            def split_v(g, j):
                                act.wait_ge(v_land[j % 2], g * 32 + (16 * (j // 2) + 16))
                                act.wait_ge(down_done, g * NT)
                                nc.scalar.copy(v_h[:, j, :], v_raw[:, j % 2, :]).then_inc(v_high, 1)

                            def activate(n, j):
                                act.wait_ge(hid_done, n + (JG + 1))
                                act.wait_ge(weighted, n + 1)
                                nc.scalar.activation(gelu[:, j % 2, :], bank[:, j % 2, :], ACT.Gelu).then_inc(gelu_done, 1)
                                act.wait_ge(weighted, n + 3)
                                act.wait_ge(down_done, n - j)
                                nc.scalar.copy(a_h[:, j, :], weight[:, j % 2, :]).then_inc(act_high, 1)

                            def group(g, first):
                                if not first:
                                    activate(g * JG - 1, JG - 1)
                                for j in range(JG):
                                    split_u(g, j)
                                for j in range(JG):
                                    split_v(g, j)
                                    if j < JG - 1:
                                        activate(g * JG + j, j)

                            act.sem_inc(gelu_done, 2)
                            group(0, True)
                            with act.Fori(1, GROUPS) as g:
                                group(g, False)
                            activate(GROUPS * JG - 1, JG - 1)

                        @block.vector
                        def _(dve):
                            def split_u(g, j):
                                dve.wait_ge(u_high, g * JG + (j + 1))
                                nc.vector.tensor_tensor(u_l[:, j], u_raw[:, j % 2], u_h[:, j].bitcast(F32),
                                                        ALU.subtract).then_inc(u_low, 1)

                            def split_v(g, j):
                                dve.wait_ge(v_high, g * JG + (j + 1))
                                nc.vector.tensor_tensor(v_l[:, j, :], v_raw[:, j % 2, :], v_h[:, j, :].bitcast(F32),
                                                        ALU.subtract).then_inc(v_low, 1)

                            def activate(n, j):
                                if j == 0:
                                    dve.wait_ge(g_land[0], n * (16 // JG) + 16)
                                dve.wait_ge(gelu_done, n + 3)
                                nc.vector.tensor_tensor(weight[:, j % 2, :], gelu[:, j % 2, :], gates[:, j, :],
                                                        ALU.mult).then_inc(weighted, 1)
                                dve.wait_ge(act_high, n + 1)
                                nc.vector.tensor_tensor(a_l[:, j, :], weight[:, j % 2, :], a_h[:, j, :].bitcast(F32),
                                                        ALU.subtract).then_inc(act_low, 1)

                            def add_down(g, t):
                                dve.wait_ge(down_done, g * NT + (t + 1))
                                b = 2 + 2 * (t % 2)
                                nc.vector.tensor_tensor(x[:, t, :], x[:, t, :],
                                                        bank[:, b:b + 2, :].rearrange("p b n -> p (b n)"),
                                                        ALU.add).then_inc(down_added, 1)

                            def group(g, first):
                                if not first:
                                    activate(g * JG - 1, JG - 1)
                                for j in range(JG):
                                    split_u(g, j)
                                    if not first:
                                        add_down(g - 1, j)
                                for j in range(JG):
                                    split_v(g, j)
                                    if j < JG - 1:
                                        activate(g * JG + j, j)

                            dve.sem_inc(u_low, 2)
                            dve.sem_inc(v_low, 2)
                            dve.sem_inc(weighted, 2)
                            for t in range(NT):
                                nc.vector.tensor_scalar(x[:, t, :], x[:, t, :], ALPHA, None,
                                                        ALU.mult).then_inc(x_scaled, 1)
                            dve.wait_ge(x_scaled, NT)
                            dve.sem_inc(down_added, 2)
                            group(0, True)
                            with dve.Fori(1, GROUPS) as g:
                                group(g, False)
                            activate(GROUPS * JG - 1, JG - 1)
                            for t in range(NT):
                                add_down(GROUPS - 1, t)
            layer_norm(nc, layer, 1, x, bank, ln_gb, ln_sems[1])

        stored = top.enter_context(nc.semaphore("stored"))
        with nc.Block() as block:
            @block.sync
            def _(sp):
                for t in range(NT):
                    sp.dma_start(out[t * P:(t + 1) * P, :], x[:, t, :]).then_inc(stored, 16)
                sp.wait_ge(stored, 16 * NT)


def _rotary():
    tab = np.zeros((2, P, 2, T), np.float32)
    for which, dim in ((0, HD), (1, ROPE)):
        inv = (np.float32(10000.0) ** (-np.arange(0, dim, 2, dtype=np.float32) / np.float32(dim))).astype(np.float32)
        ang = np.arange(T, dtype=np.float32)[:, None] * inv[None, :]
        cos, sin = np.cos(ang).T, np.sin(ang).T
        c, s = np.concatenate([cos, cos]), np.concatenate([-sin, sin])
        if which == 0:
            tab[0, :, 0], tab[0, :, 1] = np.concatenate([c, c]), np.concatenate([s, s])
        else:
            tab[1, NOPE:QK, 0], tab[1, NOPE:QK, 1] = c, s
    return tab


def _swap(start, dim):
    return [start + (f + dim // 2) % dim for f in range(dim)]


def _in_columns():
    aq, akv, akr = 0, Q_RANK, Q_RANK + KV_RANK
    bq = akr + ROPE
    bk, bv = bq + B_HEADS * HD, bq + 2 * B_HEADS * HD
    cq = bv + B_HEADS * HD
    ck = cq + C_HEADS * HD
    cv = ck + 2 * HD
    tiles = [list(range(m * P, (m + 1) * P)) for m in range(KQ + KKV)]
    kr = list(range(akr, akr + ROPE)) + _swap(akr, ROPE)
    tiles.append(kr + kr)
    tiles += [list(range(bq + m * P, bq + (m + 1) * P)) for m in range(2)]
    tiles += [list(range(bk + m * P, bk + (m + 1) * P)) for m in range(2)]
    heads = _c_heads()
    for swapped in (False, True):
        for m in range(2):
            cols = []
            for h in heads[2 * m:2 * m + 2]:
                cols += _swap(cq + h * HD, HD) if swapped else list(range(cq + h * HD, cq + (h + 1) * HD))
            tiles.append(cols)
    tiles.append(list(range(ck, ck + P)))
    tiles.append(_swap(ck, HD) + _swap(ck + HD, HD))
    values = list(range(bv, bv + B_HEADS * HD)) + list(range(cv, cv + 2 * HD))
    return tiles, values


def _c_heads():
    return [(s % 2) * 2 + s // 2 for s in range(C_HEADS)]


def kernel(**inputs):
    import concourse.bacc as _bacc
    from concourse import mybir as _mybir
    from concourse.bass_utils import run_bass_kernel_spmd as _run

    g = {k: np.asarray(v) for k, v in inputs.items()}
    L = DEPTH
    heads = _c_heads()
    tiles, values = _in_columns()
    w_in = g["w_in"].reshape(L, KD, P, -1)
    uq = g["mla_w_uq"].reshape(L, KQ, P, A_HEADS, QK)
    ukv = g["mla_w_ukv"].reshape(L, KKV, P, A_HEADS, NOPE + V_DIM)
    mix_rows = list(range(768)) + [768 + h * HD + d for h in heads for d in range(HD)]
    arrays = {
        "x_in": g["x"].reshape(T, D),
        "rope_tab": _rotary(),
        "w_in": w_in[..., np.array(tiles)].transpose(0, 3, 2, 1, 4),
        "w_v": w_in[..., np.array(values)].transpose(0, 2, 1, 3),
        "norms": np.concatenate([g["mla_q_norm"], g["mla_kv_norm"]], 1).reshape(L, KQ + KKV, P).transpose(0, 2, 1),
        "w_uq": uq[..., np.array(list(range(QK)) + _swap(NOPE, ROPE))].transpose(0, 2, 1, 3, 4),
        "w_uk": ukv[..., :NOPE].transpose(0, 2, 1, 3, 4).reshape(L, P, KKV, -1),
        "w_uv": ukv[..., NOPE:].transpose(0, 2, 1, 3, 4).reshape(L, P, KKV, -1),
        "rel_bias": g["rel_bias"][:, :, ::-1].reshape(L * B_HEADS, REL_TABLE),
        "sinks": g["swa_sinks"][:, np.array(heads)],
        "w_out": g["w_out"][:, np.array(mix_rows)].reshape(L, KD, P, D).transpose(0, 2, 1, 3),
        "ln_gb": np.stack([np.stack([g["ln1_g"], g["ln1_b"]], 1), np.stack([g["ln2_g"], g["ln2_b"]], 1)], 1),
        "peer_wq": g["peer_wq"].reshape(L, KD, P, PH, P).transpose(0, 3, 2, 1, 4),
        "peer_keys": g["peer_keys"].transpose(0, 2, 4, 1, 3).reshape(L, P, PH, NK),
        "peer_u": g["peer_u"].reshape(L, NK, NK, KD, P).transpose(0, 2, 4, 3, 1),
        "peer_v": g["peer_v"].reshape(L, NK, NK, D),
    }
    nc = _bacc.Bacc("TRN2", target_bir_lowering=False, num_devices=1)
    given, args = {}, []
    for name, a in arrays.items():
        a = np.ascontiguousarray(a)
        given[f"in_{name}"] = a
        args.append(nc.dram_tensor(f"in_{name}", a.shape, _mybir.dt.from_np(a.dtype), kind="ExternalInput").ap())
    result = nc.dram_tensor("result", (T, D), F32, kind="ExternalOutput").ap()
    program(nc, *args, result)
    r = _run(nc, [given], core_ids=[0])
    return r.results[0]["result"].reshape(1, T, D)
```

```python
import math
from contextlib import ExitStack

import numpy as np
import concourse.bass as bass
from concourse import mybir

F32 = mybir.dt.float32
F32R = mybir.dt.float32r
U32 = mybir.dt.uint32
ALU = mybir.AluOpType
ACT = mybir.ActivationFunctionType
AX = mybir.AxisListType

P = 128
D = 1024
T = 512
DEPTH = 2
KD = D // P
NT = T // P
ALPHA = (2.0 * DEPTH) ** 0.25
LN_EPS = 1e-5
RMS_EPS = 1e-6
MASKED = -1e30
HUGE = 3e38
CHUNK = 64

Q_RANK, KV_RANK, ROPE, NOPE, V_DIM, A_HEADS = 384, 256, 32, 64, 64, 8
QK = NOPE + ROPE
KQ, KKV = Q_RANK // P, KV_RANK // P
B_HEADS, C_HEADS, HD = 4, 4, 64
MAX_REL = 256
REL_TABLE = (CHUNK - 1) + MAX_REL + 1
REL_ROW = 640
V_COLS = 384

W_TILES = 16
(T_AQ, T_AKV, T_KR, T_BQ, T_BK, T_CQ, T_CQR, T_CK, T_CKR) = (0, 3, 5, 6, 8, 10, 12, 14, 15)

PH, NK, TOPK, KEY_HALF = 8, 128, 16, 64
NEXP = NK * NK
SEG = 2 * PH
JG = 4
GROUPS = NK // JG
ROUTE_TILES = 44
GATE_TILES = 32
EARLY_TILES = ROUTE_TILES + GATE_TILES
EARLY_GROUPS = EARLY_TILES // JG
LATE_GROUPS = GROUPS - EARLY_GROUPS


def passes(high, low, other_high, other_low):
    return ((high, other_high), (high, other_low), (low, other_high))


def layer_norm(nc, layer, which, x, bank, ln_gb, s):
    with ExitStack() as ctx:
        gb = ctx.enter_context(nc.sbuf_tensor(f"ln_gb{which}", [P, 2, D], F32))
        neg_mean = ctx.enter_context(nc.sbuf_tensor(f"ln_neg_mean{which}", [P, NT], F32))
        var = ctx.enter_context(nc.sbuf_tensor(f"ln_var_t{which}", [P, NT], F32))
        inv = ctx.enter_context(nc.sbuf_tensor(f"ln_inv{which}", [P, NT], F32))
        work = ctx.enter_context(nc.sbuf_tensor(f"ln_work{which}", [P, NT], F32))
        with nc.Block() as block:
            @block.sync
            def _(sp):
                sp.dma_start(gb[:], ln_gb[layer, which].partition_broadcast(P)).then_inc(s["land"], 16)

            @block.scalar
            def _(act):
                for t in range(NT):
                    act.wait_ge(s["mean"], NT + 1)
                    squares_out = bank[:, 2 * t:2 * t + 2, :].rearrange("p b n -> p (b n)")
                    nc.scalar.activation(squares_out, x[:, t, :], ACT.Square, bias=neg_mean[:, t:t + 1],
                                         accum_out=var[:, t:t + 1]).then_inc(s["squares"], 1)
                act.wait_ge(s["var"], 1)
                nc.scalar.activation(inv[:], var[:], ACT.Sqrt).then_inc(s["root"], 1)

            @block.vector
            def _(dve):
                for t in range(NT):
                    nc.vector.reduce_sum(neg_mean[:, t:t + 1], x[:, t, :], AX.X).then_inc(s["mean"], 1)
                dve.wait_ge(s["mean"], NT)
                nc.vector.tensor_scalar(neg_mean[:], neg_mean[:], -1.0 / D, None,
                                        ALU.mult).then_inc(s["mean"], 1)
                dve.wait_ge(s["squares"], NT)
                nc.vector.tensor_scalar(var[:], var[:], 1.0 / D, LN_EPS, ALU.mult,
                                        ALU.add).then_inc(s["var"], 1)
                dve.wait_ge(s["root"], 1)
                steps = (lambda: nc.vector.reciprocal(inv[:], inv[:]),
                         lambda: nc.vector.tensor_tensor(work[:], inv[:], inv[:], ALU.mult),
                         lambda: nc.vector.scalar_tensor_tensor(out=work[:], in0=work[:], scalar=-0.5, in1=var[:],
                                                                op0=ALU.mult, op1=ALU.mult),
                         lambda: nc.vector.scalar_tensor_tensor(out=inv[:], in0=work[:], scalar=1.5, in1=inv[:],
                                                                op0=ALU.add, op1=ALU.mult))
                for c, take in enumerate(steps):
                    take().then_inc(s["chain"], 1)
                    dve.wait_ge(s["chain"], c + 1)
                dve.wait_ge(s["land"], 16)
                for t in range(NT):
                    nc.vector.tensor_scalar(x[:, t, :], x[:, t, :], neg_mean[:, t:t + 1], inv[:, t:t + 1],
                                            ALU.add, ALU.mult).then_inc(s["chain"], 1)
                for j, op in enumerate((ALU.mult, ALU.add)):
                    for t in range(NT):
                        dve.wait_ge(s["chain"], len(steps) + 1 + j * NT + t)
                        nc.vector.tensor_tensor(x[:, t, :], x[:, t, :], gb[:, j, :], op).then_inc(s["chain"], 1)


def program(nc, x_in, rope_tab, w_in, w_v, norms, w_uq, w_uk, w_uv, rel_bias, sinks, w_out,
            ln_gb, peer_wq, peer_keys, peer_u, peer_v, out):
    top = ExitStack()

    def sb(ctx, name, shape, dt=F32):
        return ctx.enter_context(nc.sbuf_tensor(name, shape, dt))

    def sem(name):
        s = top.enter_context(nc.semaphore(name))
        layer_sems.append(s)
        return s

    layer_sems = []
    with top:
        bank = top.enter_context(nc.psum_tensor("bank", [P, 8, 512], F32))
        gate_dram = nc.dram_tensor("gate_dram", [GROUPS, P, JG, T], F32, kind="Internal")
        rel_dram = nc.dram_tensor("rel_dram", [DEPTH * B_HEADS, REL_ROW], F32, kind="Internal")
        hid_dram = nc.dram_tensor("hid_dram", [EARLY_TILES, P, T], F32, kind="Internal")
        rel_copies = nc.dram_tensor("rel_copies", [B_HEADS, P, REL_ROW], F32, kind="Internal")

        x = sb(top, "x", [P, NT, D])
        ident = sb(top, "ident", [P, P])
        ones = sb(top, "ones", [P, P])
        iota = sb(top, "iota", [P, P])
        rope_c = sb(top, "rope_c", [P, 2, T])
        rope_a = sb(top, "rope_a", [P, 2, T])
        mask_causal = sb(top, "mask_causal", [P, T])
        mask_window = sb(top, "mask_window", [P, 2 * P])

        setup_dma = top.enter_context(nc.semaphore("setup_dma"))
        setup_row = top.enter_context(nc.semaphore("setup_row"))
        setup_pool = top.enter_context(nc.semaphore("setup_pool"))
        setup_store = top.enter_context(nc.semaphore("setup_store"))
        with ExitStack() as ctx:
            rel_rows = sb(ctx, "rel_rows", [DEPTH * B_HEADS, REL_ROW])
            with nc.Block() as block:
                @block.sync
                def _(sp):
                    sp.dma_start(rel_rows[:, MAX_REL - 1:MAX_REL - 1 + REL_TABLE],
                                 rel_bias).then_inc(setup_row, 16)
                    for t in range(NT):
                        sp.dma_start(x[:, t, :], x_in[t * P:(t + 1) * P, :]).then_inc(setup_dma, 16)
                    sp.dma_start(rope_c[:], rope_tab[0]).then_inc(setup_dma, 16)
                    sp.dma_start(rope_a[:], rope_tab[1]).then_inc(setup_dma, 16)
                    sp.wait_ge(setup_pool, 7)
                    sp.dma_start(rel_dram[:, :], rel_rows[:]).then_inc(setup_store, 16)
                    sp.wait_ge(setup_store, 16)
                    sp.wait_ge(setup_dma, 16 * (NT + 2))

                @block.gpsimd
                def _(pool):
                    nc.gpsimd.memset(ident[:], 0.0).then_inc(setup_pool, 1)
                    nc.gpsimd.memset(ones[:], 1.0).then_inc(setup_pool, 1)
                    nc.gpsimd.memset(mask_causal[:], 0.0).then_inc(setup_pool, 1)
                    nc.gpsimd.memset(mask_window[:], 0.0).then_inc(setup_pool, 1)
                    nc.gpsimd.memset(rel_rows[:, MAX_REL - 1 + REL_TABLE:REL_ROW], 0.0).then_inc(setup_pool, 1)
                    pool.wait_ge(setup_pool, 5)
                    nc.gpsimd.affine_select(out=ident[:], in_=ident[:], compare_op=ALU.not_equal, fill=1.0,
                                            base=0, pattern=[[-1, P]], channel_multiplier=1).then_inc(setup_pool, 1)
                    pool.wait_ge(setup_row, 16)
                    nc.gpsimd.tensor_copy(rel_rows[:, 0:MAX_REL - 1],
                                          rel_rows[:, MAX_REL - 1:MAX_REL].broadcast_to(
                                              [DEPTH * B_HEADS, MAX_REL - 1])).then_inc(setup_pool, 1)
                    nc.gpsimd.iota(iota[:], pattern=[[1, P]], base=0, channel_multiplier=0,
                                   allow_small_or_imprecise_dtypes=True).then_inc(setup_pool, 1)

                @block.vector
                def _(dve):
                    dve.wait_ge(setup_pool, 5)
                    nc.vector.memset(mask_causal[0:CHUNK, T - CHUNK:T], MASKED)
                    nc.vector.memset(mask_window[0:CHUNK, 2 * P - CHUNK:2 * P], MASKED)
                    nc.vector.memset(mask_window[CHUNK:P, 0:CHUNK], MASKED)

        w_land = [sem(f"w_land{i}") for i in range(4)]
        xt_psum = sem("xt_psum")
        xt_copied = sem("xt_copied")
        vw_land = sem("vw_land")
        up_land = sem("up_land")
        norms_land = sem("norms_land")
        job_done = sem("job_done")
        job_free = [sem(f"job_free{i}") for i in range(6)]
        dve_step = sem("dve_step")
        up_job_done = sem("up_job_done")
        up_free = [sem(f"up_free{i}") for i in range(6)]
        squares_summed = sem("squares_summed")
        mean_square = sem("mean_square")
        root = sem("root")
        newton = sem("newton")
        latent_ready = sem("latent_ready")
        rel_land = sem("rel_land")
        sink_land = sem("sink_land")
        rel_masked = sem("rel_masked")
        scores_done = sem("scores_done")
        shifted = sem("shifted")
        exp_done = sem("exp_done")
        sink_exp = sem("sink_exp")
        inverse = sem("inverse")
        probs_ready = sem("probs_ready")
        probs_turned = sem("probs_turned")
        turned_copied = sem("turned_copied")
        pv_done = sem("pv_done")
        mixed_copied = sem("mixed_copied")
        wo_land = sem("wo_land")
        mix_out = sem("mix_out")
        mix_added = sem("mix_added")
        ln_land = [sem(f"ln_land{i}") for i in range(2)]
        ln_mean = [sem(f"ln_mean{i}") for i in range(2)]
        ln_squares = [sem(f"ln_squares{i}") for i in range(2)]
        ln_var = [sem(f"ln_var{i}") for i in range(2)]
        ln_root = [sem(f"ln_root{i}") for i in range(2)]
        ln_chain = [sem(f"ln_chain{i}") for i in range(2)]
        rq_land = [sem(f"rq_land{i}") for i in range(2)]
        keys_land = sem("keys_land")
        r_xt_psum = sem("r_xt_psum")
        r_xt_copied = sem("r_xt_copied")
        x_high = sem("x_high")
        query_done = sem("query_done")
        query_copied = sem("query_copied")
        keysc_done = sem("keysc_done")
        keysc_copied = sem("keysc_copied")
        route = sem("route")
        gate_shift = sem("gate_shift")
        gate_exp = sem("gate_exp")
        routed = sem("routed")
        route_turned = sem("route_turned")
        route_copied = sem("route_copied")
        rows_ready = sem("rows_ready")
        x_low = sem("x_low")
        e_land = [sem(f"e_land{i}") for i in range(2)]
        e_store = [sem(f"e_store{i}") for i in range(2)]
        e_high = sem("e_high")
        e_low = sem("e_low")
        e_hid = sem("e_hid")
        e_gelu = sem("e_gelu")
        h_land = [sem(f"h_land{i}") for i in range(2)]
        h_store = [sem(f"h_store{i}") for i in range(2)]
        h_high = sem("h_high")
        h_low = sem("h_low")
        h_hid = sem("h_hid")
        h_gelu = sem("h_gelu")
        f_land = [sem(f"f_land{i}") for i in range(2)]
        fv_land = [sem(f"fv_land{i}") for i in range(2)]
        f_weighted = sem("f_weighted")
        fv_high = sem("fv_high")
        fv_low = sem("fv_low")
        fa_high = sem("fa_high")
        fa_low = sem("fa_low")
        f_done = sem("f_done")
        f_added = sem("f_added")
        gate_mm = sem("gate_mm")
        gate_copied = sem("gate_copied")
        gate_store = [sem(f"gate_store{i}") for i in range(2)]
        u_land = [sem(f"u_land{i}") for i in range(2)]
        v_land = [sem(f"v_land{i}") for i in range(2)]
        g_land = [sem(f"g_land{i}") for i in range(2)]
        u_high = sem("u_high")
        u_low = sem("u_low")
        v_high = sem("v_high")
        v_low = sem("v_low")
        hid_done = sem("hid_done")
        gelu_done = sem("gelu_done")
        weighted = sem("weighted")
        act_high = sem("act_high")
        act_low = sem("act_low")
        down_done = sem("down_done")
        down_added = sem("down_added")
        x_scaled = sem("x_scaled")
        ln_sems = [{"land": ln_land[i], "mean": ln_mean[i], "squares": ln_squares[i], "var": ln_var[i],
                    "root": ln_root[i], "chain": ln_chain[i]} for i in range(2)]

        with nc.Fori(0, DEPTH) as layer:
            with nc.Block() as block:
                @block.gpsimd
                def _(pool):
                    for s in layer_sems:
                        pool.sem_clear(s)

            with ExitStack() as mixer:
                q_a = sb(mixer, "q_a", [QK, A_HEADS, T])
                k_a = sb(mixer, "k_a", [QK, A_HEADS, T])
                v_a = sb(mixer, "v_a", [P, NT, A_HEADS * V_DIM])
                v_bc = sb(mixer, "v_bc", [P, NT, V_COLS])
                q_b = sb(mixer, "q_b", [P, 2, T])
                k_b = sb(mixer, "k_b", [P, 2, T])
                q_c = sb(mixer, "q_c", [P, 2, T])
                k_c = sb(mixer, "k_c", [P, T])

                with ExitStack() as ctx:
                    xt = sb(ctx, "xt", [P, KD, T])
                    wt = sb(ctx, "wt", [P, 4, KD, P])
                    wv = sb(ctx, "wv", [P, KD, V_COLS])
                    latent = sb(ctx, "latent", [P, KQ + KKV, T])
                    squares = sb(ctx, "squares", [P, KQ + KKV, T])
                    gains = sb(ctx, "gains", [P, KQ + KKV])
                    wuq = sb(ctx, "wuq", [P, KQ, A_HEADS, P])
                    wuk = sb(ctx, "wuk", [P, KKV, A_HEADS * NOPE])
                    wuv = sb(ctx, "wuv", [P, KKV, A_HEADS * V_DIM])
                    k_rope = sb(ctx, "k_rope", [QK, T])
                    turn = sb(ctx, "turn", [P, 2, T])
                    mean_sq = sb(ctx, "mean_sq", [P, 2, T])
                    scale_row = sb(ctx, "scale_row", [P, 2, T])

                    jobs = [(T_AQ + m, 0, P, "latent", m) for m in range(KQ + KKV)]
                    jobs += [(T_KR, 0, ROPE, "rope_cos", None), (T_KR, ROPE, ROPE, "rope_sin", "k_rope")]
                    jobs += [(T_BQ + m, 0, P, "copy_q", m) for m in range(2)]
                    jobs += [(T_BK + m, 0, P, "copy_k", m) for m in range(2)]
                    for m in range(2):
                        jobs += [(T_CQ + m, 0, P, "rope_cos", None), (T_CQR + m, 0, P, "rope_sin", ("q_c", m))]
                    jobs += [(T_CK, 0, P, "rope_cos", None), (T_CKR, 0, P, "rope_sin", "k_c")]
                    order = [j[0] for j in jobs]
                    tiles = sorted(set(order), key=order.index)
                    jobs += [(None, t, V_COLS, "values", t) for t in range(NT)]

                    def job_bank(n):
                        return bank[:, 2 + n % 6, :]

                    def rope_rows(n):
                        return slice(NOPE, QK) if jobs[n][0] == T_KR else slice(0, P)

                    with nc.Block() as block:
                        @block.sync
                        def _(sp):
                            sp.dma_start(gains[:], norms[layer]).then_inc(norms_land, 16)
                            for n, tile in enumerate(tiles):
                                if n >= 4:
                                    sp.wait_ge(job_done, len(order) - order[::-1].index(tiles[n - 4]))
                                sp.dma_start(wt[:, n % 4], w_in[layer, tile]).then_inc(w_land[n % 4], 16)
                                if n == 3:
                                    sp.dma_start(wv[:], w_v[layer]).then_inc(vw_land, 16)
                            sp.dma_start(wuq[:], w_uq[layer]).then_inc(up_land, 16)
                            sp.dma_start(wuk[:], w_uk[layer]).then_inc(up_land, 16)
                            sp.dma_start(wuv[:], w_uv[layer]).then_inc(up_land, 16)

                        @block.tensor
                        def _(pe):
                            for k in range(KD):
                                if k >= 2:
                                    pe.wait_ge(xt_copied, k - 1)
                                for t in range(NT):
                                    mm = nc.tensor.transpose(bank[:, k % 2, t * P:(t + 1) * P],
                                                             x[:, t, k * P:(k + 1) * P], ident[:])
                                mm.then_inc(xt_psum, 1)
                            for n, (tile, c0, width, kind, _) in enumerate(jobs):
                                if n >= 6:
                                    pe.wait_ge(job_free[n % 6], n // 6)
                                if kind == "values":
                                    if c0 == 0:
                                        pe.wait_ge(vw_land, 16)
                                    for k in range(KD):
                                        mm = nc.tensor.matmul(job_bank(n)[:, 0:width],
                                                              xt[:, k, c0 * P:(c0 + 1) * P],
                                                              wv[:, k, :], start=(k == 0), stop=(k == KD - 1))
                                    mm.then_inc(job_done, 1)
                                    continue
                                at = tiles.index(tile)
                                if c0 == 0:
                                    pe.wait_ge(w_land[at % 4], 16 * (at // 4 + 1))
                                rows_out = rope_rows(n) if tile == T_KR else slice(0, P)
                                for k in range(KD):
                                    if n == 0:
                                        pe.wait_ge(xt_copied, k + 1)
                                    mm = nc.tensor.matmul(job_bank(n)[rows_out, :],
                                                          wt[:, at % 4, k, c0:c0 + width], xt[:, k, :],
                                                          start=(k == 0), stop=(k == KD - 1))
                                mm.then_inc(job_done, 1)

                        @block.scalar
                        def _(act):
                            for n, (_, _, width, kind, m) in enumerate(jobs):
                                if kind.startswith("rope"):
                                    continue
                                act.wait_ge(job_done, n + 1)
                                if kind == "latent":
                                    nc.scalar.copy(latent[:, m, :], job_bank(n))
                                    nc.scalar.activation(squares[:, m, :], job_bank(n),
                                                         ACT.Square).then_inc(job_free[n % 6], 1)
                                elif kind == "copy_q":
                                    nc.scalar.mul(q_b[:, m, :], job_bank(n), HD ** -0.5).then_inc(job_free[n % 6], 1)
                                elif kind == "copy_k":
                                    nc.scalar.copy(k_b[:, m, :], job_bank(n)).then_inc(job_free[n % 6], 1)
                                else:
                                    nc.scalar.copy(v_bc[:, m, :], job_bank(n)[:, 0:width]).then_inc(job_free[n % 6], 1)

                        @block.vector
                        def _(dve):
                            for k in range(KD):
                                dve.wait_ge(xt_psum, k + 1)
                                nc.vector.tensor_copy(xt[:, k, :], bank[:, k % 2, :]).then_inc(xt_copied, 1)
                            steps = 0
                            for n, (tile, _, _, kind, what) in enumerate(jobs):
                                if not kind.startswith("rope"):
                                    continue
                                r = rope_rows(n)
                                table = rope_a if tile == T_KR else rope_c
                                dve.wait_ge(job_done, n + 1)
                                part = 0 if kind == "rope_cos" else 1
                                nc.vector.tensor_tensor(turn[r, part, :], job_bank(n)[r, :], table[r, part, :],
                                                        ALU.mult).then_inc(job_free[n % 6], 1)
                                if part == 1:
                                    if what == "k_rope":
                                        dst = k_rope[r, :]
                                    else:
                                        dst = k_c[:] if what == "k_c" else q_c[:, what[1], :]
                                    dve.wait_ge(job_free[n % 6], n // 6 + 1)
                                    nc.vector.tensor_tensor(dst, turn[r, 0, :], turn[r, 1, :],
                                                            ALU.add).then_inc(dve_step, 1)
                                    steps += 1
                                    dve.wait_ge(dve_step, steps)

                    up_jobs = [("q", h) for h in range(A_HEADS)]
                    up_jobs = [(kind, h) for _, h in up_jobs for kind in ("q", "q_turned")]
                    up_jobs += [("k", h) for h in range(A_HEADS)] + [("v", t) for t in range(NT)]
                    up_reads = [2 if kind == "q" else 1 for kind, _ in up_jobs]

                    with nc.Block() as block:
                        @block.tensor
                        def _(pe):
                            for part, (m0, m1) in enumerate(((0, KQ), (KQ, KQ + KKV))):
                                for m in range(m0, m1):
                                    mm = nc.tensor.matmul(bank[:, 6 + part, :], ones[:], squares[:, m, :],
                                                          start=(m == m0), stop=(m == m1 - 1))
                                mm.then_inc(squares_summed, 1)
                            pe.wait_ge(up_land, 48)
                            for n, (kind, h) in enumerate(up_jobs):
                                if n >= 6:
                                    pe.wait_ge(up_free[n % 6], sum(up_reads[n % 6:n:6]))
                                if n == 0:
                                    pe.wait_ge(latent_ready, KQ)
                                if (kind, h) == ("k", 0):
                                    pe.wait_ge(latent_ready, KQ + KKV)
                                b = bank[:, n % 6, :]
                                if kind == "q":
                                    for k in range(KQ):
                                        mm = nc.tensor.matmul(b[0:QK, :], wuq[:, k, h, 0:QK], latent[:, k, :],
                                                              start=(k == 0), stop=(k == KQ - 1))
                                elif kind == "q_turned":
                                    for k in range(KQ):
                                        mm = nc.tensor.matmul(b[NOPE:QK, :], wuq[:, k, h, QK:P], latent[:, k, :],
                                                              start=(k == 0), stop=(k == KQ - 1))
                                elif kind == "k":
                                    for k in range(KKV):
                                        mm = nc.tensor.matmul(b[0:NOPE, :], wuk[:, k, h * NOPE:(h + 1) * NOPE],
                                                              latent[:, KQ + k, :],
                                                              start=(k == 0), stop=(k == KKV - 1))
                                else:
                                    for k in range(KKV):
                                        mm = nc.tensor.matmul(b, latent[:, KQ + k, h * P:(h + 1) * P], wuv[:, k, :],
                                                              start=(k == 0), stop=(k == KKV - 1))
                                mm.then_inc(up_job_done, 1)

                        @block.scalar
                        def _(act):
                            for part in range(2):
                                act.wait_ge(mean_square, part + 1)
                                nc.scalar.activation(scale_row[:, part, :], mean_sq[:, part, :],
                                                     ACT.Sqrt).then_inc(root, 1)
                            for n, (kind, h) in enumerate(up_jobs):
                                if kind == "q_turned":
                                    continue
                                act.wait_ge(up_job_done, n + 1)
                                b = bank[:, n % 6, :]
                                dst = {"q": lambda: q_a[0:NOPE, h, :], "k": lambda: k_a[0:NOPE, h, :],
                                       "v": lambda: v_a[:, h, :]}[kind]()
                                src = b if kind == "v" else b[0:NOPE, :]
                                nc.scalar.copy(dst, src).then_inc(up_free[n % 6], 1)

                        @block.vector
                        def _(dve):
                            for part, rank in enumerate((Q_RANK, KV_RANK)):
                                dve.wait_ge(squares_summed, part + 1)
                                nc.vector.tensor_scalar(mean_sq[:, part, :], bank[:, 6 + part, :], 1.0 / rank,
                                                        RMS_EPS, ALU.mult, ALU.add).then_inc(mean_square, 1)
                            dve.wait_ge(norms_land, 16)
                            for part, (m0, m1) in enumerate(((0, KQ), (KQ, KQ + KKV))):
                                dve.wait_ge(root, part + 1)
                                v, y, z = mean_sq[:, part, :], scale_row[:, part, :], turn[:, part, :]
                                steps = (lambda: nc.vector.reciprocal(y, y),
                                         lambda: nc.vector.tensor_tensor(z, y, y, ALU.mult),
                                         lambda: nc.vector.scalar_tensor_tensor(out=z, in0=z, scalar=-0.5, in1=v,
                                                                                op0=ALU.mult, op1=ALU.mult),
                                         lambda: nc.vector.scalar_tensor_tensor(out=y, in0=z, scalar=1.5, in1=y,
                                                                                op0=ALU.add, op1=ALU.mult))
                                for c, take in enumerate(steps):
                                    take().then_inc(newton, 1)
                                    dve.wait_ge(newton, len(steps) * part + c + 1)
                                for m in range(m0, m1):
                                    nc.vector.scalar_tensor_tensor(
                                        out=latent[:, m, :], in0=latent[:, m, :], scalar=gains[:, m:m + 1],
                                        in1=scale_row[:, part, :], op0=ALU.mult,
                                        op1=ALU.mult).then_inc(latent_ready, 1)
                            r = slice(NOPE, QK)
                            for n, (kind, h) in enumerate(up_jobs):
                                if kind not in ("q", "q_turned"):
                                    continue
                                dve.wait_ge(up_job_done, n + 1)
                                part = 0 if kind == "q" else 1
                                nc.vector.tensor_tensor(turn[r, part, :], bank[r, n % 6, :], rope_a[r, part, :],
                                                        ALU.mult).then_inc(up_free[n % 6], 1)
                                if part == 1:
                                    dve.wait_ge(up_free[n % 6], sum(up_reads[n % 6:n + 1:6]))
                                    nc.vector.tensor_tensor(q_a[r, h, :], turn[r, 0, :], turn[r, 1, :],
                                                            ALU.add).then_inc(dve_step, 1)
                                    dve.wait_ge(dve_step, 4 + h + 1)

                        @block.gpsimd
                        def _(pool):
                            for h in range(A_HEADS):
                                nc.gpsimd.tensor_copy(k_a[NOPE:QK, h, :], k_rope[NOPE:QK, :])

                with ExitStack() as ctx:
                    mixed = sb(ctx, "mixed", [P, KD, T])
                    wo = sb(ctx, "wo", [P, KD, D])
                    with ExitStack() as inner:
                        rel = sb(inner, "rel", [P, B_HEADS, T])
                        sink = sb(inner, "sink", [P, C_HEADS])
                        neg_sink = sb(inner, "neg_sink", [P, C_HEADS])
                        shifted_s = sb(inner, "shifted_s", [P, 3, T])
                        probs = sb(inner, "probs", [P, 3, T])
                        probs_t = sb(inner, "probs_t", [P, 3, T])
                        neg_max = sb(inner, "neg_max", [P, 64])
                        row_sum = sb(inner, "row_sum", [P, 64])
                        sink_e = sb(inner, "sink_e", [P, 16])
                        row_inv = sb(inner, "row_inv", [P, 64])
                        units = [("a", h, i) for h in range(A_HEADS) for i in range(NT)]
                        units += [("b", h, i) for h in range(B_HEADS) for i in range(NT)]
                        units += [("c", h, i) for h in range(C_HEADS) for i in range(NT)]
                        U = len(units)

                        def key_tiles(u):
                            kind, _, i = units[u]
                            return list(range(i + 1)) if kind != "c" else list(range(max(0, i - 1), i + 1))

                        def n_keys(u):
                            return P * len(key_tiles(u))

                        with nc.Block() as block:
                            @block.sync
                            def _(sp):
                                sp.dma_start(rel_copies[:, :, :].rearrange("h p n -> p h n"),
                                             rel_dram[bass.ts(layer, B_HEADS), :].partition_broadcast(P)
                                             ).then_inc(rel_land, 16)
                                sp.dma_start(sink[:], sinks[layer].partition_broadcast(P)).then_inc(sink_land, 16)
                                sp.wait_ge(rel_land, 16)
                                sp.dma_start(rel[:], bass.AP(rel_copies, P - 1, [[REL_ROW - 1, P], [P * REL_ROW, B_HEADS], [1, T]])
                                             ).then_inc(rel_land, 16)
                                sp.dma_start(wo[:], w_out[layer]).then_inc(wo_land, 16)

                            @block.gpsimd
                            def _(pool):
                                pool.wait_ge(rel_land, 32)
                                for h in range(B_HEADS):
                                    mm = nc.gpsimd.memset(rel[0:CHUNK, h, T - CHUNK:T], MASKED)
                                mm.then_inc(rel_masked, 1)

                            @block.tensor
                            def _(pe):
                                def scores(u):
                                    kind, h, i = units[u]
                                    if u >= 3:
                                        pe.wait_ge(shifted, u - 2)
                                    qc, kc = slice(i * P, (i + 1) * P), slice(key_tiles(u)[0] * P, (i + 1) * P)
                                    r = slice(CHUNK * (h % 2), CHUNK * (h % 2) + CHUNK)
                                    q, k = {"a": lambda: (q_a[:, h, qc], k_a[:, h, kc]),
                                            "b": lambda: (q_b[r, h // 2, qc], k_b[r, h // 2, kc]),
                                            "c": lambda: (q_c[r, h // 2, qc], k_c[r, kc])}[kind]()
                                    nc.tensor.matmul(bank[:, u % 3, 0:n_keys(u)], q, k, start=True,
                                                     stop=True).then_inc(scores_done, 1)

                                def turn_probs(u):
                                    pe.wait_ge(probs_ready, u + 1)
                                    if u >= 2:
                                        pe.wait_ge(turned_copied, u - 1)
                                    for j in range(len(key_tiles(u))):
                                        mm = nc.tensor.transpose(bank[:, 3 + u % 2, j * P:(j + 1) * P],
                                                                 probs[:, u % 3, j * P:(j + 1) * P], ident[:])
                                    mm.then_inc(probs_turned, 1)

                                def values(u):
                                    kind, h, i = units[u]
                                    pair = u // (2 * NT)
                                    pe.wait_ge(turned_copied, u + 1)
                                    if u % (2 * NT) == 0 and pair >= 2:
                                        pe.wait_ge(mixed_copied, pair - 1)
                                    r = slice(V_DIM * (h % 2), V_DIM * (h % 2) + V_DIM)
                                    tiles_of = key_tiles(u)
                                    for j, kt in enumerate(tiles_of):
                                        v = {"a": lambda: v_a[:, kt, h * V_DIM:(h + 1) * V_DIM],
                                             "b": lambda: v_bc[:, kt, h * HD:(h + 1) * HD],
                                             "c": lambda: v_bc[:, kt, B_HEADS * HD + (h % 2) * HD:
                                                               B_HEADS * HD + (h % 2 + 1) * HD]}[kind]()
                                        mm = nc.tensor.matmul(bank[r, 5 + pair % 2, i * P:(i + 1) * P], v,
                                                              probs_t[:, u % 3, j * P:(j + 1) * P],
                                                              start=(j == 0), stop=(j == len(tiles_of) - 1))
                                    mm.then_inc(pv_done, 1)

                                for u in range(U + 3):
                                    if u < U:
                                        scores(u)
                                    if 2 <= u < U + 2:
                                        turn_probs(u - 2)
                                    if u >= 3:
                                        values(u - 3)

                            @block.scalar
                            def _(act):
                                act.wait_ge(sink_land, 16)
                                nc.scalar.mul(neg_sink[:], sink[:], -1.0).then_inc(sink_exp, 1)

                                def exponent(u):
                                    kind, h, i = units[u]
                                    n = n_keys(u)
                                    act.wait_ge(shifted, u + 1)
                                    if u >= 3:
                                        act.wait_ge(probs_turned, u - 2)
                                    if kind == "c":
                                        c = u - (U - C_HEADS * NT)
                                        nc.scalar.activation(sink_e[:, c:c + 1], sink[:, h:h + 1], ACT.Exp,
                                                             bias=neg_max[:, u:u + 1])
                                    nc.scalar.activation(probs[:, u % 3, 0:n], shifted_s[:, u % 3, 0:n], ACT.Exp,
                                                         bias=neg_max[:, u:u + 1], scale=-1.0,
                                                         accum_out=row_sum[:, u:u + 1]).then_inc(exp_done, 1)

                                def copy_turned(u):
                                    n = n_keys(u)
                                    act.wait_ge(probs_turned, u + 1)
                                    if u >= 3:
                                        act.wait_ge(pv_done, u - 2)
                                    nc.scalar.copy(probs_t[:, u % 3, 0:n],
                                                   bank[:, 3 + u % 2, 0:n]).then_inc(turned_copied, 1)

                                for u in range(U + 2):
                                    if u < U:
                                        exponent(u)
                                    if u >= 2:
                                        copy_turned(u - 2)

                            @block.vector
                            def _(dve):
                                def shift(u):
                                    kind, h, i = units[u]
                                    n = n_keys(u)
                                    bias, scale, start = {
                                        "a": lambda: (mask_causal[:, T - n:T], -QK ** -0.5, HUGE),
                                        "b": lambda: (rel[:, h, T - n:T], -1.0, HUGE),
                                        "c": lambda: (mask_window[:, 2 * P - n:2 * P], -HD ** -0.5,
                                                      neg_sink[:, h:h + 1])}[kind]()
                                    dve.wait_ge(scores_done, u + 1)
                                    if u >= 3:
                                        dve.wait_ge(exp_done, u - 2)
                                    nc.vector.tensor_tensor_reduce(
                                        out=shifted_s[:, u % 3, 0:n], in0=bank[:, u % 3, 0:n], in1=bias,
                                        scale=scale, scalar=start, op0=ALU.add, op1=ALU.min,
                                        accum_out=neg_max[:, u:u + 1]).then_inc(shifted, 1)

                                def normalise(u):
                                    dve.wait_ge(exp_done, u + 1)
                                    c = u - (U - C_HEADS * NT)
                                    if c >= 0:
                                        nc.vector.tensor_tensor(row_sum[:, u:u + 1], row_sum[:, u:u + 1],
                                                                sink_e[:, c:c + 1], ALU.add).then_inc(dve_step, 1)
                                        dve.wait_ge(dve_step, 4 + A_HEADS + c + 1)
                                    nc.vector.reciprocal(row_inv[:, u:u + 1],
                                                         row_sum[:, u:u + 1]).then_inc(inverse, 1)
                                    dve.wait_ge(inverse, u + 1)
                                    n = n_keys(u)
                                    nc.vector.tensor_scalar(probs[:, u % 3, 0:n], probs[:, u % 3, 0:n],
                                                            row_inv[:, u:u + 1], None,
                                                            ALU.mult).then_inc(probs_ready, 1)

                                dve.wait_ge(rel_masked, 1)
                                dve.wait_ge(sink_exp, 1)
                                for u in range(U + 5):
                                    if u < U:
                                        shift(u)
                                    if 1 <= u <= U:
                                        normalise(u - 1)
                                    if u >= 4 + 2 * NT - 1 and (u - 4) % (2 * NT) == 2 * NT - 1:
                                        pair = (u - 4) // (2 * NT)
                                        dve.wait_ge(pv_done, (pair + 1) * 2 * NT)
                                        nc.vector.tensor_copy(mixed[:, pair, :],
                                                              bank[:, 5 + pair % 2, :]).then_inc(mixed_copied, 1)
                    with nc.Block() as block:
                        @block.tensor
                        def _(pe):
                            pe.wait_ge(wo_land, 16)
                            for t in range(NT):
                                if t >= 2:
                                    pe.wait_ge(mix_added, t - 1)
                                for half in range(2):
                                    for k in range(KD):
                                        mm = nc.tensor.matmul(bank[:, 2 * (t % 2) + half, :],
                                                              mixed[:, k, t * P:(t + 1) * P],
                                                              wo[:, k, half * 512:(half + 1) * 512],
                                                              start=(k == 0), stop=(k == KD - 1))
                                mm.then_inc(mix_out, 1)

                        @block.vector
                        def _(dve):
                            for t in range(NT):
                                dve.wait_ge(mix_out, t + 1)
                                b = 2 * (t % 2)
                                nc.vector.scalar_tensor_tensor(
                                    out=x[:, t, :], in0=x[:, t, :], scalar=ALPHA,
                                    in1=bank[:, b:b + 2, :].rearrange("p b n -> p (b n)"),
                                    op0=ALU.mult, op1=ALU.add).then_inc(mix_added, 1)
            layer_norm(nc, layer, 0, x, bank, ln_gb, ln_sems[0])

            with ExitStack() as peer:
                x_h = sb(peer, "x_h", [P, KD, T], F32R)
                x_l = sb(peer, "x_l", [P, KD, T], F32R)
                with ExitStack() as ctx:
                    row_t = sb(ctx, "row_t", [P, T])
                    e_raw = sb(ctx, "e_raw", [P, 2, KD, P])
                    e_h = sb(ctx, "e_h", [P, 2, KD, P], F32R)
                    e_l = sb(ctx, "e_l", [P, 2, KD, P], F32R)
                    e_out = sb(ctx, "e_out", [P, 2, T])
                    col_t = sb(ctx, "col_t", [P, T])
                    gate_t = sb(ctx, "gate_t", [P, T])
                    with ExitStack() as inner:
                        xt1 = sb(inner, "xt1", [P, KD, T])
                        wqt = sb(inner, "wqt", [P, 2, KD, P])
                        keys = sb(inner, "keys", [P, PH, NK])
                        query = sb(inner, "query", [P, PH, T])
                        keysc = sb(inner, "keysc", [P, 2, SEG, NK])
                        rest = sb(inner, "rest", [P, SEG, NK])
                        best = sb(inner, "best", [P, SEG, TOPK])
                        best_i = sb(inner, "best_i", [P, SEG, TOPK], U32)
                        best_f = sb(inner, "best_f", [P, SEG, TOPK])
                        pair = sb(inner, "pair", [P, PH, TOPK * TOPK])
                        pair_rest = sb(inner, "pair_rest", [P, PH, TOPK * TOPK])
                        won = sb(inner, "won", [P, PH, TOPK])
                        won_i = sb(inner, "won_i", [P, PH * TOPK], U32)
                        half_i = sb(inner, "half_i", [P, 2, PH * TOPK], U32)
                        half_f = sb(inner, "half_f", [P, 2, PH * TOPK])
                        hit = sb(inner, "hit", [P, PH * TOPK, TOPK])
                        chosen = sb(inner, "chosen", [P, 2, 3, PH * TOPK])
                        gate_d = sb(inner, "gate_d", [P, PH, TOPK])
                        gate_e = sb(inner, "gate_e", [P, PH, TOPK])
                        gate_s = sb(inner, "gate_s", [P, PH])
                        gate_r = sb(inner, "gate_r", [P, PH])
                        with nc.Block() as block:
                            @block.sync
                            def _(sp):
                                for h in range(PH):
                                    if h >= 2:
                                        sp.wait_ge(query_done, h - 1)
                                    sp.dma_start(wqt[:, h % 2], peer_wq[layer, h]).then_inc(rq_land[h % 2], 16)
                                sp.dma_start(keys[:], peer_keys[layer]).then_inc(keys_land, 16)
                                for n in range(ROUTE_TILES):
                                    if n >= 2:
                                        sp.wait_ge(e_low, n - 1)
                                    sp.dma_start(e_raw[:, n % 2], peer_u[layer, n]).then_inc(e_land[n % 2], 16)
                                    if n >= 2:
                                        sp.wait_ge(e_gelu, n - 1)
                                        sp.dma_start(hid_dram[n - 2], e_out[:, n % 2, :]).then_inc(e_store[n % 2], 16)
                                for n in range(ROUTE_TILES - 2, ROUTE_TILES):
                                    sp.wait_ge(e_gelu, n + 1)
                                    sp.dma_start(hid_dram[n], e_out[:, n % 2, :]).then_inc(e_store[n % 2], 16)
                                for i in range(2):
                                    sp.wait_ge(e_store[i], 16 * ROUTE_TILES // 2)

                            @block.gpsimd
                            def _(pool):
                                for n in range(ROUTE_TILES):
                                    pool.wait_ge(e_high, n + 1)
                                    nc.gpsimd.tensor_tensor(e_l[:, n % 2], e_raw[:, n % 2], e_h[:, n % 2].bitcast(F32),
                                                            ALU.subtract).then_inc(e_low, 1)

                            @block.tensor
                            def _(pe):
                                for k in range(KD):
                                    if k >= 2:
                                        pe.wait_ge(r_xt_copied, k - 1)
                                    for t in range(NT):
                                        mm = nc.tensor.transpose(bank[:, k % 2, t * P:(t + 1) * P],
                                                                 x[:, t, k * P:(k + 1) * P], ident[:])
                                    mm.then_inc(r_xt_psum, 1)
                                for h in range(PH):
                                    if h >= 2:
                                        pe.wait_ge(query_copied, h - 1)
                                    pe.wait_ge(rq_land[h % 2], 16 * (h // 2 + 1))
                                    for k in range(KD):
                                        if h == 0:
                                            pe.wait_ge(r_xt_copied, k + 1)
                                        mm = nc.tensor.matmul(bank[:, 2 + h % 2, :], wqt[:, h % 2, k, :], xt1[:, k, :],
                                                              start=(k == 0), stop=(k == KD - 1))
                                    mm.then_inc(query_done, 1)
                                pe.wait_ge(keys_land, 16)
                                pe.wait_ge(query_copied, PH)

                                def key_scores(t):
                                    if t:
                                        pe.wait_ge(keysc_copied, 4 * t)
                                    for h in range(PH):
                                        for half in range(2):
                                            r = slice(KEY_HALF * half, KEY_HALF * half + KEY_HALF)
                                            mm = nc.tensor.matmul(
                                                bank[:, 2 + 2 * half + h // 4, (h % 4) * NK:(h % 4 + 1) * NK],
                                                query[r, h, t * P:(t + 1) * P], keys[r, h, :], start=True, stop=True)
                                    mm.then_inc(keysc_done, 1)

                                def turn_route(t):
                                    pe.wait_ge(routed, t + 1)
                                    if t >= 2:
                                        pe.wait_ge(route_copied, t - 1)
                                    for j in range(3):
                                        mm = nc.tensor.transpose(bank[:, t % 2, j * P:(j + 1) * P],
                                                                 chosen[:, t % 2, j, :], ident[:])
                                    mm.then_inc(route_turned, 1)

                                def hidden(n):
                                    pe.wait_ge(e_low, n + 1)
                                    if n >= 2:
                                        pe.wait_ge(e_gelu, n - 1)
                                    for k in range(KD):
                                        for c, (w, m) in enumerate(passes(e_h[:, n % 2, k, :], e_l[:, n % 2, k, :],
                                                                          x_h[:, k, :], x_l[:, k, :])):
                                            mm = nc.tensor.matmul(bank[:, 6 + n % 2, :], w, m, start=(k == 0 and c == 0),
                                                                  stop=(k == KD - 1 and c == 2))
                                    mm.then_inc(e_hid, 1)

                                pe.wait_ge(x_high, KD)
                                pe.wait_ge(x_low, KD)
                                key_scores(0)
                                n = 0
                                for t in range(NT):
                                    if t + 1 < NT:
                                        key_scores(t + 1)
                                    for _ in range(ROUTE_TILES // NT):
                                        hidden(n)
                                        n += 1
                                    turn_route(t)

                            @block.scalar
                            def _(act):
                                for k in range(KD):
                                    act.wait_ge(r_xt_copied, k + 1)
                                    nc.scalar.copy(x_h[:, k, :], xt1[:, k, :]).then_inc(x_high, 1)
                                for h in range(PH):
                                    act.wait_ge(query_done, h + 1)
                                    nc.scalar.copy(query[:, h, :], bank[:, 2 + h % 2, :]).then_inc(query_copied, 1)

                                def copy_scores(t):
                                    act.wait_ge(keysc_done, t + 1)
                                    if t >= 2:
                                        act.wait_ge(routed, t - 1)
                                    for c in range(4):
                                        nc.scalar.copy(keysc[:, t % 2, 4 * c:4 * c + 4, :].rearrange("p s n -> p (s n)"),
                                                       bank[:, 2 + c, :]).then_inc(keysc_copied, 1)

                                def split(n):
                                    act.wait_ge(e_land[n % 2], 16 * (n // 2 + 1))
                                    if n >= 2:
                                        act.wait_ge(e_hid, n - 1)
                                    nc.scalar.copy(e_h[:, n % 2], e_raw[:, n % 2]).then_inc(e_high, 1)

                                def activate(n):
                                    act.wait_ge(e_hid, n + 1)
                                    if n >= 2:
                                        act.wait_ge(e_store[n % 2], 16 * (n // 2))
                                    nc.scalar.activation(e_out[:, n % 2, :], bank[:, 6 + n % 2, :],
                                                         ACT.Gelu).then_inc(e_gelu, 1)

                                copy_scores(0)
                                split(0)
                                split(1)
                                n = 0
                                for t in range(NT):
                                    if t + 1 < NT:
                                        copy_scores(t + 1)
                                    for i in range(ROUTE_TILES // NT):
                                        if i == ROUTE_TILES // NT - 1:
                                            act.wait_ge(gate_shift, t + 1)
                                            nc.scalar.activation(gate_e[:], gate_d[:], ACT.Exp).then_inc(gate_exp, 1)
                                        if n + 2 < ROUTE_TILES:
                                            split(n + 2)
                                        activate(n)
                                        n += 1
                                    act.wait_ge(route_turned, t + 1)
                                    for j, dst in enumerate((row_t, col_t, gate_t)):
                                        last = nc.scalar.copy(dst[:, t * P:(t + 1) * P],
                                                              bank[:, t % 2, j * P:(j + 1) * P])
                                    last.then_inc(route_copied, 1)

                            @block.vector
                            def _(dve):
                                for k in range(KD):
                                    dve.wait_ge(r_xt_psum, k + 1)
                                    nc.vector.tensor_copy(xt1[:, k, :], bank[:, k % 2, :]).then_inc(r_xt_copied, 1)
                                for k in range(KD):
                                    dve.wait_ge(x_high, k + 1)
                                    nc.vector.tensor_tensor(x_l[:, k, :], xt1[:, k, :], x_h[:, k, :].bitcast(F32),
                                                            ALU.subtract).then_inc(x_low, 1)
                                step = [0]

                                def then_wait(ins):
                                    step[0] += 1
                                    ins.then_inc(route, 1)
                                    dve.wait_ge(route, step[0])

                                def top16(score, left, value, index, n):
                                    for s in range(n):
                                        ins = nc.vector.max(value[:, s, 0:8], score[:, s, :])
                                    then_wait(ins)
                                    for s in range(n):
                                        ins = nc.vector.match_replace(out=left[:, s, :], in_to_replace=value[:, s, 0:8],
                                                                      in_values=score[:, s, :], imm_value=-HUGE)
                                    then_wait(ins)
                                    for s in range(n):
                                        nc.vector.max(value[:, s, 8:16], left[:, s, :])
                                        ins = nc.vector.max_index(out=index[:, s, 0:8], in_max=value[:, s, 0:8],
                                                                  in_values=score[:, s, :])
                                    then_wait(ins)
                                    for s in range(n):
                                        ins = nc.vector.max_index(out=index[:, s, 8:16], in_max=value[:, s, 8:16],
                                                                  in_values=left[:, s, :])
                                    then_wait(ins)

                                first16 = iota[:, 0:TOPK].unsqueeze(1).broadcast_to([P, PH * TOPK, TOPK])
                                for t in range(NT):
                                    dve.wait_ge(keysc_copied, 4 * (t + 1))
                                    top16(keysc[:, t % 2], rest, best, best_i, SEG)
                                    nc.vector.tensor_copy(best_f[:], best_i[:])
                                    then_wait(nc.vector.tensor_tensor(
                                        pair[:].rearrange("p h (a b) -> p h a b", b=TOPK),
                                        best[:, 0:PH, :].unsqueeze(3).broadcast_to([P, PH, TOPK, TOPK]),
                                        best[:, PH:SEG, :].unsqueeze(2).broadcast_to([P, PH, TOPK, TOPK]), ALU.add))
                                    top16(pair, pair_rest, won, won_i[:].rearrange("p (h k) -> p h k", h=PH), PH)
                                    nc.vector.tensor_tensor(gate_d[:], won[:], won[:, :, 0:1].broadcast_to([P, PH, TOPK]),
                                                            ALU.subtract).then_inc(gate_shift, 1)
                                    nc.vector.tensor_scalar(half_i[:, 0, :], won_i[:], 4, None, ALU.logical_shift_right)
                                    then_wait(nc.vector.tensor_scalar(half_i[:, 1, :], won_i[:], TOPK - 1, None,
                                                                      ALU.bitwise_and))
                                    then_wait(nc.vector.tensor_copy(half_f[:], half_i[:]))
                                    if t >= 2:
                                        dve.wait_ge(route_turned, t - 1)
                                    for half in range(2):
                                        then_wait(nc.vector.tensor_tensor(
                                            hit[:], first16,
                                            half_f[:, half, :].unsqueeze(2).broadcast_to([P, PH * TOPK, TOPK]),
                                            ALU.is_equal))
                                        then_wait(nc.vector.tensor_tensor(
                                            hit[:].rearrange("p (h k) a -> p h k a", h=PH),
                                            hit[:].rearrange("p (h k) a -> p h k a", h=PH),
                                            best_f[:, half * PH:(half + 1) * PH, :].unsqueeze(2).broadcast_to(
                                                [P, PH, TOPK, TOPK]), ALU.mult))
                                        then_wait(nc.vector.reduce_sum(chosen[:, t % 2, half, :], hit[:], AX.X))
                                    dve.wait_ge(gate_exp, t + 1)
                                    then_wait(nc.vector.reduce_sum(gate_s[:], gate_e[:], AX.X))
                                    then_wait(nc.vector.reciprocal(gate_r[:], gate_s[:]))
                                    nc.vector.tensor_tensor(
                                        chosen[:, t % 2, 2, :].rearrange("p (h k) -> p h k", h=PH), gate_e[:],
                                        gate_r[:].unsqueeze(2).broadcast_to([P, PH, TOPK]),
                                        ALU.mult).then_inc(routed, 1)
                                    dve.wait_ge(routed, t + 1)
                    rows = sb(ctx, "rows", [P, 16, NK])
                    cols = sb(ctx, "cols", [P, 16, NK])
                    stage = sb(ctx, "stage", [P, 2, NK, CHUNK])
                    with nc.Block() as block:
                        def four_of(pair, half, it, f):
                            return pair * 32 + it * 8 + (half * 16 + f)

                        def tile_of(pair, half, it, tile):
                            return pair * 8 + it * 2 + (half * 4 + tile)

                        @block.sync
                        def _(sp):
                            sp.dma_start(e_raw[:, 0], peer_u[layer, ROUTE_TILES]).then_inc(h_land[0], 16)
                            with sp.Fori(0, GATE_TILES // 2) as i:
                                for ahead, slot in ((1, 1), (2, 0)):
                                    sp.wait_ge(h_low, i * 2 + (ahead + 1))
                                    sp.dma_start(e_raw[:, slot], peer_u[layer, i * 2 + (ROUTE_TILES + ahead)]
                                                 ).then_inc(h_land[slot], 16)

                        @block.gpsimd
                        def _(pool):
                            def low(n, slot):
                                pool.wait_ge(h_high, n + 1)
                                nc.gpsimd.tensor_tensor(e_l[:, slot], e_raw[:, slot], e_h[:, slot].bitcast(F32),
                                                        ALU.subtract).then_inc(h_low, 1)

                            pool.sem_inc(h_low, 2)
                            low(0, 0)
                            with pool.Fori(0, GATE_TILES // 2) as i:
                                low(i * 2 + 1, 1)
                                low(i * 2 + 2, 0)

                        @block.vector
                        def _(dve):
                            with dve.Fori(0, 4) as pair:
                                for half in range(2):
                                    with dve.Fori(0, 2) as it:
                                        for f in range(8):
                                            four = four_of(pair, half, it, f)
                                            tok = pair * P + it * 32 + (half * CHUNK + 4 * f)
                                            dve.wait_ge(gate_mm, four + 1)
                                            nc.vector.tensor_tensor(
                                                cols[:, 4 * (f % 4):4 * (f % 4) + 4, :],
                                                iota[:].unsqueeze(1).broadcast_to([P, 4, NK]),
                                                col_t[:, bass.ds(tok, 4)].unsqueeze(2).broadcast_to([P, 4, NK]),
                                                ALU.is_equal)
                                            for s in range(4):
                                                ins = nc.vector.tensor_scalar(rows[:, 4 * (f % 4) + s, :], iota[:],
                                                                              row_t[:, bass.ds(tok + s, 1)],
                                                                              gate_t[:, bass.ds(tok + s, 1)],
                                                                              ALU.is_equal, ALU.mult)
                                            ins.then_inc(rows_ready, 1)

                        @block.tensor
                        def _(pe):
                            pe.sem_inc(gate_mm, 4)
                            pe.sem_inc(h_hid, 2)
                            with pe.Fori(0, 4) as pair:
                                for half in range(2):
                                    with pe.Fori(0, 2) as it:
                                        for f in range(8):
                                            four = four_of(pair, half, it, f)
                                            pe.wait_ge(rows_ready, four + 1)
                                            pe.wait_ge(gate_copied, four + 1)
                                            for s in range(4):
                                                slot = 4 * (f % 4) + s
                                                mm = nc.tensor.matmul(bank[:, f % 4, s * NK:(s + 1) * NK],
                                                                      rows[:, slot, :], cols[:, slot, :],
                                                                      start=True, stop=True)
                                            mm.then_inc(gate_mm, 1)
                                            tile, quarter = f // 4, f % 4
                                            if quarter == 0:
                                                m = tile_of(pair, half, it, tile)
                                                pe.wait_ge(h_low, m + 3)
                                                pe.wait_ge(h_gelu, m + 1)
                                            for k in (2 * quarter, 2 * quarter + 1):
                                                for c, (w, x_part) in enumerate(passes(
                                                        e_h[:, tile, k, :], e_l[:, tile, k, :], x_h[:, k, :], x_l[:, k, :])):
                                                    mm = nc.tensor.matmul(bank[:, 6 + tile, :], w, x_part,
                                                                          start=(k == 0 and c == 0),
                                                                          stop=(k == KD - 1 and c == 2))
                                            if quarter == 3:
                                                mm.then_inc(h_hid, 1)

                        @block.scalar
                        def _(act):
                            def split(n, slot, run):
                                act.wait_ge(h_land[slot], run)
                                act.wait_ge(h_hid, n + 1)
                                nc.scalar.copy(e_h[:, slot], e_raw[:, slot]).then_inc(h_high, 1)

                            act.sem_inc(gate_copied, 4)
                            act.sem_inc(h_gelu, 2)
                            split(0, 0, 16)
                            with act.Fori(0, 4) as pair:
                                for half in range(2):
                                    act.wait_ge(gate_store[half], pair * (16 * JG))
                                    with act.Fori(0, 2) as it:
                                        runs = pair * 4 + it + half * 2
                                        for f in range(8):
                                            four, tile = four_of(pair, half, it, f), f // 4
                                            m = tile_of(pair, half, it, tile)
                                            act.wait_ge(gate_mm, four + 5)
                                            nc.scalar.copy(
                                                stage[:, half, :, bass.ds(it * 32 + 4 * f, 4)].rearrange("p j t -> p t j"),
                                                bank[:, f % 4, :].rearrange("p (t j) -> p t j", t=4)
                                            ).then_inc(gate_copied, 1)
                                            if f % 4 == 0:
                                                split(m + 1, 1 - tile, runs * 16 + (16 if tile == 0 else 32))
                                            if f % 4 == 3:
                                                act.wait_ge(h_hid, m + 3)
                                                act.wait_ge(h_store[tile], runs * 16)
                                                nc.scalar.activation(e_out[:, tile, :], bank[:, 6 + tile, :],
                                                                     ACT.Gelu).then_inc(h_gelu, 1)
                                                act.wait_ge(h_gelu, m + 3)
                                                act.dma_start(hid_dram[m + ROUTE_TILES], e_out[:, tile, :]
                                                              ).then_inc(h_store[tile], 16)
                                    act.wait_ge(gate_copied, pair * 32 + (half * 16 + 16 + 4))
                                    for j in range(JG):
                                        act.dma_start(
                                            gate_dram[:, :, j, bass.ds(pair * P + half * CHUNK, CHUNK)].rearrange(
                                                "g i t -> i g t"), stage[:, half, j::JG, :]).then_inc(gate_store[half], 16)
                            for i in range(2):
                                act.wait_ge(gate_store[i], 16 * JG * 4)
                                act.wait_ge(h_store[i], 16 * GATE_TILES // 2)
                with ExitStack() as ctx:
                    u_raw = sb(ctx, "u_raw", [P, 2, KD, P])
                    u_h = sb(ctx, "u_h", [P, JG, KD, P], F32R)
                    u_l = sb(ctx, "u_l", [P, JG, KD, P], F32R)
                    v_raw = sb(ctx, "v_raw", [P, 2, D])
                    v_h = sb(ctx, "v_h", [P, JG, D], F32R)
                    v_l = sb(ctx, "v_l", [P, JG, D], F32R)
                    gates = sb(ctx, "gates", [P, JG, T])
                    gelu = sb(ctx, "gelu", [P, 2, T])
                    weight = sb(ctx, "weight", [P, 2, T])
                    a_h = sb(ctx, "a_h", [P, JG, T], F32R)
                    a_l = sb(ctx, "a_l", [P, JG, T], F32R)
                    with nc.Block() as block:
                        @block.sync
                        def _(sp):
                            with sp.Fori(0, LATE_GROUPS) as g:
                                for j in range(JG):
                                    sp.wait_ge(u_low, g * JG + (j + 1))
                                    sp.dma_start(u_raw[:, j % 2], peer_u[layer, g * JG + (EARLY_TILES + j)]).then_inc(u_land[j % 2], 16)
                                    if j == 1:
                                        sp.wait_ge(weighted, g * JG + 2)
                                        sp.dma_start(gates[:], gate_dram[g + EARLY_GROUPS]).then_inc(g_land[0], 16)
                                for j in range(JG):
                                    sp.wait_ge(v_low, g * JG + (j + 1))
                                    sp.dma_start(v_raw[:, j % 2, :], peer_v[layer, :, g * JG + (EARLY_TILES + j), :]).then_inc(v_land[j % 2], 16)

                        @block.tensor
                        def _(pe):
                            pe.sem_inc(hid_done, JG)
                            with pe.Fori(0, LATE_GROUPS) as g:
                                for j in range(JG):
                                    n = g * JG + j
                                    pe.wait_ge(u_low, n + 3)
                                    pe.wait_ge(gelu_done, n + 1)
                                    for k in range(KD):
                                        for c, (w, m) in enumerate(passes(u_h[:, j, k, :], u_l[:, j, k, :],
                                                                          x_h[:, k, :], x_l[:, k, :])):
                                            mm = nc.tensor.matmul(bank[:, j % 2, :], w, m, start=(k == 0 and c == 0),
                                                                  stop=(k == KD - 1 and c == 2))
                                    mm.then_inc(hid_done, 1)
                                for t in range(NT):
                                    pe.wait_ge(down_added, g * NT + (t + 1))
                                    tok = slice(t * P, (t + 1) * P)
                                    for j in range(JG):
                                        if t == 0:
                                            pe.wait_ge(act_low, g * JG + (j + 1))
                                            pe.wait_ge(v_low, g * JG + (j + 3))
                                        for half in range(2):
                                            c0 = slice(half * 512, (half + 1) * 512)
                                            for c, (w, m) in enumerate(passes(a_h[:, j, tok], a_l[:, j, tok],
                                                                              v_h[:, j, c0], v_l[:, j, c0])):
                                                mm = nc.tensor.matmul(bank[:, 2 + 2 * (t % 2) + half, :], w, m,
                                                                      start=(j == 0 and c == 0),
                                                                      stop=(j == JG - 1 and c == 2))
                                    mm.then_inc(down_done, 1)

                        @block.scalar
                        def _(act):
                            def split_u(g, j):
                                act.wait_ge(u_land[j % 2], g * 32 + (16 * (j // 2) + 16))
                                act.wait_ge(hid_done, g * JG + (j + 1))
                                nc.scalar.copy(u_h[:, j], u_raw[:, j % 2]).then_inc(u_high, 1)

                            def split_v(g, j):
                                act.wait_ge(v_land[j % 2], g * 32 + (16 * (j // 2) + 16))
                                act.wait_ge(down_done, g * NT)
                                nc.scalar.copy(v_h[:, j, :], v_raw[:, j % 2, :]).then_inc(v_high, 1)

                            def activate(n, j):
                                act.wait_ge(hid_done, n + (JG + 1))
                                act.wait_ge(weighted, n + 1)
                                nc.scalar.activation(gelu[:, j % 2, :], bank[:, j % 2, :], ACT.Gelu).then_inc(gelu_done, 1)
                                act.wait_ge(weighted, n + 3)
                                act.wait_ge(down_done, n - j)
                                nc.scalar.copy(a_h[:, j, :], weight[:, j % 2, :]).then_inc(act_high, 1)

                            def group(g, first):
                                if not first:
                                    activate(g * JG - 1, JG - 1)
                                for j in range(JG):
                                    split_u(g, j)
                                for j in range(JG):
                                    split_v(g, j)
                                    if j < JG - 1:
                                        activate(g * JG + j, j)

                            act.sem_inc(gelu_done, 2)
                            group(0, True)
                            with act.Fori(1, LATE_GROUPS) as g:
                                group(g, False)
                            activate(LATE_GROUPS * JG - 1, JG - 1)

                        @block.vector
                        def _(dve):
                            def split_u(g, j):
                                dve.wait_ge(u_high, g * JG + (j + 1))
                                nc.vector.tensor_tensor(u_l[:, j], u_raw[:, j % 2], u_h[:, j].bitcast(F32),
                                                        ALU.subtract).then_inc(u_low, 1)

                            def split_v(g, j):
                                dve.wait_ge(v_high, g * JG + (j + 1))
                                nc.vector.tensor_tensor(v_l[:, j, :], v_raw[:, j % 2, :], v_h[:, j, :].bitcast(F32),
                                                        ALU.subtract).then_inc(v_low, 1)

                            def activate(n, j):
                                if j == 0:
                                    dve.wait_ge(g_land[0], n * (16 // JG) + 16)
                                dve.wait_ge(gelu_done, n + 3)
                                nc.vector.tensor_tensor(weight[:, j % 2, :], gelu[:, j % 2, :], gates[:, j, :],
                                                        ALU.mult).then_inc(weighted, 1)
                                dve.wait_ge(act_high, n + 1)
                                nc.vector.tensor_tensor(a_l[:, j, :], weight[:, j % 2, :], a_h[:, j, :].bitcast(F32),
                                                        ALU.subtract).then_inc(act_low, 1)

                            def add_down(g, t):
                                dve.wait_ge(down_done, g * NT + (t + 1))
                                b = 2 + 2 * (t % 2)
                                nc.vector.tensor_tensor(x[:, t, :], x[:, t, :],
                                                        bank[:, b:b + 2, :].rearrange("p b n -> p (b n)"),
                                                        ALU.add).then_inc(down_added, 1)

                            def group(g, first):
                                if not first:
                                    activate(g * JG - 1, JG - 1)
                                for j in range(JG):
                                    split_u(g, j)
                                    if not first:
                                        add_down(g - 1, j)
                                for j in range(JG):
                                    split_v(g, j)
                                    if j < JG - 1:
                                        activate(g * JG + j, j)

                            dve.sem_inc(u_low, 2)
                            dve.sem_inc(v_low, 2)
                            dve.sem_inc(weighted, 2)
                            for t in range(NT):
                                nc.vector.tensor_scalar(x[:, t, :], x[:, t, :], ALPHA, None,
                                                        ALU.mult).then_inc(x_scaled, 1)
                            dve.wait_ge(x_scaled, NT)
                            dve.sem_inc(down_added, 2)
                            group(0, True)
                            with dve.Fori(1, LATE_GROUPS) as g:
                                group(g, False)
                            activate(LATE_GROUPS * JG - 1, JG - 1)
                            for t in range(NT):
                                add_down(LATE_GROUPS - 1, t)
            with ExitStack() as ctx:
                f_hid = sb(ctx, "f_hid", [P, 2, JG, T])
                f_gates = sb(ctx, "f_gates", [P, 2, JG, T])
                f_raw = sb(ctx, "f_raw", [P, 2, D])
                f_weight = sb(ctx, "f_weight", [P, 2, T])
                fv_h = sb(ctx, "fv_h", [P, 2, JG, D], F32R)
                fv_l = sb(ctx, "fv_l", [P, 2, JG, D], F32R)
                fa_h = sb(ctx, "fa_h", [P, 2, JG, T], F32R)
                fa_l = sb(ctx, "fa_l", [P, 2, JG, T], F32R)
                with nc.Block() as block:
                    def each_group(engine, group):
                        group(0, 0, True)
                        with engine.Fori(0, (EARLY_GROUPS - 1) // 2) as i:
                            group(i * 2 + 1, 1, False)
                            group(i * 2 + 2, 0, False)

                    @block.sync
                    def _(sp):
                        def group(g, b, first):
                            sp.wait_ge(f_weighted, g * JG + JG)
                            sp.dma_start(f_hid[:, b], hid_dram[bass.ts(g, JG)].rearrange("j p t -> p j t")
                                         ).then_inc(f_land[b], 16)
                            sp.dma_start(f_gates[:, b], gate_dram[g]).then_inc(f_land[b], 16)
                            for j in range(JG):
                                sp.wait_ge(fv_low, g * JG + (j + 1))
                                sp.dma_start(f_raw[:, j % 2, :], peer_v[layer, :, g * JG + j, :]
                                             ).then_inc(fv_land[j % 2], 16)

                        each_group(sp, group)

                    @block.tensor
                    def _(pe):
                        pe.sem_inc(f_done, 2 * NT)

                        def group(g, b, first):
                            for t in range(NT):
                                pe.wait_ge(f_added, g * NT + (t + 1))
                                tok = slice(t * P, (t + 1) * P)
                                for j in range(JG):
                                    if t == 0:
                                        pe.wait_ge(fa_low, g * JG + (j + 1))
                                        pe.wait_ge(fv_low, g * JG + (j + 3))
                                    for half in range(2):
                                        c0 = slice(half * 512, (half + 1) * 512)
                                        for c, (w, m) in enumerate(passes(fa_h[:, b, j, tok], fa_l[:, b, j, tok],
                                                                          fv_h[:, b, j, c0], fv_l[:, b, j, c0])):
                                            mm = nc.tensor.matmul(bank[:, 2 * (t % 2) + half, :], w, m,
                                                                  start=(j == 0 and c == 0),
                                                                  stop=(j == JG - 1 and c == 2))
                                mm.then_inc(f_done, 1)

                        each_group(pe, group)

                    @block.scalar
                    def _(act):
                        def group(g, b, first):
                            act.wait_ge(f_done, g * NT + NT)
                            for j in range(JG):
                                act.wait_ge(fv_land[j % 2], g * 32 + (16 * (j // 2) + 16))
                                nc.scalar.copy(fv_h[:, b, j, :], f_raw[:, j % 2, :]).then_inc(fv_high, 1)
                                act.wait_ge(f_weighted, g * JG + (j + 1 + 2 * JG))
                                nc.scalar.copy(fa_h[:, b, j, :], f_weight[:, j % 2, :]).then_inc(fa_high, 1)

                        each_group(act, group)

                    @block.vector
                    def _(dve):
                        def add(g, t):
                            dve.wait_ge(f_done, g * NT + (t + 1 + 2 * NT))
                            nc.vector.tensor_tensor(
                                x[:, t, :], x[:, t, :],
                                bank[:, 2 * (t % 2):2 * (t % 2) + 2, :].rearrange("p b n -> p (b n)"),
                                ALU.add).then_inc(f_added, 1)

                        def group(g, b, first):
                            dve.wait_ge(f_land[b], 32 if first else (g + (2 - b)) * 16)
                            for j in range(JG):
                                nc.vector.tensor_tensor(f_weight[:, j % 2, :], f_hid[:, b, j, :],
                                                        f_gates[:, b, j, :], ALU.mult).then_inc(f_weighted, 1)
                                dve.wait_ge(fv_high, g * JG + (j + 1))
                                nc.vector.tensor_tensor(fv_l[:, b, j, :], f_raw[:, j % 2, :],
                                                        fv_h[:, b, j, :].bitcast(F32),
                                                        ALU.subtract).then_inc(fv_low, 1)
                                dve.wait_ge(fa_high, g * JG + (j + 1))
                                nc.vector.tensor_tensor(fa_l[:, b, j, :], f_weight[:, j % 2, :],
                                                        fa_h[:, b, j, :].bitcast(F32),
                                                        ALU.subtract).then_inc(fa_low, 1)
                                if not first:
                                    add(g - 1, j)

                        dve.sem_inc(f_weighted, 2 * JG)
                        dve.sem_inc(fv_low, 2)
                        dve.sem_inc(f_added, 2)
                        each_group(dve, group)
                        for t in range(NT):
                            add(EARLY_GROUPS - 1, t)
            layer_norm(nc, layer, 1, x, bank, ln_gb, ln_sems[1])

        stored = top.enter_context(nc.semaphore("stored"))
        with nc.Block() as block:
            @block.sync
            def _(sp):
                for t in range(NT):
                    sp.dma_start(out[t * P:(t + 1) * P, :], x[:, t, :]).then_inc(stored, 16)
                sp.wait_ge(stored, 16 * NT)


def _rotary():
    tab = np.zeros((2, P, 2, T), np.float32)
    for which, dim in ((0, HD), (1, ROPE)):
        inv = (np.float32(10000.0) ** (-np.arange(0, dim, 2, dtype=np.float32) / np.float32(dim))).astype(np.float32)
        ang = np.arange(T, dtype=np.float32)[:, None] * inv[None, :]
        cos, sin = np.cos(ang).T, np.sin(ang).T
        c, s = np.concatenate([cos, cos]), np.concatenate([-sin, sin])
        if which == 0:
            tab[0, :, 0], tab[0, :, 1] = np.concatenate([c, c]), np.concatenate([s, s])
        else:
            tab[1, NOPE:QK, 0], tab[1, NOPE:QK, 1] = c, s
    return tab


def _swap(start, dim):
    return [start + (f + dim // 2) % dim for f in range(dim)]


def _in_columns():
    aq, akv, akr = 0, Q_RANK, Q_RANK + KV_RANK
    bq = akr + ROPE
    bk, bv = bq + B_HEADS * HD, bq + 2 * B_HEADS * HD
    cq = bv + B_HEADS * HD
    ck = cq + C_HEADS * HD
    cv = ck + 2 * HD
    tiles = [list(range(m * P, (m + 1) * P)) for m in range(KQ + KKV)]
    kr = list(range(akr, akr + ROPE)) + _swap(akr, ROPE)
    tiles.append(kr + kr)
    tiles += [list(range(bq + m * P, bq + (m + 1) * P)) for m in range(2)]
    tiles += [list(range(bk + m * P, bk + (m + 1) * P)) for m in range(2)]
    heads = _c_heads()
    for swapped in (False, True):
        for m in range(2):
            cols = []
            for h in heads[2 * m:2 * m + 2]:
                cols += _swap(cq + h * HD, HD) if swapped else list(range(cq + h * HD, cq + (h + 1) * HD))
            tiles.append(cols)
    tiles.append(list(range(ck, ck + P)))
    tiles.append(_swap(ck, HD) + _swap(ck + HD, HD))
    values = list(range(bv, bv + B_HEADS * HD)) + list(range(cv, cv + 2 * HD))
    return tiles, values


def _c_heads():
    return [(s % 2) * 2 + s // 2 for s in range(C_HEADS)]


def kernel(**inputs):
    import concourse.bacc as _bacc
    from concourse import mybir as _mybir
    from concourse.bass_utils import run_bass_kernel_spmd as _run

    g = {k: np.asarray(v) for k, v in inputs.items()}
    L = DEPTH
    heads = _c_heads()
    tiles, values = _in_columns()
    w_in = g["w_in"].reshape(L, KD, P, -1)
    uq = g["mla_w_uq"].reshape(L, KQ, P, A_HEADS, QK)
    ukv = g["mla_w_ukv"].reshape(L, KKV, P, A_HEADS, NOPE + V_DIM)
    mix_rows = list(range(768)) + [768 + h * HD + d for h in heads for d in range(HD)]
    arrays = {
        "x_in": g["x"].reshape(T, D),
        "rope_tab": _rotary(),
        "w_in": w_in[..., np.array(tiles)].transpose(0, 3, 2, 1, 4),
        "w_v": w_in[..., np.array(values)].transpose(0, 2, 1, 3),
        "norms": np.concatenate([g["mla_q_norm"], g["mla_kv_norm"]], 1).reshape(L, KQ + KKV, P).transpose(0, 2, 1),
        "w_uq": uq[..., np.array(list(range(QK)) + _swap(NOPE, ROPE))].transpose(0, 2, 1, 3, 4),
        "w_uk": ukv[..., :NOPE].transpose(0, 2, 1, 3, 4).reshape(L, P, KKV, -1),
        "w_uv": ukv[..., NOPE:].transpose(0, 2, 1, 3, 4).reshape(L, P, KKV, -1),
        "rel_bias": g["rel_bias"][:, :, ::-1].reshape(L * B_HEADS, REL_TABLE),
        "sinks": g["swa_sinks"][:, np.array(heads)],
        "w_out": g["w_out"][:, np.array(mix_rows)].reshape(L, KD, P, D).transpose(0, 2, 1, 3),
        "ln_gb": np.stack([np.stack([g["ln1_g"], g["ln1_b"]], 1), np.stack([g["ln2_g"], g["ln2_b"]], 1)], 1),
        "peer_wq": g["peer_wq"].reshape(L, KD, P, PH, P).transpose(0, 3, 2, 1, 4),
        "peer_keys": g["peer_keys"].transpose(0, 2, 4, 1, 3).reshape(L, P, PH, NK),
        "peer_u": g["peer_u"].reshape(L, NK, NK, KD, P).transpose(0, 2, 4, 3, 1),
        "peer_v": g["peer_v"].reshape(L, NK, NK, D),
    }
    nc = _bacc.Bacc("TRN2", target_bir_lowering=False, num_devices=1)
    given, args = {}, []
    for name, a in arrays.items():
        a = np.ascontiguousarray(a)
        given[f"in_{name}"] = a
        args.append(nc.dram_tensor(f"in_{name}", a.shape, _mybir.dt.from_np(a.dtype), kind="ExternalInput").ap())
    result = nc.dram_tensor("result", (T, D), F32, kind="ExternalOutput").ap()
    program(nc, *args, result)
    r = _run(nc, [given], core_ids=[0])
    return r.results[0]["result"].reshape(1, T, D)
```

```python
import math
from contextlib import ExitStack

import numpy as np
import concourse.bass as bass
from concourse import mybir

F32 = mybir.dt.float32
F32R = mybir.dt.float32r
U32 = mybir.dt.uint32
ALU = mybir.AluOpType
ACT = mybir.ActivationFunctionType
AX = mybir.AxisListType

P = 128
D = 1024
T = 512
DEPTH = 2
KD = D // P
NT = T // P
ALPHA = (2.0 * DEPTH) ** 0.25
LN_EPS = 1e-5
RMS_EPS = 1e-6
MASKED = -1e30
HUGE = 3e38
CHUNK = 64

Q_RANK, KV_RANK, ROPE, NOPE, V_DIM, A_HEADS = 384, 256, 32, 64, 64, 8
QK = NOPE + ROPE
KQ, KKV = Q_RANK // P, KV_RANK // P
B_HEADS, C_HEADS, HD = 4, 4, 64
MAX_REL = 256
REL_TABLE = (CHUNK - 1) + MAX_REL + 1
REL_ROW = 640
V_COLS = 384

PH, NK, TOPK, KEY_HALF = 8, 128, 16, 64
SEG = 2 * PH
JG = 4
GROUPS = NK // JG
ROUTE_TILES = 40
GATE_TILES = 32
STORE_TILES = 4
EARLY_TILES = ROUTE_TILES + GATE_TILES + STORE_TILES
EARLY_GROUPS = EARLY_TILES // JG
LATE_GROUPS = GROUPS - EARLY_GROUPS


def passes(high, low, other_high, other_low):
    return ((high, other_high), (high, other_low), (low, other_high))


def norm_buffers(ctx, nc, which, gb, scaled):
    names = ("neg_mean", "var", "inv", "work")
    return {"gb": gb, "scaled": scaled} | {
        k: ctx.enter_context(nc.sbuf_tensor(f"ln_{k}{which}", [P, NT], F32)) for k in names}


def norm_on_act(nc, act, t, x, unused, n, s):
    act.wait_ge(s["mean"], t + 1)
    nc.scalar.activation(unused, x[:, t, :], ACT.Square, bias=n["neg_mean"][:, t:t + 1],
                         accum_out=n["var"][:, t:t + 1]).then_inc(s["squares"], 1)
    act.wait_ge(s["var"], t + 1)
    nc.scalar.activation(n["inv"][:, t:t + 1], n["var"][:, t:t + 1], ACT.Sqrt).then_inc(s["root"], 1)


def add_and_norm(nc, dve, t, x, b, n, s):
    mean = n["neg_mean"][:, t:t + 1]
    nc.vector.tensor_tensor_reduce(out=x[:, t, :], in0=x[:, t, :], in1=b, scale=1.0, scalar=0.0, op0=ALU.add,
                                   op1=ALU.add, accum_out=mean).then_inc(s["sum"], 1)
    dve.wait_ge(s["sum"], t + 1)
    nc.vector.tensor_scalar(mean, mean, -1.0 / D, None, ALU.mult).then_inc(s["mean"], 1)
    if t == 0:
        dve.wait_ge(s["land"], 16)
    dve.wait_ge(s["mean"], t + 1)
    nc.vector.scalar_tensor_tensor(out=n["scaled"][t % 2], in0=x[:, t, :], scalar=mean, in1=n["gb"][:, 0, :],
                                   op0=ALU.add, op1=ALU.mult).then_inc(s["scaled"], 1)


def mean_square(nc, dve, t, n, s):
    var = n["var"][:, t:t + 1]
    dve.wait_ge(s["squares"], t + 1)
    nc.vector.tensor_scalar(var, var, 1.0 / D, LN_EPS, ALU.mult, ALU.add).then_inc(s["var"], 1)


def norm_by_root(nc, dve, t, x, n, s):
    var, y, z = (n[k][:, t:t + 1] for k in ("var", "inv", "work"))
    dve.wait_ge(s["root"], t + 1)
    steps = (lambda: nc.vector.reciprocal(y, y),
             lambda: nc.vector.tensor_tensor(z, y, y, ALU.mult),
             lambda: nc.vector.scalar_tensor_tensor(out=z, in0=z, scalar=-0.5, in1=var, op0=ALU.mult, op1=ALU.mult),
             lambda: nc.vector.scalar_tensor_tensor(out=y, in0=z, scalar=1.5, in1=y, op0=ALU.add, op1=ALU.mult))
    for c, take in enumerate(steps):
        take().then_inc(s["chain"], 1)
        dve.wait_ge(s["chain"], len(steps) * t + c + 1)
    dve.wait_ge(s["scaled"], t + 1)
    nc.vector.scalar_tensor_tensor(out=x[:, t, :], in0=n["scaled"][t % 2], scalar=y, in1=n["gb"][:, 1, :],
                                   op0=ALU.mult, op1=ALU.add).then_inc(s["normed"], 1)


def program(nc, x_in, rope_tab, w_in, norms, w_up, rel_bias, sinks, w_out,
            ln_gb, peer_wq, peer_keys, peer_u, peer_v, out):
    top = ExitStack()

    def sb(ctx, name, shape, dt=F32):
        return ctx.enter_context(nc.sbuf_tensor(name, shape, dt))

    def sem(name):
        s = top.enter_context(nc.semaphore(name))
        layer_sems.append(s)
        return s

    layer_sems = []
    with top:
        bank = top.enter_context(nc.psum_tensor("bank", [P, 8, 512], F32))
        gate_dram = nc.dram_tensor("gate_dram", [T // CHUNK, P, NK, CHUNK], F32, kind="Internal")
        rel_dram = nc.dram_tensor("rel_dram", [DEPTH * B_HEADS, REL_ROW], F32, kind="Internal")
        hid_dram = nc.dram_tensor("hid_dram", [EARLY_TILES, P, T], F32, kind="Internal")
        rel_copies = nc.dram_tensor("rel_copies", [B_HEADS, P, REL_ROW], F32, kind="Internal")

        x = sb(top, "x", [P, NT, D])
        w_raw = sb(top, "w_raw", [P, 2, KD, P])
        ident = sb(top, "ident", [P, P])
        ones = sb(top, "ones", [P, P])
        iota = sb(top, "iota", [P, P])
        rope_c = sb(top, "rope_c", [P, 2, T])
        rope_a = sb(top, "rope_a", [P, T])
        mask_causal = sb(top, "mask_causal", [P, T])
        mask_window = sb(top, "mask_window", [P, 2 * P])

        setup_dma = top.enter_context(nc.semaphore("setup_dma"))
        setup_row = top.enter_context(nc.semaphore("setup_row"))
        setup_pool = top.enter_context(nc.semaphore("setup_pool"))
        setup_store = top.enter_context(nc.semaphore("setup_store"))
        with ExitStack() as ctx:
            rel_rows = sb(ctx, "rel_rows", [DEPTH * B_HEADS, REL_ROW])
            with nc.Block() as block:
                @block.sync
                def _(sp):
                    sp.dma_start(rel_rows[:, MAX_REL - 1:MAX_REL - 1 + REL_TABLE],
                                 rel_bias).then_inc(setup_row, 16)
                    for t in range(NT):
                        sp.dma_start(x[:, t, :], x_in[t * P:(t + 1) * P, :]).then_inc(setup_dma, 16)
                    sp.dma_start(rope_c[:], rope_tab[:, 0:2, :]).then_inc(setup_dma, 16)
                    sp.dma_start(rope_a[:], rope_tab[:, 2, :]).then_inc(setup_dma, 16)
                    sp.wait_ge(setup_pool, 7)
                    sp.dma_start(rel_dram[:, :], rel_rows[:]).then_inc(setup_store, 16)
                    sp.wait_ge(setup_store, 16)
                    sp.wait_ge(setup_dma, 16 * (NT + 2))

                @block.gpsimd
                def _(pool):
                    nc.gpsimd.memset(ident[:], 0.0).then_inc(setup_pool, 1)
                    nc.gpsimd.memset(ones[:], 1.0).then_inc(setup_pool, 1)
                    nc.gpsimd.memset(mask_causal[:], 0.0).then_inc(setup_pool, 1)
                    nc.gpsimd.memset(mask_window[:], 0.0).then_inc(setup_pool, 1)
                    nc.gpsimd.memset(rel_rows[:, MAX_REL - 1 + REL_TABLE:REL_ROW], 0.0).then_inc(setup_pool, 1)
                    pool.wait_ge(setup_pool, 5)
                    nc.gpsimd.affine_select(out=ident[:], in_=ident[:], compare_op=ALU.not_equal, fill=1.0,
                                            base=0, pattern=[[-1, P]], channel_multiplier=1).then_inc(setup_pool, 1)
                    pool.wait_ge(setup_row, 16)
                    nc.gpsimd.tensor_copy(rel_rows[:, 0:MAX_REL - 1],
                                          rel_rows[:, MAX_REL - 1:MAX_REL].broadcast_to(
                                              [DEPTH * B_HEADS, MAX_REL - 1])).then_inc(setup_pool, 1)
                    nc.gpsimd.iota(iota[:], pattern=[[1, P]], base=0, channel_multiplier=0,
                                   allow_small_or_imprecise_dtypes=True).then_inc(setup_pool, 1)

                @block.vector
                def _(dve):
                    dve.wait_ge(setup_pool, 5)
                    nc.vector.memset(mask_causal[0:CHUNK, T - CHUNK:T], MASKED)
                    nc.vector.memset(mask_window[0:CHUNK, 2 * P - CHUNK:2 * P], MASKED)
                    nc.vector.memset(mask_window[CHUNK:P, 0:CHUNK], MASKED)

        w_land = [sem(f"w_land{i}") for i in range(2)]
        w_high = sem("w_high")
        w_low = sem("w_low")
        xt_psum = sem("xt_psum")
        xt_high = sem("xt_high")
        xt_low = sem("xt_low")
        squared = sem("squared")
        up_land = [sem(f"up_land{i}") for i in range(KQ + 2)]
        up_high = sem("up_high")
        up_low = sem("up_low")
        up_turned = sem("up_turned")
        latent_high = sem("latent_high")
        norms_land = sem("norms_land")
        job_done = sem("job_done")
        job_free = [sem(f"job_free{i}") for i in range(5)]
        dve_step = sem("dve_step")
        up_job_done = sem("up_job_done")
        up_free = [sem(f"up_free{i}") for i in range(6)]
        squares_summed = sem("squares_summed")
        mean_squared = sem("mean_squared")
        root = sem("root")
        newton = sem("newton")
        latent_ready = sem("latent_ready")
        rel_land = sem("rel_land")
        sink_land = sem("sink_land")
        rel_masked = sem("rel_masked")
        scores_done = sem("scores_done")
        shifted = sem("shifted")
        exp_done = sem("exp_done")
        sink_exp = sem("sink_exp")
        inverse = sem("inverse")
        probs_ready = sem("probs_ready")
        probs_turned = sem("probs_turned")
        turned_copied = sem("turned_copied")
        pv_done = sem("pv_done")
        mixed_copied = sem("mixed_copied")
        wo_land = [sem(f"wo_land{i}") for i in range(2)]
        wo_high = sem("wo_high")
        wo_low = sem("wo_low")
        mixed_low = sem("mixed_low")
        mix_out = sem("mix_out")
        ln_sems = [{k: sem(f"ln_{k}{i}") for k in ("land", "sum", "mean", "scaled", "squares", "var", "root",
                                                   "chain", "normed")} for i in range(2)]
        keys_land = sem("keys_land")
        r_xt_psum = sem("r_xt_psum")
        x_high = sem("x_high")
        keysc_done = sem("keysc_done")
        keysc_copied = sem("keysc_copied")
        route = sem("route")
        gate_shift = sem("gate_shift")
        gate_exp = sem("gate_exp")
        routed = sem("routed")
        route_turned = sem("route_turned")
        route_copied = sem("route_copied")
        rows_ready = sem("rows_ready")
        x_low = sem("x_low")
        e_land = [sem(f"e_land{i}") for i in range(2)]
        e_store = [sem(f"e_store{i}") for i in range(2)]
        e_high = sem("e_high")
        e_low = sem("e_low")
        e_hid = sem("e_hid")
        e_read = sem("e_read")
        h_land = [sem(f"h_land{i}") for i in range(2)]
        h_store = [sem(f"h_store{i}") for i in range(2)]
        h_high = sem("h_high")
        h_low = sem("h_low")
        h_last_low = sem("h_last_low")
        h_hid = sem("h_hid")
        h_gelu = sem("h_gelu")
        f_land = [sem(f"f_land{i}") for i in range(2)]
        fv_land = [sem(f"fv_land{i}") for i in range(2)]
        f_weighted = sem("f_weighted")
        fv_high = sem("fv_high")
        fv_low = sem("fv_low")
        fa_high = sem("fa_high")
        fa_low = sem("fa_low")
        f_done = sem("f_done")
        f_added = sem("f_added")
        gate_mm = sem("gate_mm")
        gate_copied = sem("gate_copied")
        gate_store = [sem(f"gate_store{i}") for i in range(2)]
        u_land = [sem(f"u_land{i}") for i in range(2)]
        v_land = [sem(f"v_land{i}") for i in range(2)]
        g_land = [sem(f"g_land{i}") for i in range(2)]
        u_high = sem("u_high")
        u_low = sem("u_low")
        v_high = sem("v_high")
        v_low = sem("v_low")
        hid_done = sem("hid_done")
        gelu_done = sem("gelu_done")
        weighted = sem("weighted")
        act_high = sem("act_high")
        act_low = sem("act_low")
        down_done = sem("down_done")
        down_added = sem("down_added")
        x_scaled = sem("x_scaled")

        with nc.Fori(0, DEPTH) as layer:
            with nc.Block() as block:
                @block.gpsimd
                def _(pool):
                    numbers = sorted(s.num for s in layer_sems)
                    assert numbers == list(range(numbers[0], numbers[-1] + 1))
                    pool.sem_clear(range(numbers[0], numbers[-1] + 1))

            with ExitStack() as mixer:
                q_a = sb(mixer, "q_a", [P, A_HEADS, T])
                k_a = sb(mixer, "k_a", [P, A_HEADS, T])
                v_a = sb(mixer, "v_a", [P, NT, A_HEADS * V_DIM])
                v_bc = sb(mixer, "v_bc", [P, NT, V_COLS])
                q_b = sb(mixer, "q_b", [P, 2, T])
                k_b = sb(mixer, "k_b", [P, 2, T])
                q_c = sb(mixer, "q_c", [P, 2, T])
                k_c = sb(mixer, "k_c", [P, T])

                k_rope = sb(mixer, "k_rope", [QK, T])
                with ExitStack() as ctx:
                    latent_h = sb(ctx, "latent_h", [P, KQ + KKV, T], F32R)
                    latent_l = sb(ctx, "latent_l", [P, KQ + KKV, T], F32R)
                    turn = sb(ctx, "turn", [P, 2, T])
                    up_pair = sb(ctx, "up_pair", [P, 2, D])
                    up_raw = [up_pair[:, 0, :], up_pair[:, 1, :],
                              v_a[:, 0:2, :].rearrange("p t n -> p (t n)"),
                              v_a[:, 2:4, :].rearrange("p t n -> p (t n)"), up_pair[:, 0, :]]
                    with ExitStack() as inner:
                        xt_h = sb(inner, "xt_h", [P, KD, T], F32R)
                        xt_l = sb(inner, "xt_l", [P, KD, T], F32R)
                        wt_h = sb(inner, "wt_h", [P, 2, KD, P], F32R)
                        wt_l = sb(inner, "wt_l", [P, 2, KD, P], F32R)
                        wv_h = sb(inner, "wv_h", [P, KD, V_COLS], F32R)
                        wv_l = sb(inner, "wv_l", [P, KD, V_COLS], F32R)
                        gains = sb(inner, "gains", [P, KQ + KKV])
                        scale_row = sb(inner, "scale_row", [P, 2, T])
                        mean_sq = k_a[:, KQ + KKV:KQ + KKV + 2, :]
                        jobs = [("latent", m) for m in range(KQ + KKV)] + [("k_rope", 0)]
                        jobs += [("q_b", m) for m in range(2)] + [("k_b", m) for m in range(2)]
                        jobs += [("q_c", m) for m in range(2)] + [("k_c", 0)]
                        AHEAD = 4
                        turn_bank = (0, 1, 6, 7)
                        W_JOBS = len(jobs)
                        jobs += [("values", t) for t in range(NT)]
                        W_TILES = W_JOBS + V_COLS // P
                        SUM_AFTER = KQ + KKV + 2
                        raw_latent, square = q_a, k_a

                        def job_bank(n):
                            return bank[:, 2 + n % 5, :]

                        with nc.Block() as block:
                            @block.sync
                            def _(sp):
                                sp.dma_start(gains[:], norms[layer]).then_inc(norms_land, 16)
                                for n in range(W_TILES):
                                    if n >= 2:
                                        sp.wait_ge(w_low, n - 1)
                                    sp.dma_start(w_raw[:, n % 2], w_in[layer, n]).then_inc(w_land[n % 2], 16)
                                for n in range(4):
                                    sp.dma_start(up_raw[n], w_up[layer, n]).then_inc(up_land[n], 16)

                            @block.gpsimd
                            def _(pool):
                                for n in range(W_TILES):
                                    pool.wait_ge(w_high, n + 1)
                                    if n < W_JOBS:
                                        low, high = wt_l[:, n % 2], wt_h[:, n % 2]
                                    else:
                                        cs = slice((n - W_JOBS) * P, (n - W_JOBS + 1) * P)
                                        low, high = wv_l[:, :, cs], wv_h[:, :, cs]
                                    nc.gpsimd.tensor_tensor(low, w_raw[:, n % 2], high.bitcast(F32),
                                                            ALU.subtract).then_inc(w_low, 1)

                            @block.tensor
                            def _(pe):
                                def turn(k):
                                    if k >= 4:
                                        pe.wait_ge(xt_low, k - 3)
                                    for t in range(NT):
                                        mm = nc.tensor.transpose(bank[:, turn_bank[k % 4], t * P:(t + 1) * P],
                                                                 x[:, t, k * P:(k + 1) * P], ident[:])
                                    mm.then_inc(xt_psum, 1)

                                for k in range(AHEAD):
                                    turn(k)
                                for n, (kind, m) in enumerate(jobs):
                                    if n >= 5:
                                        pe.wait_ge(job_free[n % 5], n // 5)
                                    if kind == "values":
                                        if m == 0:
                                            pe.wait_ge(w_low, W_TILES)
                                        tok = slice(m * P, (m + 1) * P)
                                        for k in range(KD):
                                            for c, (w, v) in enumerate(passes(xt_h[:, k, tok], xt_l[:, k, tok],
                                                                              wv_h[:, k, :], wv_l[:, k, :])):
                                                mm = nc.tensor.matmul(job_bank(n)[:, 0:V_COLS], w, v,
                                                                      start=(k == 0 and c == 0),
                                                                      stop=(k == KD - 1 and c == 2))
                                    else:
                                        pe.wait_ge(w_low, n + 1)
                                        for k in range(KD):
                                            if n == 0:
                                                if k + AHEAD < KD:
                                                    turn(k + AHEAD)
                                                pe.wait_ge(xt_low, k + 1)
                                            for c, (w, v) in enumerate(passes(wt_h[:, n % 2, k, :], wt_l[:, n % 2, k, :],
                                                                              xt_h[:, k, :], xt_l[:, k, :])):
                                                mm = nc.tensor.matmul(job_bank(n), w, v, start=(k == 0 and c == 0),
                                                                      stop=(k == KD - 1 and c == 2))
                                    mm.then_inc(job_done, 1)
                                    if n == SUM_AFTER:
                                        pe.wait_ge(squared, KQ + KKV)
                                        for part, (m0, m1) in enumerate(((0, KQ), (KQ, KQ + KKV))):
                                            for i in range(m0, m1):
                                                mm = nc.tensor.matmul(bank[:, 7 * part, :], ones[:], square[:, i, :],
                                                                      start=(i == m0), stop=(i == m1 - 1))
                                            mm.then_inc(squares_summed, 1)

                            @block.scalar
                            def _(act):
                                def split_weights(n):
                                    act.wait_ge(w_land[n % 2], 16 * (n // 2 + 1))
                                    if n < W_JOBS:
                                        if n >= 2:
                                            act.wait_ge(job_done, n - 1)
                                        high = wt_h[:, n % 2]
                                    else:
                                        high = wv_h[:, :, (n - W_JOBS) * P:(n - W_JOBS + 1) * P]
                                    nc.scalar.copy(high, w_raw[:, n % 2]).then_inc(w_high, 1)

                                for k in range(KD):
                                    act.wait_ge(xt_psum, k + 1)
                                    nc.scalar.copy(xt_h[:, k, :], bank[:, turn_bank[k % 4], :]).then_inc(xt_high, 1)
                                    if k == 2:
                                        split_weights(0)
                                split_weights(1)
                                for n, (kind, m) in enumerate(jobs):
                                    if n <= W_JOBS - 3:
                                        split_weights(n + 2)
                                    if W_JOBS - 3 <= n < W_TILES - 3:
                                        split_weights(n + 3)
                                    if kind == "k_c":
                                        for part in range(KQ + KKV):
                                            act.wait_ge(latent_ready, part + 1)
                                            nc.scalar.copy(latent_h[:, part, :], raw_latent[:, part, :]).then_inc(latent_high, 1)
                                    if kind in ("k_rope", "q_c", "k_c"):
                                        continue
                                    act.wait_ge(job_done, n + 1)
                                    if kind == "latent":
                                        nc.scalar.activation(square[:, m, :], job_bank(n), ACT.Square).then_inc(squared, 1)
                                        nc.scalar.copy(raw_latent[:, m, :], job_bank(n)).then_inc(job_free[n % 5], 1)
                                    elif kind == "q_b":
                                        nc.scalar.mul(q_b[:, m, :], job_bank(n), HD ** -0.5).then_inc(job_free[n % 5], 1)
                                    elif kind == "k_b":
                                        nc.scalar.copy(k_b[:, m, :], job_bank(n)).then_inc(job_free[n % 5], 1)
                                        if m == 0:
                                            for part in range(2):
                                                act.wait_ge(mean_squared, part + 1)
                                                nc.scalar.activation(scale_row[:, part, :], mean_sq[:, part, :],
                                                                     ACT.Sqrt).then_inc(root, 1)
                                    else:
                                        nc.scalar.copy(v_bc[:, m, :], job_bank(n)[:, 0:V_COLS]).then_inc(job_free[n % 5], 1)

                            @block.vector
                            def _(dve):
                                for k in range(KD):
                                    dve.wait_ge(xt_high, k + 1)
                                    nc.vector.tensor_tensor(xt_l[:, k, :], bank[:, turn_bank[k % 4], :], xt_h[:, k, :].bitcast(F32),
                                                            ALU.subtract).then_inc(xt_low, 1)
                                def scale_latents():
                                    for part, rank in enumerate((Q_RANK, KV_RANK)):
                                        dve.wait_ge(squares_summed, part + 1)
                                        nc.vector.tensor_scalar(mean_sq[:, part, :], bank[:, 7 * part, :], 1.0 / rank,
                                                                RMS_EPS, ALU.mult, ALU.add).then_inc(mean_squared, 1)
                                    dve.wait_ge(norms_land, 16)
                                    for part, (m0, m1) in enumerate(((0, KQ), (KQ, KQ + KKV))):
                                        dve.wait_ge(root, part + 1)
                                        v, y, z = mean_sq[:, part, :], scale_row[:, part, :], turn[:, part, :]
                                        refine = (lambda: nc.vector.reciprocal(y, y),
                                                  lambda: nc.vector.tensor_tensor(z, y, y, ALU.mult),
                                                  lambda: nc.vector.scalar_tensor_tensor(out=z, in0=z, scalar=-0.5, in1=v,
                                                                                         op0=ALU.mult, op1=ALU.mult),
                                                  lambda: nc.vector.scalar_tensor_tensor(out=y, in0=z, scalar=1.5, in1=y,
                                                                                         op0=ALU.add, op1=ALU.mult))
                                        for c, take in enumerate(refine):
                                            take().then_inc(newton, 1)
                                            dve.wait_ge(newton, len(refine) * part + c + 1)
                                        for m in range(m0, m1):
                                            nc.vector.scalar_tensor_tensor(
                                                out=raw_latent[:, m, :], in0=raw_latent[:, m, :], scalar=gains[:, m:m + 1],
                                                in1=scale_row[:, part, :], op0=ALU.mult,
                                                op1=ALU.mult).then_inc(latent_ready, 1)

                                steps = 0
                                for n, (kind, m) in enumerate(jobs):
                                    if kind not in ("k_rope", "q_c", "k_c"):
                                        continue
                                    if (kind, m) == ("q_c", 0):
                                        scale_latents()
                                    b = job_bank(n)
                                    dve.wait_ge(job_done, n + 1)
                                    if kind == "k_rope":
                                        r = slice(NOPE, QK)
                                        nc.vector.tensor_tensor(turn[r, 0, :], b[r, :], rope_a[r, :], ALU.mult)
                                        ins = nc.vector.tensor_tensor(turn[r, 1, :], b[QK:P, :], rope_a[QK:P, :], ALU.mult)
                                        dst = k_rope[r, :]
                                    else:
                                        r = slice(0, P)
                                        nc.vector.tensor_tensor(turn[:, 0, :], b, rope_c[:, 0, :], ALU.mult)
                                        for quad in range(4):
                                            src = slice(32 * quad, 32 * quad + 32)
                                            to = slice(32 * (quad ^ 1), 32 * (quad ^ 1) + 32)
                                            ins = nc.vector.tensor_tensor(turn[to, 1, :], b[src, :], rope_c[src, 1, :],
                                                                          ALU.mult)
                                        dst = k_c[:] if kind == "k_c" else q_c[:, m, :]
                                    ins.then_inc(job_free[n % 5], 1)
                                    dve.wait_ge(job_free[n % 5], n // 5 + 1)
                                    nc.vector.tensor_tensor(dst, turn[r, 0, :], turn[r, 1, :], ALU.add).then_inc(dve_step, 1)
                                    steps += 1
                                    dve.wait_ge(dve_step, steps)
                                for m in range(KQ + KKV):
                                    dve.wait_ge(latent_high, m + 1)
                                    nc.vector.tensor_tensor(latent_l[:, m, :], raw_latent[:, m, :],
                                                            latent_h[:, m, :].bitcast(F32), ALU.subtract)
                    wuq_h = sb(ctx, "wuq_h", [P, KQ, D], F32R)
                    wuq_l = sb(ctx, "wuq_l", [P, KQ, D], F32R)
                    wuk_h = sb(ctx, "wuk_h", [P, D], F32R)
                    wuk_l = sb(ctx, "wuk_l", [P, D], F32R)
                    wuv_h = sb(ctx, "wuv_h", [P, D], F32R)
                    wuv_l = sb(ctx, "wuv_l", [P, D], F32R)
                    up_jobs = [("q", h) for h in range(A_HEADS)] + [("k", m) for m in range(A_HEADS // 2)]
                    up_jobs += [("v", t) for t in range(NT)]
                    up_reads = [2 if kind == "q" else 1 for kind, _ in up_jobs]
                    up_tiles = [(wuq_h[:, k], wuq_l[:, k], k) for k in range(KQ)]
                    up_tiles += [(wuk_h[:], wuk_l[:], KQ), (wuv_h[:], wuv_l[:], KQ + 1)]

                    with nc.Block() as block:
                        @block.sync
                        def _(sp):
                            sp.wait_ge(up_low, 1)
                            sp.dma_start(up_raw[4], w_up[layer, 4]).then_inc(up_land[4], 16)

                        @block.tensor
                        def _(pe):
                            for n, (kind, h) in enumerate(up_jobs):
                                if n >= 6:
                                    pe.wait_ge(up_free[n % 6], sum(up_reads[n % 6:n:6]))
                                b = bank[:, n % 6, :]
                                if kind == "q":
                                    for k in range(KQ):
                                        if h == 0:
                                            pe.wait_ge(up_low, k + 1)
                                        for c, (w, v) in enumerate(passes(
                                                wuq_h[:, k, h * P:(h + 1) * P], wuq_l[:, k, h * P:(h + 1) * P],
                                                latent_h[:, k, :], latent_l[:, k, :])):
                                            mm = nc.tensor.matmul(b, w, v, start=(k == 0 and c == 0),
                                                                  stop=(k == KQ - 1 and c == 2))
                                elif kind == "k":
                                    if h == 0:
                                        pe.wait_ge(up_low, KQ + 2)
                                    for k in range(KKV):
                                        cs = slice((k * A_HEADS + 2 * h) * NOPE, (k * A_HEADS + 2 * h + 2) * NOPE)
                                        for c, (w, v) in enumerate(passes(wuk_h[:, cs], wuk_l[:, cs],
                                                                          latent_h[:, KQ + k, :],
                                                                          latent_l[:, KQ + k, :])):
                                            mm = nc.tensor.matmul(b, w, v, start=(k == 0 and c == 0),
                                                                  stop=(k == KKV - 1 and c == 2))
                                else:
                                    tok = slice(h * P, (h + 1) * P)
                                    for k in range(KKV):
                                        cs = slice(k * A_HEADS * V_DIM, (k + 1) * A_HEADS * V_DIM)
                                        for c, (w, v) in enumerate(passes(latent_h[:, KQ + k, tok],
                                                                          latent_l[:, KQ + k, tok],
                                                                          wuv_h[:, cs], wuv_l[:, cs])):
                                            mm = nc.tensor.matmul(b, w, v, start=(k == 0 and c == 0),
                                                                  stop=(k == KKV - 1 and c == 2))
                                mm.then_inc(up_job_done, 1)

                        @block.scalar
                        def _(act):
                            for high, _, n in up_tiles:
                                act.wait_ge(up_land[n], 16)
                                nc.scalar.copy(high, up_raw[n]).then_inc(up_high, 1)
                            for n, (kind, h) in enumerate(up_jobs):
                                act.wait_ge(up_job_done, n + 1)
                                b = bank[:, n % 6, :]
                                if kind == "q":
                                    ins = nc.scalar.copy(q_a[0:NOPE, h, :], b[0:NOPE, :])
                                elif kind == "k":
                                    nc.scalar.copy(k_a[0:NOPE, 2 * h, :], b[0:NOPE, :])
                                    ins = nc.scalar.copy(k_a[0:NOPE, 2 * h + 1, :], b[NOPE:P, :])
                                else:
                                    ins = nc.scalar.copy(v_a[:, h, :], b)
                                ins.then_inc(up_free[n % 6], 1)

                        @block.vector
                        def _(dve):
                            for high, low, n in up_tiles:
                                dve.wait_ge(up_high, n + 1)
                                nc.vector.tensor_tensor(low, up_raw[n], high.bitcast(F32),
                                                        ALU.subtract).then_inc(up_low, 1)
                            r = slice(NOPE, QK)
                            for n, (kind, h) in enumerate(up_jobs):
                                if kind != "q":
                                    continue
                                b = bank[:, n % 6, :]
                                dve.wait_ge(up_job_done, n + 1)
                                nc.vector.tensor_tensor(turn[r, 0, :], b[r, :], rope_a[r, :], ALU.mult)
                                nc.vector.tensor_tensor(turn[r, 1, :], b[QK:P, :], rope_a[QK:P, :],
                                                        ALU.mult).then_inc(up_free[n % 6], 1)
                                dve.wait_ge(up_free[n % 6], sum(up_reads[n % 6:n + 1:6]))
                                nc.vector.tensor_tensor(q_a[r, h, :], turn[r, 0, :], turn[r, 1, :],
                                                        ALU.add).then_inc(up_turned, 1)
                                dve.wait_ge(up_turned, h + 1)

                        @block.gpsimd
                        def _(pool):
                            for h in range(A_HEADS):
                                nc.gpsimd.tensor_copy(k_a[NOPE:QK, h, :], k_rope[NOPE:QK, :])

                with ExitStack() as ctx:
                    mixed_h = sb(ctx, "mixed_h", [P, KD, T], F32R)
                    mixed_l = sb(ctx, "mixed_l", [P, KD, T], F32R)
                    wo_raw = sb(ctx, "wo_raw", [P, 2, D // 2])
                    wo_h = sb(ctx, "wo_h", [P, KD, D // 2], F32R)
                    wo_l = sb(ctx, "wo_l", [P, KD, D // 2], F32R)
                    mix_gb = sb(ctx, "mix_gb", [P, 2, D])
                    with ExitStack() as inner:
                        rel = sb(inner, "rel", [P, B_HEADS, T])
                        sink = sb(inner, "sink", [P, C_HEADS])
                        neg_sink = sb(inner, "neg_sink", [P, C_HEADS])
                        shifted_s = sb(inner, "shifted_s", [P, 4, T])
                        probs = sb(inner, "probs", [P, 4, T])
                        probs_t = sb(inner, "probs_t", [P, 4, T])
                        neg_max = sb(inner, "neg_max", [P, 64])
                        row_sum = sb(inner, "row_sum", [P, 64])
                        sink_e = sb(inner, "sink_e", [P, 16])
                        row_inv = sb(inner, "row_inv", [P, 64])
                        units = [("a", h, i) for h in range(A_HEADS) for i in range(NT)]
                        units += [("b", h, i) for h in range(B_HEADS) for i in range(NT)]
                        units += [("c", h, i) for h in range(C_HEADS) for i in range(NT)]
                        U = len(units)

                        def key_tiles(u):
                            kind, _, i = units[u]
                            return list(range(i + 1)) if kind != "c" else list(range(max(0, i - 1), i + 1))

                        def n_keys(u):
                            return P * len(key_tiles(u))

                        with nc.Block() as block:
                            @block.sync
                            def _(sp):
                                sp.dma_start(rel_copies[:, :, :].rearrange("h p n -> p h n"),
                                             rel_dram[bass.ts(layer, B_HEADS), :].partition_broadcast(P)
                                             ).then_inc(rel_land, 16)
                                sp.dma_start(sink[:], sinks[layer].partition_broadcast(P)).then_inc(sink_land, 16)
                                sp.wait_ge(rel_land, 16)
                                sp.dma_start(rel[:], bass.AP(rel_copies, P - 1, [[REL_ROW - 1, P], [P * REL_ROW, B_HEADS], [1, T]])
                                             ).then_inc(rel_land, 16)
                                for n in range(2):
                                    sp.dma_start(w_raw[:, n], peer_wq[layer, n]).then_inc(e_land[n], 16)
                                sp.dma_start(mix_gb[:], ln_gb[layer, 0].partition_broadcast(P)
                                             ).then_inc(ln_sems[0]["land"], 16)
                                for n in range(KD + 2):
                                    if n >= 2:
                                        sp.wait_ge(wo_low, n - 1)
                                    sp.dma_start(wo_raw[:, n % 2, :], w_out[layer, n // KD, n % KD]
                                                 ).then_inc(wo_land[n % 2], 16)

                            @block.gpsimd
                            def _(pool):
                                pool.wait_ge(rel_land, 32)
                                for h in range(B_HEADS):
                                    mm = nc.gpsimd.memset(rel[0:CHUNK, h, T - CHUNK:T], MASKED)
                                mm.then_inc(rel_masked, 1)
                                for t in range(NT):
                                    nc.gpsimd.tensor_scalar(x[:, t, :], x[:, t, :], ALPHA, None, ALU.mult)
                                for k in range(KD):
                                    pool.wait_ge(wo_land[k % 2], 16 * (k // 2 + 1))
                                    nc.gpsimd.tensor_copy(wo_h[:, k, :], wo_raw[:, k % 2, :]).then_inc(wo_high, 1)
                                    pool.wait_ge(wo_high, k + 1)
                                    nc.gpsimd.tensor_tensor(wo_l[:, k, :], wo_raw[:, k % 2, :],
                                                            wo_h[:, k, :].bitcast(F32), ALU.subtract).then_inc(wo_low, 1)

                            @block.tensor
                            def _(pe):
                                def scores(u):
                                    kind, h, i = units[u]
                                    if u >= 4:
                                        pe.wait_ge(shifted, u - 3)
                                    qc, kc = slice(i * P, (i + 1) * P), slice(key_tiles(u)[0] * P, (i + 1) * P)
                                    r = slice(CHUNK * (h % 2), CHUNK * (h % 2) + CHUNK)
                                    q, k = {"a": lambda: (q_a[0:QK, h, qc], k_a[0:QK, h, kc]),
                                            "b": lambda: (q_b[r, h // 2, qc], k_b[r, h // 2, kc]),
                                            "c": lambda: (q_c[r, h // 2, qc], k_c[r, kc])}[kind]()
                                    nc.tensor.matmul(bank[:, u % 4, 0:n_keys(u)], q, k, start=True,
                                                     stop=True).then_inc(scores_done, 1)

                                def turn_probs(u):
                                    pe.wait_ge(probs_ready, u + 1)
                                    if u >= 2:
                                        pe.wait_ge(turned_copied, u - 1)
                                    for j in range(len(key_tiles(u))):
                                        mm = nc.tensor.transpose(bank[:, 4 + u % 2, j * P:(j + 1) * P],
                                                                 probs[:, u % 4, j * P:(j + 1) * P], ident[:])
                                    mm.then_inc(probs_turned, 1)

                                def values(u):
                                    kind, h, i = units[u]
                                    pair = u // (2 * NT)
                                    pe.wait_ge(turned_copied, u + 1)
                                    if u % (2 * NT) == 0 and pair >= 2:
                                        pe.wait_ge(mixed_low, pair - 1)
                                    r = slice(V_DIM * (h % 2), V_DIM * (h % 2) + V_DIM)
                                    tiles_of = key_tiles(u)
                                    for j, kt in enumerate(tiles_of):
                                        v = {"a": lambda: v_a[:, kt, h * V_DIM:(h + 1) * V_DIM],
                                             "b": lambda: v_bc[:, kt, h * HD:(h + 1) * HD],
                                             "c": lambda: v_bc[:, kt, B_HEADS * HD + (h % 2) * HD:
                                                               B_HEADS * HD + (h % 2 + 1) * HD]}[kind]()
                                        mm = nc.tensor.matmul(bank[r, 6 + pair % 2, i * P:(i + 1) * P], v,
                                                              probs_t[:, u % 4, j * P:(j + 1) * P],
                                                              start=(j == 0), stop=(j == len(tiles_of) - 1))
                                    mm.then_inc(pv_done, 1)

                                for u in range(U + 5):
                                    if u < U:
                                        scores(u)
                                    if 3 <= u < U + 3:
                                        turn_probs(u - 3)
                                    if u >= 5:
                                        values(u - 5)

                            @block.scalar
                            def _(act):
                                def exponent(u):
                                    kind, h, i = units[u]
                                    n = n_keys(u)
                                    act.wait_ge(shifted, u + 1)
                                    if u >= 4:
                                        act.wait_ge(probs_turned, u - 3)
                                    if kind == "c":
                                        c = u - (U - C_HEADS * NT)
                                        nc.scalar.activation(sink_e[:, c:c + 1], sink[:, h:h + 1], ACT.Exp,
                                                             bias=neg_max[:, u:u + 1])
                                    nc.scalar.activation(probs[:, u % 4, 0:n], shifted_s[:, u % 4, 0:n], ACT.Exp,
                                                         bias=neg_max[:, u:u + 1], scale=-1.0,
                                                         accum_out=row_sum[:, u:u + 1]).then_inc(exp_done, 1)

                                def copy_turned(u):
                                    n = n_keys(u)
                                    act.wait_ge(probs_turned, u + 1)
                                    if u >= 4:
                                        act.wait_ge(pv_done, u - 3)
                                    nc.scalar.copy(probs_t[:, u % 4, 0:n],
                                                   bank[:, 4 + u % 2, 0:n]).then_inc(turned_copied, 1)

                                for u in range(U + 3):
                                    if u == 2 * NT:
                                        act.wait_ge(sink_land, 16)
                                        nc.scalar.mul(neg_sink[:], sink[:], -1.0).then_inc(sink_exp, 1)
                                    if u < U:
                                        exponent(u)
                                    if u >= 3:
                                        copy_turned(u - 3)

                            @block.vector
                            def _(dve):
                                def shift(u):
                                    kind, h, i = units[u]
                                    n = n_keys(u)
                                    bias, scale, start = {
                                        "a": lambda: (mask_causal[:, T - n:T], -QK ** -0.5, HUGE),
                                        "b": lambda: (rel[:, h, T - n:T], -1.0, HUGE),
                                        "c": lambda: (mask_window[:, 2 * P - n:2 * P], -HD ** -0.5,
                                                      neg_sink[:, h:h + 1])}[kind]()
                                    dve.wait_ge(scores_done, u + 1)
                                    if u >= 4:
                                        dve.wait_ge(exp_done, u - 3)
                                    nc.vector.tensor_tensor_reduce(
                                        out=shifted_s[:, u % 4, 0:n], in0=bank[:, u % 4, 0:n], in1=bias,
                                        scale=scale, scalar=start, op0=ALU.add, op1=ALU.min,
                                        accum_out=neg_max[:, u:u + 1]).then_inc(shifted, 1)

                                def normalise(u):
                                    dve.wait_ge(exp_done, u + 1)
                                    c = u - (U - C_HEADS * NT)
                                    if c >= 0:
                                        nc.vector.tensor_tensor(row_sum[:, u:u + 1], row_sum[:, u:u + 1],
                                                                sink_e[:, c:c + 1], ALU.add).then_inc(dve_step, 1)
                                        dve.wait_ge(dve_step, 4 + c + 1)
                                    nc.vector.reciprocal(row_inv[:, u:u + 1],
                                                         row_sum[:, u:u + 1]).then_inc(inverse, 1)
                                    dve.wait_ge(inverse, u + 1)
                                    n = n_keys(u)
                                    nc.vector.tensor_scalar(probs[:, u % 4, 0:n], probs[:, u % 4, 0:n],
                                                            row_inv[:, u:u + 1], None,
                                                            ALU.mult).then_inc(probs_ready, 1)

                                for u in range(U + 7):
                                    if u == A_HEADS * NT:
                                        dve.wait_ge(rel_masked, 1)
                                    if u == U - C_HEADS * NT:
                                        dve.wait_ge(sink_exp, 1)
                                    if u < U:
                                        shift(u)
                                    if 1 <= u <= U:
                                        normalise(u - 1)
                                    if u >= 6 + 2 * NT - 1 and (u - 6) % (2 * NT) == 2 * NT - 1:
                                        pair = (u - 6) // (2 * NT)
                                        dve.wait_ge(pv_done, (pair + 1) * 2 * NT)
                                        nc.vector.tensor_copy(mixed_h[:, pair, :],
                                                              bank[:, 6 + pair % 2, :]).then_inc(mixed_copied, 1)
                                        dve.wait_ge(mixed_copied, pair + 1)
                                        nc.vector.tensor_tensor(mixed_l[:, pair, :], bank[:, 6 + pair % 2, :],
                                                                mixed_h[:, pair, :].bitcast(F32),
                                                                ALU.subtract).then_inc(mixed_low, 1)
                    second_h = sb(ctx, "second_h", [P, KD, D // 2], F32R)
                    second_l = sb(ctx, "second_l", [P, KD, D // 2], F32R)
                    norm = norm_buffers(ctx, nc, 0, mix_gb, [
                        q_a[:, 2 * i:2 * i + 2, :].rearrange("p h n -> p (h n)") for i in range(2)])
                    with nc.Block() as block:
                        def both_banks(t):
                            return bank[:, 2 * t:2 * t + 2, :].rearrange("p b n -> p (b n)")

                        @block.sync
                        def _(sp):
                            for k in range(2, KD):
                                sp.wait_ge(wo_low, KD + k - 1)
                                sp.dma_start(wo_raw[:, k % 2, :], w_out[layer, 1, k]).then_inc(wo_land[k % 2], 16)

                        @block.tensor
                        def _(pe):
                            for half, (high, low) in enumerate(((wo_h, wo_l), (second_h, second_l))):
                                for t in range(NT):
                                    tok = slice(t * P, (t + 1) * P)
                                    for k in range(KD):
                                        if t == 0:
                                            pe.wait_ge(wo_low, half * KD + k + 1)
                                        for c, (w, m) in enumerate(passes(mixed_h[:, k, tok], mixed_l[:, k, tok],
                                                                          high[:, k, :], low[:, k, :])):
                                            mm = nc.tensor.matmul(bank[:, 2 * t + half, :], w, m,
                                                                  start=(k == 0 and c == 0),
                                                                  stop=(k == KD - 1 and c == 2))
                                    if half == 1:
                                        mm.then_inc(mix_out, 1)

                        @block.scalar
                        def _(act):
                            for k in range(KD):
                                act.wait_ge(wo_land[k % 2], 16 * ((KD + k) // 2 + 1))
                                nc.scalar.copy(second_h[:, k, :], wo_raw[:, k % 2, :]).then_inc(wo_high, 1)
                            for t in range(NT):
                                norm_on_act(nc, act, t, x, both_banks(t), norm, ln_sems[0])

                        @block.vector
                        def _(dve):
                            for k in range(KD):
                                dve.wait_ge(wo_high, KD + k + 1)
                                nc.vector.tensor_tensor(second_l[:, k, :], wo_raw[:, k % 2, :],
                                                        second_h[:, k, :].bitcast(F32), ALU.subtract).then_inc(wo_low, 1)
                            for t in range(NT + 1):
                                if t >= 1:
                                    mean_square(nc, dve, t - 1, norm, ln_sems[0])
                                if t < NT:
                                    dve.wait_ge(mix_out, t + 1)
                                    if t >= 2:
                                        dve.wait_ge(ln_sems[0]["normed"], t - 1)
                                    add_and_norm(nc, dve, t, x, both_banks(t), norm, ln_sems[0])
                                if t >= 1:
                                    norm_by_root(nc, dve, t - 1, x, norm, ln_sems[0])

            with ExitStack() as peer:
                x_h = sb(peer, "x_h", [P, KD, T], F32R)
                x_l = sb(peer, "x_l", [P, KD, T], F32R)
                e_h = sb(peer, "e_h", [P, 2, KD, P], F32R)
                e_l = sb(peer, "e_l", [P, 2, KD, P], F32R)
                e_out = sb(peer, "e_out", [P, 2, T])
                f_hid = sb(peer, "f_hid", [P, 2, JG, T])
                f_gates = sb(peer, "f_gates", [P, 2, T // CHUNK, JG, CHUNK])
                with ExitStack() as ctx:
                    row_t = sb(ctx, "row_t", [P, T])
                    col_t = sb(ctx, "col_t", [P, T])
                    gate_t = sb(ctx, "gate_t", [P, T])
                    with ExitStack() as inner:
                        keys = sb(inner, "keys", [P, PH, NK])
                        query = sb(inner, "query", [P, PH, T])
                        keysc = sb(inner, "keysc", [P, 2, SEG, NK])
                        rest = sb(inner, "rest", [P, SEG, NK])
                        best = sb(inner, "best", [P, SEG, TOPK])
                        best_i = sb(inner, "best_i", [P, SEG, TOPK], U32)
                        best_f = sb(inner, "best_f", [P, SEG, TOPK])
                        pair = sb(inner, "pair", [P, PH, TOPK * TOPK])
                        pair_rest = sb(inner, "pair_rest", [P, PH, TOPK * TOPK])
                        won = sb(inner, "won", [P, PH, TOPK])
                        won_i = sb(inner, "won_i", [P, PH * TOPK], U32)
                        half_i = sb(inner, "half_i", [P, 2, PH * TOPK], U32)
                        half_f = sb(inner, "half_f", [P, 2, PH * TOPK])
                        hit = sb(inner, "hit", [P, PH * TOPK, TOPK])
                        chosen = sb(inner, "chosen", [P, 2, 3, PH * TOPK])
                        gate_d = sb(inner, "gate_d", [P, PH, TOPK])
                        gate_e = sb(inner, "gate_e", [P, PH, TOPK])
                        gate_s = sb(inner, "gate_s", [P, PH])
                        gate_r = sb(inner, "gate_r", [P, PH])
                        with nc.Block() as block:
                            E_TILES = PH + ROUTE_TILES
                            AHEAD = 4

                            @block.sync
                            def _(sp):
                                def store(n):
                                    sp.wait_ge(e_read, n + 1)
                                    sp.dma_start(hid_dram[n - PH], e_out[:, n % 2, :]).then_inc(e_store[n % 2], 16)

                                for n in range(E_TILES):
                                    if n >= 2:
                                        sp.wait_ge(e_low, n - 1)
                                        sp.dma_start(w_raw[:, n % 2], peer_wq[layer, n] if n < PH else peer_u[layer, n - PH]
                                                     ).then_inc(e_land[n % 2], 16)
                                    if n == 2:
                                        sp.dma_start(keys[:], peer_keys[layer]).then_inc(keys_land, 16)
                                    if n - 3 >= PH:
                                        store(n - 3)
                                for j in range(2):
                                    sp.wait_ge(e_low, E_TILES + j - 1)
                                    sp.dma_start(w_raw[:, j], peer_u[layer, ROUTE_TILES + j]).then_inc(h_land[j], 16)
                                for n in range(E_TILES - 3, E_TILES):
                                    store(n)

                            @block.gpsimd
                            def _(pool):
                                for n in range(E_TILES):
                                    pool.wait_ge(e_high, n + 1)
                                    nc.gpsimd.tensor_tensor(e_l[:, n % 2], w_raw[:, n % 2], e_h[:, n % 2].bitcast(F32),
                                                            ALU.subtract).then_inc(e_low, 1)

                            @block.tensor
                            def _(pe):
                                def turn(k):
                                    if k >= 4:
                                        pe.wait_ge(x_low, k - 3)
                                    for t in range(NT):
                                        mm = nc.tensor.transpose(bank[:, k % 4, t * P:(t + 1) * P],
                                                                 x[:, t, k * P:(k + 1) * P], ident[:])
                                    mm.then_inc(r_xt_psum, 1)

                                def key_scores(t):
                                    if t:
                                        pe.wait_ge(keysc_copied, 4 * t)
                                    for h in range(PH):
                                        for half in range(2):
                                            r = slice(KEY_HALF * half, KEY_HALF * half + KEY_HALF)
                                            mm = nc.tensor.matmul(
                                                bank[:, 2 + 2 * half + h // 4, (h % 4) * NK:(h % 4 + 1) * NK],
                                                query[r, h, t * P:(t + 1) * P], keys[r, h, :], start=True, stop=True)
                                    mm.then_inc(keysc_done, 1)

                                def turn_route(t):
                                    pe.wait_ge(routed, t + 1)
                                    if t >= 2:
                                        pe.wait_ge(route_copied, t - 1)
                                    for j in range(3):
                                        mm = nc.tensor.transpose(bank[:, t % 2, j * P:(j + 1) * P],
                                                                 chosen[:, t % 2, j, :], ident[:])
                                    mm.then_inc(route_turned, 1)

                                def product(n):
                                    pe.wait_ge(e_low, n + 1)
                                    if n >= 2:
                                        pe.wait_ge(e_read, n - 1)
                                    for k in range(KD):
                                        if n == 0:
                                            if k + AHEAD < KD:
                                                turn(k + AHEAD)
                                            pe.wait_ge(x_low, k + 1)
                                        for c, (w, m) in enumerate(passes(e_h[:, n % 2, k, :], e_l[:, n % 2, k, :],
                                                                          x_h[:, k, :], x_l[:, k, :])):
                                            mm = nc.tensor.matmul(bank[:, 6 + n % 2, :], w, m, start=(k == 0 and c == 0),
                                                                  stop=(k == KD - 1 and c == 2))
                                    mm.then_inc(e_hid, 1)

                                for k in range(AHEAD):
                                    turn(k)
                                for n in range(PH):
                                    product(n)
                                pe.wait_ge(keys_land, 16)
                                pe.wait_ge(e_read, PH)
                                key_scores(0)
                                n = PH
                                for t in range(NT):
                                    for i in range(ROUTE_TILES // NT):
                                        product(n)
                                        n += 1
                                        if i == 0 and t + 1 < NT:
                                            key_scores(t + 1)
                                    turn_route(t)

                            @block.scalar
                            def _(act):
                                def copy_scores(t):
                                    act.wait_ge(keysc_done, t + 1)
                                    if t >= 2:
                                        act.wait_ge(routed, t - 1)
                                    for c in range(4):
                                        nc.scalar.copy(keysc[:, t % 2, 4 * c:4 * c + 4, :].rearrange("p s n -> p (s n)"),
                                                       bank[:, 2 + c, :]).then_inc(keysc_copied, 1)

                                def split(n):
                                    act.wait_ge(e_land[n % 2], 16 * (n // 2 + 1))
                                    if n >= 2:
                                        act.wait_ge(e_hid, n - 1)
                                    nc.scalar.copy(e_h[:, n % 2], w_raw[:, n % 2]).then_inc(e_high, 1)

                                def activate(n):
                                    act.wait_ge(e_hid, n + 1)
                                    if n >= PH + 2:
                                        act.wait_ge(e_store[n % 2], 16 * ((n - PH) // 2))
                                    nc.scalar.activation(e_out[:, n % 2, :], bank[:, 6 + n % 2, :],
                                                         ACT.Gelu).then_inc(e_read, 1)

                                split(0)
                                for k in range(KD):
                                    act.wait_ge(r_xt_psum, k + 1)
                                    nc.scalar.copy(x_h[:, k, :], bank[:, k % 4, :]).then_inc(x_high, 1)
                                split(1)
                                for n in range(PH):
                                    act.wait_ge(e_hid, n + 1)
                                    nc.scalar.copy(query[:, n, :], bank[:, 6 + n % 2, :]).then_inc(e_read, 1)
                                    split(n + 2)
                                copy_scores(0)
                                n = PH
                                for t in range(NT):
                                    for i in range(ROUTE_TILES // NT):
                                        if i == ROUTE_TILES // NT - 1:
                                            act.wait_ge(gate_shift, t + 1)
                                            nc.scalar.activation(gate_e[:], gate_d[:], ACT.Exp).then_inc(gate_exp, 1)
                                        if n + 2 < E_TILES:
                                            split(n + 2)
                                        if n >= E_TILES - 2:
                                            act.wait_ge(h_land[n % 2], 16)
                                            act.wait_ge(e_hid, n + 1)
                                            nc.scalar.copy(e_h[:, n % 2], w_raw[:, n % 2]).then_inc(h_high, 1)
                                        activate(n)
                                        if i == 0 and t + 1 < NT:
                                            copy_scores(t + 1)
                                        n += 1
                                    act.wait_ge(route_turned, t + 1)
                                    for j, dst in enumerate((row_t, col_t, gate_t)):
                                        last = nc.scalar.copy(dst[:, t * P:(t + 1) * P],
                                                              bank[:, t % 2, j * P:(j + 1) * P])
                                    last.then_inc(route_copied, 1)

                            @block.vector
                            def _(dve):
                                for k in range(KD):
                                    dve.wait_ge(x_high, k + 1)
                                    nc.vector.tensor_tensor(x_l[:, k, :], bank[:, k % 4, :],
                                                            x_h[:, k, :].bitcast(F32), ALU.subtract).then_inc(x_low, 1)
                                step = [0]

                                def then_wait(ins):
                                    step[0] += 1
                                    ins.then_inc(route, 1)
                                    dve.wait_ge(route, step[0])

                                def top16(score, left, value, index, n):
                                    for s in range(n):
                                        ins = nc.vector.max(value[:, s, 0:8], score[:, s, :])
                                    then_wait(ins)
                                    for s in range(n):
                                        ins = nc.vector.match_replace(out=left[:, s, :], in_to_replace=value[:, s, 0:8],
                                                                      in_values=score[:, s, :], imm_value=-HUGE)
                                    then_wait(ins)
                                    for s in range(n):
                                        nc.vector.max(value[:, s, 8:16], left[:, s, :])
                                        ins = nc.vector.max_index(out=index[:, s, 0:8], in_max=value[:, s, 0:8],
                                                                  in_values=score[:, s, :])
                                    then_wait(ins)
                                    for s in range(n):
                                        ins = nc.vector.max_index(out=index[:, s, 8:16], in_max=value[:, s, 8:16],
                                                                  in_values=left[:, s, :])
                                    then_wait(ins)

                                first16 = iota[:, 0:TOPK].unsqueeze(1).broadcast_to([P, PH * TOPK, TOPK])
                                for t in range(NT):
                                    dve.wait_ge(keysc_copied, 4 * (t + 1))
                                    top16(keysc[:, t % 2], rest, best, best_i, SEG)
                                    nc.vector.tensor_copy(best_f[:], best_i[:])
                                    then_wait(nc.vector.tensor_tensor(
                                        pair[:].rearrange("p h (a b) -> p h a b", b=TOPK),
                                        best[:, 0:PH, :].unsqueeze(3).broadcast_to([P, PH, TOPK, TOPK]),
                                        best[:, PH:SEG, :].unsqueeze(2).broadcast_to([P, PH, TOPK, TOPK]), ALU.add))
                                    top16(pair, pair_rest, won, won_i[:].rearrange("p (h k) -> p h k", h=PH), PH)
                                    nc.vector.tensor_tensor(gate_d[:], won[:], won[:, :, 0:1].broadcast_to([P, PH, TOPK]),
                                                            ALU.subtract).then_inc(gate_shift, 1)
                                    nc.vector.tensor_scalar(half_i[:, 0, :], won_i[:], 4, None, ALU.logical_shift_right)
                                    then_wait(nc.vector.tensor_scalar(half_i[:, 1, :], won_i[:], TOPK - 1, None,
                                                                      ALU.bitwise_and))
                                    then_wait(nc.vector.tensor_copy(half_f[:], half_i[:]))
                                    if t >= 2:
                                        dve.wait_ge(route_turned, t - 1)
                                    for half in range(2):
                                        then_wait(nc.vector.tensor_tensor(
                                            hit[:], first16,
                                            half_f[:, half, :].unsqueeze(2).broadcast_to([P, PH * TOPK, TOPK]),
                                            ALU.is_equal))
                                        then_wait(nc.vector.tensor_tensor(
                                            hit[:].rearrange("p (h k) a -> p h k a", h=PH),
                                            hit[:].rearrange("p (h k) a -> p h k a", h=PH),
                                            best_f[:, half * PH:(half + 1) * PH, :].unsqueeze(2).broadcast_to(
                                                [P, PH, TOPK, TOPK]), ALU.mult))
                                        then_wait(nc.vector.reduce_sum(chosen[:, t % 2, half, :], hit[:], AX.X))
                                    dve.wait_ge(gate_exp, t + 1)
                                    then_wait(nc.vector.reduce_sum(gate_s[:], gate_e[:], AX.X))
                                    then_wait(nc.vector.reciprocal(gate_r[:], gate_s[:]))
                                    nc.vector.tensor_tensor(
                                        chosen[:, t % 2, 2, :].rearrange("p (h k) -> p h k", h=PH), gate_e[:],
                                        gate_r[:].unsqueeze(2).broadcast_to([P, PH, TOPK]),
                                        ALU.mult).then_inc(routed, 1)
                                    dve.wait_ge(routed, t + 1)
                                for j in range(2):
                                    dve.wait_ge(h_high, j + 1)
                                    nc.vector.tensor_tensor(e_l[:, j], w_raw[:, j], e_h[:, j].bitcast(F32),
                                                            ALU.subtract).then_inc(h_low, 1)
                    rows = sb(ctx, "rows", [P, 16, NK])
                    cols = sb(ctx, "cols", [P, 16, NK])
                    stage = sb(ctx, "stage", [P, 2, NK, CHUNK])
                    with nc.Block() as block:
                        def four_of(pair, half, it, f):
                            return pair * 32 + it * 8 + (half * 16 + f)

                        def tile_of(pair, half, it, tile):
                            return pair * 8 + it * 2 + (half * 4 + tile)

                        @block.sync
                        def _(sp):
                            with sp.Fori(1, GATE_TILES // 2) as i:
                                for slot in range(2):
                                    sp.wait_ge(h_low, i * 2 + (slot + 1))
                                    sp.dma_start(w_raw[:, slot], peer_u[layer, i * 2 + (ROUTE_TILES + slot)]
                                                 ).then_inc(h_land[slot], 16)
                            for n in range(GATE_TILES, GATE_TILES + STORE_TILES):
                                if n < GATE_TILES + 2:
                                    sp.wait_ge(h_low, n + 1)
                                else:
                                    sp.wait_ge(h_last_low, n - GATE_TILES - 1)
                                sp.dma_start(w_raw[:, n % 2], peer_u[layer, ROUTE_TILES + n]
                                             ).then_inc(h_land[n % 2], 16)
                            for j in range(2):
                                sp.wait_ge(h_last_low, STORE_TILES + j - 1)
                                sp.dma_start(w_raw[:, j], peer_u[layer, EARLY_TILES + j]).then_inc(u_land[j], 16)

                        @block.gpsimd
                        def _(pool):
                            pool.sem_inc(h_low, 2)
                            with pool.Fori(1, GATE_TILES // 2) as i:
                                for slot in range(2):
                                    pool.wait_ge(h_high, i * 2 + (slot + 1))
                                    nc.gpsimd.tensor_tensor(e_l[:, slot], w_raw[:, slot], e_h[:, slot].bitcast(F32),
                                                            ALU.subtract).then_inc(h_low, 1)

                        @block.vector
                        def _(dve):
                            with dve.Fori(0, 4) as pair:
                                for half in range(2):
                                    with dve.Fori(0, 2) as it:
                                        for f in range(8):
                                            four = four_of(pair, half, it, f)
                                            tok = pair * P + it * 32 + (half * CHUNK + 4 * f)
                                            dve.wait_ge(gate_mm, four + 1)
                                            nc.vector.tensor_tensor(
                                                cols[:, 4 * (f % 4):4 * (f % 4) + 4, :],
                                                iota[:].unsqueeze(1).broadcast_to([P, 4, NK]),
                                                col_t[:, bass.ds(tok, 4)].unsqueeze(2).broadcast_to([P, 4, NK]),
                                                ALU.is_equal)
                                            for s in range(4):
                                                ins = nc.vector.tensor_scalar(rows[:, 4 * (f % 4) + s, :], iota[:],
                                                                              row_t[:, bass.ds(tok + s, 1)],
                                                                              gate_t[:, bass.ds(tok + s, 1)],
                                                                              ALU.is_equal, ALU.mult)
                                            ins.then_inc(rows_ready, 1)

                            for n in range(GATE_TILES, GATE_TILES + STORE_TILES):
                                dve.wait_ge(h_high, n + 1)
                                nc.vector.tensor_tensor(e_l[:, n % 2], w_raw[:, n % 2], e_h[:, n % 2].bitcast(F32),
                                                        ALU.subtract).then_inc(h_last_low, 1)
                            for j in range(2):
                                dve.wait_ge(u_high, j + 1)
                                nc.vector.tensor_tensor(e_l[:, j], w_raw[:, j], e_h[:, j].bitcast(F32),
                                                        ALU.subtract).then_inc(u_low, 1)

                        @block.tensor
                        def _(pe):
                            pe.sem_inc(gate_mm, 4)
                            pe.sem_inc(h_hid, 2)
                            with pe.Fori(0, 4) as pair:
                                for half in range(2):
                                    with pe.Fori(0, 2) as it:
                                        for f in range(8):
                                            tile, quarter = f // 4, f % 4
                                            if quarter == 0:
                                                m = tile_of(pair, half, it, tile)
                                                pe.wait_ge(h_low, m + 3)
                                                pe.wait_ge(h_gelu, m + 1)
                                            for k in (2 * quarter, 2 * quarter + 1):
                                                for c, (w, x_part) in enumerate(passes(
                                                        e_h[:, tile, k, :], e_l[:, tile, k, :], x_h[:, k, :], x_l[:, k, :])):
                                                    mm = nc.tensor.matmul(bank[:, 6 + tile, :], w, x_part,
                                                                          start=(k == 0 and c == 0),
                                                                          stop=(k == KD - 1 and c == 2))
                                            if quarter == 3:
                                                mm.then_inc(h_hid, 1)
                                            four = four_of(pair, half, it, f)
                                            pe.wait_ge(rows_ready, four + 1)
                                            pe.wait_ge(gate_copied, four + 1)
                                            for s in range(4):
                                                slot = 4 * (f % 4) + s
                                                mm = nc.tensor.matmul(bank[:, f % 4, s * NK:(s + 1) * NK],
                                                                      rows[:, slot, :], cols[:, slot, :],
                                                                      start=True, stop=True)
                                            mm.then_inc(gate_mm, 1)
                            for m in range(GATE_TILES, GATE_TILES + STORE_TILES):
                                pe.wait_ge(h_last_low, m - GATE_TILES + 1)
                                pe.wait_ge(h_gelu, m + 1)
                                for k in range(KD):
                                    for c, (w, x_part) in enumerate(passes(e_h[:, m % 2, k, :], e_l[:, m % 2, k, :],
                                                                           x_h[:, k, :], x_l[:, k, :])):
                                        mm = nc.tensor.matmul(bank[:, 6 + m % 2, :], w, x_part,
                                                              start=(k == 0 and c == 0), stop=(k == KD - 1 and c == 2))
                                mm.then_inc(h_hid, 1)

                        @block.scalar
                        def _(act):
                            def split(n, slot, run):
                                act.wait_ge(h_land[slot], run)
                                act.wait_ge(h_hid, n + 1)
                                nc.scalar.copy(e_h[:, slot], w_raw[:, slot]).then_inc(h_high, 1)

                            def activate(m, slot, stores):
                                act.wait_ge(h_hid, m + 3)
                                act.wait_ge(h_store[slot], stores)
                                nc.scalar.activation(e_out[:, slot, :], bank[:, 6 + slot, :],
                                                     ACT.Gelu).then_inc(h_gelu, 1)
                                act.wait_ge(h_gelu, m + 3)
                                act.dma_start(hid_dram[m + ROUTE_TILES], e_out[:, slot, :]
                                              ).then_inc(h_store[slot], 16)

                            act.sem_inc(gate_copied, 4)
                            act.sem_inc(h_gelu, 2)
                            for i in range(2):
                                act.wait_ge(e_store[i], 16 * ROUTE_TILES // 2)
                            with act.Fori(0, 4) as pair:
                                for half in range(2):
                                    act.wait_ge(gate_store[half], pair * 16)
                                    with act.Fori(0, 2) as it:
                                        runs = pair * 4 + it + half * 2
                                        for f in range(8):
                                            four, tile = four_of(pair, half, it, f), f // 4
                                            m = tile_of(pair, half, it, tile)
                                            act.wait_ge(gate_mm, four + 5)
                                            nc.scalar.copy(
                                                stage[:, half, :, bass.ds(it * 32 + 4 * f, 4)].rearrange("p j t -> p t j"),
                                                bank[:, f % 4, :].rearrange("p (t j) -> p t j", t=4)
                                            ).then_inc(gate_copied, 1)
                                            if f % 4 == 3:
                                                activate(m, tile, runs * 16)
                                                split(m + 2, tile, runs * 16 + 32)
                                    act.wait_ge(gate_copied, pair * 32 + (half * 16 + 16 + 4))
                                    act.dma_start(gate_dram[pair * 2 + half], stage[:, half]
                                                  ).then_inc(gate_store[half], 16)
                            for m in range(GATE_TILES, GATE_TILES + STORE_TILES):
                                if m >= GATE_TILES + STORE_TILES - 2:
                                    act.wait_ge(u_land[m % 2], 16)
                                    act.wait_ge(h_hid, m + 3)
                                    nc.scalar.copy(e_h[:, m % 2], w_raw[:, m % 2]).then_inc(u_high, 1)
                                activate(m, m % 2, 16 * (m // 2))
                                if m + 2 < GATE_TILES + STORE_TILES:
                                    split(m + 2, m % 2, 16 * ((m + 2) // 2 + 1))
                            for i in range(2):
                                act.wait_ge(gate_store[i], 16 * 4)
                fv_h, fv_l = ([[a[:, 2 * j:2 * j + 2, :].rearrange("p a n -> p (a n)") for j in range(JG)]]
                              for a in (x_h, x_l))
                fa_h, fa_l = ([[a[:, j // 2, 4 * (j % 2):4 * (j % 2) + 4, :].rearrange("p k n -> p (k n)")
                                for j in range(JG)]] for a in (e_h, e_l))

                def by_chunk(a):
                    return a.rearrange("p (s t) -> p s t", t=CHUNK)

                def f_split_on_act(act, g, b, j):
                    act.wait_ge(fv_land[j % 2], g * 32 + (16 * (j // 2) + 16))
                    nc.scalar.copy(fv_h[b][j], w_raw[:, j % 2].rearrange("p k n -> p (k n)")).then_inc(fv_high, 1)
                    act.wait_ge(f_weighted, g * JG + (j + 1 + 2 * JG))
                    nc.scalar.copy(fa_h[b][j], e_out[:, j % 2, :]).then_inc(fa_high, 1)

                def f_split_on_dve(dve, g, b, j):
                    nc.vector.tensor_tensor(by_chunk(e_out[:, j % 2, :]), by_chunk(f_hid[:, b, j, :]),
                                            f_gates[:, b, :, j, :], ALU.mult).then_inc(f_weighted, 1)
                    dve.wait_ge(fv_high, g * JG + (j + 1))
                    nc.vector.tensor_tensor(fv_l[b][j], w_raw[:, j % 2].rearrange("p k n -> p (k n)"),
                                            fv_h[b][j].bitcast(F32), ALU.subtract).then_inc(fv_low, 1)
                    dve.wait_ge(fa_high, g * JG + (j + 1))
                    nc.vector.tensor_tensor(fa_l[b][j], e_out[:, j % 2, :], fa_h[b][j].bitcast(F32),
                                            ALU.subtract).then_inc(fa_low, 1)

                with ExitStack() as ctx:
                    more_h = sb(ctx, "more_h", [P, 2, KD, P], F32R)
                    more_l = sb(ctx, "more_l", [P, 2, KD, P], F32R)
                    u_h = [e_h[:, 0], e_h[:, 1], more_h[:, 0], more_h[:, 1]]
                    u_l = [e_l[:, 0], e_l[:, 1], more_l[:, 0], more_l[:, 1]]
                    v_raw = sb(ctx, "v_raw", [P, 2, D])
                    v_h = sb(ctx, "v_h", [P, JG, D], F32R)
                    v_l = sb(ctx, "v_l", [P, JG, D], F32R)
                    gates = sb(ctx, "gates", [P, T // CHUNK, JG, CHUNK])
                    gelu = sb(ctx, "gelu", [P, 2, T])
                    weight = sb(ctx, "weight", [P, 2, T])
                    a_h = sb(ctx, "a_h", [P, JG, T], F32R)
                    a_l = sb(ctx, "a_l", [P, JG, T], F32R)
                    with nc.Block() as block:
                        @block.sync
                        def _(sp):
                            def load_hidden(i):
                                sp.dma_start(f_hid[:, i], hid_dram[i * JG:(i + 1) * JG].rearrange("j p t -> p j t")
                                             ).then_inc(f_land[i], 16)
                                sp.dma_start(f_gates[:, i], gate_dram[:, :, i * JG:(i + 1) * JG, :].rearrange(
                                    "s i j t -> i s j t")).then_inc(f_land[i], 16)

                            def group(g, first):
                                for j in range(2 if first else 0, JG):
                                    sp.wait_ge(u_low, g * JG + (j + 1))
                                    sp.dma_start(w_raw[:, j % 2], peer_u[layer, g * JG + (EARLY_TILES + j)]).then_inc(u_land[j % 2], 16)
                                sp.wait_ge(weighted, g * JG + 2)
                                sp.dma_start(gates[:], gate_dram[:, :, bass.ds(g * JG + EARLY_TILES, JG), :].rearrange(
                                    "s i j t -> i s j t")).then_inc(g_land[0], 16)
                                for j in range(JG):
                                    sp.wait_ge(v_low, g * JG + (j + 1))
                                    sp.dma_start(v_raw[:, j % 2, :], peer_v[layer, :, g * JG + (EARLY_TILES + j), :]).then_inc(v_land[j % 2], 16)

                            group(0, True)
                            load_hidden(0)
                            with sp.Fori(1, LATE_GROUPS) as g:
                                group(g, False)
                            sp.wait_ge(u_low, LATE_GROUPS * JG + 2)
                            for j in range(JG):
                                sp.wait_ge(fv_low, j + 1)
                                sp.dma_start(w_raw[:, j % 2].rearrange("p k n -> p (k n)"), peer_v[layer, :, j, :]
                                             ).then_inc(fv_land[j % 2], 16)
                            load_hidden(1)

                        @block.tensor
                        def _(pe):
                            pe.sem_inc(hid_done, JG)
                            with pe.Fori(0, LATE_GROUPS) as g:
                                for j in range(JG):
                                    n = g * JG + j
                                    pe.wait_ge(u_low, n + 3)
                                    pe.wait_ge(gelu_done, n + 1)
                                    for k in range(KD):
                                        for c, (w, m) in enumerate(passes(u_h[j][:, k, :], u_l[j][:, k, :],
                                                                          x_h[:, k, :], x_l[:, k, :])):
                                            mm = nc.tensor.matmul(bank[:, j % 2, :], w, m, start=(k == 0 and c == 0),
                                                                  stop=(k == KD - 1 and c == 2))
                                    mm.then_inc(hid_done, 1)
                                for t in range(NT):
                                    pe.wait_ge(down_added, g * NT + (t + 1))
                                    tok = slice(t * P, (t + 1) * P)
                                    for j in range(JG):
                                        if t == 0:
                                            pe.wait_ge(act_low, g * JG + (j + 1))
                                            pe.wait_ge(v_low, g * JG + (j + 3))
                                        for half in range(2):
                                            c0 = slice(half * 512, (half + 1) * 512)
                                            for c, (w, m) in enumerate(passes(a_h[:, j, tok], a_l[:, j, tok],
                                                                              v_h[:, j, c0], v_l[:, j, c0])):
                                                mm = nc.tensor.matmul(bank[:, 2 + 2 * (t % 2) + half, :], w, m,
                                                                      start=(j == 0 and c == 0),
                                                                      stop=(j == JG - 1 and c == 2))
                                    mm.then_inc(down_done, 1)

                        @block.scalar
                        def _(act):
                            def split_u(g, j):
                                act.wait_ge(u_land[j % 2], g * 32 + (16 * (j // 2) + 16))
                                act.wait_ge(hid_done, g * JG + (j + 1))
                                nc.scalar.copy(u_h[j], w_raw[:, j % 2]).then_inc(u_high, 1)

                            def split_v(g, j):
                                act.wait_ge(v_land[j % 2], g * 32 + (16 * (j // 2) + 16))
                                act.wait_ge(down_done, g * NT)
                                nc.scalar.copy(v_h[:, j, :], v_raw[:, j % 2, :]).then_inc(v_high, 1)

                            def activate(n, j):
                                act.wait_ge(hid_done, n + (JG + 1))
                                act.wait_ge(weighted, n + 1)
                                nc.scalar.activation(gelu[:, j % 2, :], bank[:, j % 2, :], ACT.Gelu).then_inc(gelu_done, 1)
                                act.wait_ge(weighted, n + 3)
                                act.wait_ge(down_done, n - j)
                                nc.scalar.copy(a_h[:, j, :], weight[:, j % 2, :]).then_inc(act_high, 1)

                            def group(g, first):
                                if not first:
                                    activate(g * JG - 1, JG - 1)
                                for j in range(2 if first else 0, JG):
                                    split_u(g, j)
                                for j in range(JG):
                                    split_v(g, j)
                                    if j < JG - 1:
                                        activate(g * JG + j, j)

                            act.sem_inc(gelu_done, 2)
                            group(0, True)
                            with act.Fori(1, LATE_GROUPS) as g:
                                group(g, False)
                            activate(LATE_GROUPS * JG - 1, JG - 1)
                            act.wait_ge(hid_done, LATE_GROUPS * JG + JG)
                            for j in range(JG):
                                f_split_on_act(act, 0, 0, j)

                        @block.vector
                        def _(dve):
                            def split_u(g, j):
                                dve.wait_ge(u_high, g * JG + (j + 1))
                                nc.vector.tensor_tensor(u_l[j], w_raw[:, j % 2], u_h[j].bitcast(F32),
                                                        ALU.subtract).then_inc(u_low, 1)

                            def split_v(g, j):
                                dve.wait_ge(v_high, g * JG + (j + 1))
                                nc.vector.tensor_tensor(v_l[:, j, :], v_raw[:, j % 2, :], v_h[:, j, :].bitcast(F32),
                                                        ALU.subtract).then_inc(v_low, 1)

                            def activate(n, j):
                                if j == 0:
                                    dve.wait_ge(g_land[0], n * (16 // JG) + 16)
                                dve.wait_ge(gelu_done, n + 3)
                                nc.vector.tensor_tensor(by_chunk(weight[:, j % 2, :]), by_chunk(gelu[:, j % 2, :]),
                                                        gates[:, :, j, :], ALU.mult).then_inc(weighted, 1)
                                dve.wait_ge(act_high, n + 1)
                                nc.vector.tensor_tensor(a_l[:, j, :], weight[:, j % 2, :], a_h[:, j, :].bitcast(F32),
                                                        ALU.subtract).then_inc(act_low, 1)

                            def add_down(g, t):
                                dve.wait_ge(down_done, g * NT + (t + 1))
                                b = 2 + 2 * (t % 2)
                                nc.vector.tensor_tensor(x[:, t, :], x[:, t, :],
                                                        bank[:, b:b + 2, :].rearrange("p b n -> p (b n)"),
                                                        ALU.add).then_inc(down_added, 1)

                            def group(g, first):
                                if not first:
                                    activate(g * JG - 1, JG - 1)
                                for j in range(2 if first else 0, JG):
                                    split_u(g, j)
                                    if not first:
                                        add_down(g - 1, j)
                                for j in range(JG):
                                    split_v(g, j)
                                    if j < JG - 1:
                                        activate(g * JG + j, j)

                            dve.sem_inc(u_low, 2)
                            dve.sem_inc(v_low, 2)
                            dve.sem_inc(weighted, 2)
                            dve.sem_inc(f_weighted, 2 * JG)
                            dve.sem_inc(fv_low, 2)
                            for t in range(NT):
                                nc.vector.tensor_scalar(x[:, t, :], x[:, t, :], ALPHA, None,
                                                        ALU.mult).then_inc(x_scaled, 1)
                            dve.wait_ge(x_scaled, NT)
                            dve.sem_inc(down_added, 2)
                            group(0, True)
                            with dve.Fori(1, LATE_GROUPS) as g:
                                group(g, False)
                            activate(LATE_GROUPS * JG - 1, JG - 1)
                            dve.wait_ge(f_land[0], 32)
                            for i in range(2):
                                dve.wait_ge(h_store[i], 16 * (GATE_TILES + STORE_TILES) // 2)
                            dve.wait_ge(hid_done, LATE_GROUPS * JG + JG)
                            for j in range(JG):
                                f_split_on_dve(dve, 0, 0, j)
                                add_down(LATE_GROUPS - 1, j)
                with ExitStack() as ctx:
                    v_odd_h = sb(ctx, "v_odd_h", [P, JG, D], F32R)
                    v_odd_l = sb(ctx, "v_odd_l", [P, JG, D], F32R)
                    a_odd_h = sb(ctx, "a_odd_h", [P, JG, T], F32R)
                    a_odd_l = sb(ctx, "a_odd_l", [P, JG, T], F32R)
                    for both, odd in ((fv_h, v_odd_h), (fv_l, v_odd_l), (fa_h, a_odd_h), (fa_l, a_odd_l)):
                        both.append([odd[:, j, :] for j in range(JG)])
                    norm = norm_buffers(ctx, nc, 1, sb(ctx, "peer_gb", [P, 2, D]),
                                        [sb(ctx, f"peer_scaled{i}", [P, D])[:] for i in range(2)])
                    with nc.Block() as block:
                        def other_groups(engine, group):
                            with engine.Fori(0, (EARLY_GROUPS - 1) // 2) as i:
                                group(i * 2 + 1, 1)
                                group(i * 2 + 2, 0)

                        @block.sync
                        def _(sp):
                            def group(g, b, loaded):
                                if not loaded:
                                    sp.wait_ge(f_weighted, g * JG + JG)
                                    sp.dma_start(f_hid[:, b], hid_dram[bass.ts(g, JG)].rearrange("j p t -> p j t")
                                                 ).then_inc(f_land[b], 16)
                                    sp.dma_start(f_gates[:, b], gate_dram[:, :, bass.ds(g * JG, JG), :].rearrange(
                                        "s i j t -> i s j t")).then_inc(f_land[b], 16)
                                for j in range(JG):
                                    sp.wait_ge(fv_low, g * JG + (j + 1))
                                    sp.dma_start(w_raw[:, j % 2].rearrange("p k n -> p (k n)"), peer_v[layer, :, g * JG + j, :]
                                                 ).then_inc(fv_land[j % 2], 16)

                            group(1, 1, True)
                            group(2, 0, False)
                            sp.dma_start(norm["gb"][:], ln_gb[layer, 1].partition_broadcast(P)
                                         ).then_inc(ln_sems[1]["land"], 16)
                            with sp.Fori(1, (EARLY_GROUPS - 1) // 2) as i:
                                group(i * 2 + 1, 1, False)
                                group(i * 2 + 2, 0, False)

                        @block.tensor
                        def _(pe):
                            pe.sem_inc(f_done, 2 * NT)

                            def group(g, b):
                                for t in range(NT):
                                    pe.wait_ge(f_added, g * NT + (t + 1))
                                    tok = slice(t * P, (t + 1) * P)
                                    for j in range(JG):
                                        if t == 0:
                                            pe.wait_ge(fa_low, g * JG + (j + 1))
                                            pe.wait_ge(fv_low, g * JG + (j + 3))
                                        for half in range(2):
                                            c0 = slice(half * 512, (half + 1) * 512)
                                            for c, (w, m) in enumerate(passes(fa_h[b][j][:, tok], fa_l[b][j][:, tok],
                                                                              fv_h[b][j][:, c0], fv_l[b][j][:, c0])):
                                                mm = nc.tensor.matmul(bank[:, 2 * (t % 2) + half, :], w, m,
                                                                      start=(j == 0 and c == 0),
                                                                      stop=(j == JG - 1 and c == 2))
                                    mm.then_inc(f_done, 1)

                            group(0, 0)
                            other_groups(pe, group)

                        @block.scalar
                        def _(act):
                            def group(g, b):
                                act.wait_ge(f_done, g * NT + NT)
                                for j in range(JG):
                                    f_split_on_act(act, g, b, j)

                            other_groups(act, group)
                            for t in range(NT):
                                norm_on_act(nc, act, t, x, bank[:, 4:6, :].rearrange("p b n -> p (b n)"), norm, ln_sems[1])

                        @block.vector
                        def _(dve):
                            def add(g, t):
                                dve.wait_ge(f_done, g * NT + (t + 1 + 2 * NT))
                                nc.vector.tensor_tensor(
                                    x[:, t, :], x[:, t, :],
                                    bank[:, 2 * (t % 2):2 * (t % 2) + 2, :].rearrange("p b n -> p (b n)"),
                                    ALU.add).then_inc(f_added, 1)

                            def group(g, b):
                                dve.wait_ge(f_land[b], (g + (2 - b)) * 16)
                                for j in range(JG):
                                    f_split_on_dve(dve, g, b, j)
                                    add(g - 1, j)

                            dve.sem_inc(f_added, 2)
                            other_groups(dve, group)
                            for t in range(NT + 1):
                                if t >= 1:
                                    mean_square(nc, dve, t - 1, norm, ln_sems[1])
                                if t < NT:
                                    dve.wait_ge(f_done, (EARLY_GROUPS - 1) * NT + (t + 1 + 2 * NT))
                                    if t >= 2:
                                        dve.wait_ge(ln_sems[1]["normed"], t - 1)
                                    add_and_norm(nc, dve, t, x, bank[:, 2 * (t % 2):2 * (t % 2) + 2, :].rearrange(
                                        "p b n -> p (b n)"), norm, ln_sems[1])
                                    if t < 2:
                                        dve.sem_inc(f_added, 1)
                                if t >= 1:
                                    norm_by_root(nc, dve, t - 1, x, norm, ln_sems[1])

        stored = top.enter_context(nc.semaphore("stored"))
        with nc.Block() as block:
            @block.sync
            def _(sp):
                for t in range(NT):
                    sp.dma_start(out[t * P:(t + 1) * P, :], x[:, t, :]).then_inc(stored, 16)
                sp.wait_ge(stored, 16 * NT)


def _rotary():
    tab = np.zeros((P, 3, T), np.float32)
    for dim in (HD, ROPE):
        inv = (np.float32(10000.0) ** (-np.arange(0, dim, 2, dtype=np.float32) / np.float32(dim))).astype(np.float32)
        ang = np.arange(T, dtype=np.float32)[:, None] * inv[None, :]
        cos, sin = np.cos(ang).T, np.sin(ang).T
        if dim == HD:
            tab[:, 0], tab[:, 1] = np.concatenate([cos] * 4), np.concatenate([sin, -sin] * 2)
        else:
            tab[NOPE:QK, 2], tab[QK:P, 2] = np.concatenate([cos, cos]), np.concatenate([-sin, sin])
    return tab


def _swap(start, dim):
    return [start + (f + dim // 2) % dim for f in range(dim)]


def _in_columns():
    akr = Q_RANK + KV_RANK
    bq = akr + ROPE
    bk, bv = bq + B_HEADS * HD, bq + 2 * B_HEADS * HD
    cq = bv + B_HEADS * HD
    ck = cq + C_HEADS * HD
    cv = ck + 2 * HD
    columns = list(range(akr))
    columns += [akr + f % ROPE for f in range(NOPE)] + list(range(akr, bq)) + _swap(akr, ROPE)
    columns += list(range(bq, bv))
    columns += [cq + h * HD + d for h in _c_heads() for d in range(HD)]
    columns += list(range(ck, cv)) + list(range(bv, cq)) + list(range(cv, cv + 2 * HD))
    return np.array(columns).reshape(-1, P)


def _c_heads():
    return [(s % 2) * 2 + s // 2 for s in range(C_HEADS)]


def kernel(**inputs):
    import concourse.bacc as _bacc
    from concourse import mybir as _mybir
    from concourse.bass_utils import run_bass_kernel_spmd as _run

    g = {k: np.asarray(v) for k, v in inputs.items()}
    L = DEPTH
    heads = _c_heads()
    w_in = g["w_in"].reshape(L, KD, P, -1)
    uq = g["mla_w_uq"].reshape(L, KQ, P, A_HEADS, QK)
    w_uq = uq[..., np.array(list(range(QK)) + _swap(NOPE, ROPE))].reshape(L, KQ, P, -1)
    ukv = g["mla_w_ukv"].reshape(L, KKV, P, A_HEADS, NOPE + V_DIM).transpose(0, 2, 1, 3, 4)
    w_uk, w_uv = (ukv[..., part].reshape(L, 1, P, -1) for part in (slice(0, NOPE), slice(NOPE, None)))
    mix_rows = list(range(768)) + [768 + h * HD + d for h in heads for d in range(HD)]
    arrays = {
        "x_in": g["x"].reshape(T, D),
        "rope_tab": _rotary(),
        "w_in": w_in[..., _in_columns()].transpose(0, 3, 2, 1, 4),
        "norms": np.concatenate([g["mla_q_norm"], g["mla_kv_norm"]], 1).reshape(L, KQ + KKV, P).transpose(0, 2, 1),
        "w_up": np.concatenate([w_uq, w_uk, w_uv], 1),
        "rel_bias": g["rel_bias"][:, :, ::-1].reshape(L * B_HEADS, REL_TABLE),
        "sinks": g["swa_sinks"][:, np.array(heads)],
        "w_out": g["w_out"][:, np.array(mix_rows)].reshape(L, KD, P, 2, D // 2).transpose(0, 3, 1, 2, 4),
        "ln_gb": np.stack([np.stack([g["ln1_g"], g["ln1_b"]], 1), np.stack([g["ln2_g"], g["ln2_b"]], 1)], 1),
        "peer_wq": g["peer_wq"].reshape(L, KD, P, PH, P).transpose(0, 3, 2, 1, 4),
        "peer_keys": g["peer_keys"].transpose(0, 2, 4, 1, 3).reshape(L, P, PH, NK),
        "peer_u": g["peer_u"].reshape(L, NK, NK, KD, P).transpose(0, 2, 4, 3, 1),
        "peer_v": g["peer_v"].reshape(L, NK, NK, D),
    }
    nc = _bacc.Bacc("TRN2", target_bir_lowering=False, num_devices=1)
    given, args = {}, []
    for name, a in arrays.items():
        a = np.ascontiguousarray(a)
        given[f"in_{name}"] = a
        args.append(nc.dram_tensor(f"in_{name}", a.shape, _mybir.dt.from_np(a.dtype), kind="ExternalInput").ap())
    result = nc.dram_tensor("result", (T, D), F32, kind="ExternalOutput").ap()
    program(nc, *args, result)
    r = _run(nc, [given], core_ids=[0])
    return r.results[0]["result"].reshape(1, T, D)
```
